# Optimizing a Trainium2 kernel written in Bass

```python
import math
import jax, jax.numpy as jnp
from jax import lax
import numpy as np

D_MODEL = 1024
BATCH = 1
SEQ = 512
DEPTH = 1
DEC_BATCH = 8
DEC_SEQ = 8
PAST_LEN = 2048
PAGE_SIZE = 128

HEAD_DIM = 64
MIX_WIDTH = D_MODEL
WIDTH_A = MIX_WIDTH // 2
WIDTH_B = MIX_WIDTH - WIDTH_A
N_HEADS_A = WIDTH_A // HEAD_DIM
N_HEADS_B = WIDTH_B // (2 * HEAD_DIM)
DILATED_CFG = ((128, 1), (512, 4), (2048, 16))
WIN_MAX = 2048
D_FF = 256 * math.ceil(8 * D_MODEL / 3 / 256)
CONV_W = 3
ROPE_THETA = 10000.0
Q_BLOCK = 128
EPS = 1e-5
DEEPNORM_ALPHA = (2 * DEPTH) ** 0.25
DEEPNORM_BETA = (8 * DEPTH) ** -0.25

kernel_name = 'dilated_diffattn_convffn_hybrid_step'

def layer_norm(x, g, b):
    xf = x.astype(jnp.float32)
    mu = jnp.mean(xf, -1, keepdims=True)
    var = jnp.mean(jnp.square(xf - mu), -1, keepdims=True)
    return ((xf - mu) * lax.rsqrt(var + EPS)).astype(x.dtype) * g + b

def rms_norm(x, g):
    xf = x.astype(jnp.float32)
    return (xf * lax.rsqrt(jnp.mean(jnp.square(xf), -1, keepdims=True) + EPS)).astype(x.dtype) * g

def rope(x, pos):
    half = HEAD_DIM // 2
    inv = 1.0 / (ROPE_THETA ** (jnp.arange(half, dtype=jnp.float32) / half))
    ang = pos.astype(jnp.float32)[:, None] * inv[None, :]
    shape = (pos.shape[0],) + (1,) * (x.ndim - 3) + (half,)
    cos = jnp.cos(ang).reshape(shape)
    sin = jnp.sin(ang).reshape(shape)
    xf = x.astype(jnp.float32)
    x1, x2 = xf[..., :half], xf[..., half:]
    return jnp.concatenate([x1 * cos - x2 * sin, x2 * cos + x1 * sin], -1).astype(x.dtype)

def dilated_mix(q, k, v, q_idx):
    outs, lses = [], []
    for window, dil in DILATED_CFG:
        offs = dil * jnp.arange(window // dil + 1, dtype=jnp.int32)
        idx = q_idx[:, None] - offs[None, :]
        valid = idx >= 0
        idx = jnp.maximum(idx, 0)
        kg = jnp.take(k, idx, axis=1)
        vg = jnp.take(v, idx, axis=1)
        s = jnp.einsum('bqhd,bqkhd->bhqk', q, kg).astype(jnp.float32)
        s = jnp.where(valid[None, None], s, -jnp.inf)
        lse = jax.nn.logsumexp(s, axis=-1)
        p = jnp.exp(s - lse[..., None]).astype(v.dtype)
        outs.append(jnp.einsum('bhqk,bqkhd->bqhd', p, vg))
        lses.append(lse)
    w = jax.nn.softmax(jnp.stack(lses, 0), axis=0).astype(q.dtype)
    return jnp.einsum('ibhq,ibqhd->bqhd', w, jnp.stack(outs, 0))

def dilated_prompt(q, k, v):
    B, S, H, dh = q.shape
    starts = jnp.arange(S // Q_BLOCK, dtype=jnp.int32) * Q_BLOCK

    def blk(s0):
        qb = lax.dynamic_slice_in_dim(q, s0, Q_BLOCK, axis=1)
        return dilated_mix(qb, k, v, s0 + jnp.arange(Q_BLOCK, dtype=jnp.int32))

    o = lax.map(blk, starts)
    return jnp.moveaxis(o, 0, 1).reshape(B, S, H, dh)

def diff_core(q, k, v, mask, lam):
    s = jnp.einsum('bqhcd,bkhcd->bhcqk', q, k).astype(jnp.float32)
    s = jnp.where(mask, s, -jnp.inf)
    p = jax.nn.softmax(s, axis=-1)
    a = (p[:, :, 0] - lam * p[:, :, 1]).astype(v.dtype)
    return jnp.einsum('bhqk,bkhe->bqhe', a, v)

def diff_prompt(q, k, v, lam):
    B, S = q.shape[:2]
    kpos = jnp.arange(S, dtype=jnp.int32)
    starts = jnp.arange(S // Q_BLOCK, dtype=jnp.int32) * Q_BLOCK

    def blk(s0):
        qb = lax.dynamic_slice_in_dim(q, s0, Q_BLOCK, axis=1)
        qpos = s0 + jnp.arange(Q_BLOCK, dtype=jnp.int32)
        return diff_core(qb, k, v, kpos[None, :] <= qpos[:, None], lam)

    o = lax.map(blk, starts)
    return jnp.moveaxis(o, 0, 1).reshape(B, S, N_HEADS_B, 2 * HEAD_DIM)

def layer(x, c, pos, conv_buf, attend_a, attend_b, lam, lam_init, w_ada, b_ada, w_in, w_o,
          subln_g, ln1_g, ln1_b, w_up, b_up, w_conv, b_conv, w_down, b_down, ln2_g, ln2_b):
    B, S, _ = x.shape
    mod = (jax.nn.silu(c) @ w_ada + b_ada).reshape(B, 6, 1, D_MODEL)
    shift1, scale1, gate1, shift2, scale2, gate2 = [mod[:, i] for i in range(6)]
    h = x * (1 + scale1) + shift1
    proj = h @ w_in
    qa, ka, va, qb, kb, vb = jnp.split(
        proj, [WIDTH_A, 2 * WIDTH_A, 3 * WIDTH_A, 3 * WIDTH_A + WIDTH_B, 3 * WIDTH_A + 2 * WIDTH_B], axis=-1)
    qa = rope(qa.reshape(B, S, N_HEADS_A, HEAD_DIM), pos) * HEAD_DIM ** -0.5
    ka = rope(ka.reshape(B, S, N_HEADS_A, HEAD_DIM), pos)
    va = va.reshape(B, S, N_HEADS_A, HEAD_DIM)
    qb = rope(qb.reshape(B, S, N_HEADS_B, 2, HEAD_DIM), pos) * HEAD_DIM ** -0.5
    kb = rope(kb.reshape(B, S, N_HEADS_B, 2, HEAD_DIM), pos)
    vb = vb.reshape(B, S, N_HEADS_B, 2 * HEAD_DIM)
    oa, win_state = attend_a(qa, ka, va)
    ob = rms_norm(attend_b(qb, kb, vb, lam), subln_g) * (1.0 - lam_init)
    mixed = jnp.concatenate([oa.reshape(B, S, WIDTH_A), ob.reshape(B, S, WIDTH_B)], -1) @ w_o
    x = layer_norm(DEEPNORM_ALPHA * x + gate1 * mixed, ln1_g, ln1_b)
    h = x * (1 + scale2) + shift2
    u = h @ w_up + b_up
    ext = jnp.concatenate([conv_buf.astype(u.dtype), u], 1)
    uc = b_conv + sum(ext[:, j:j + S] * w_conv[j] for j in range(CONV_W))
    a, g = jnp.split(uc, 2, axis=-1)
    y = (jax.nn.gelu(a, approximate=False) * g) @ w_down + b_down
    x = layer_norm(DEEPNORM_ALPHA * x + gate2 * y, ln2_g, ln2_b)
    kv_rows = (kb.reshape(B, S, N_HEADS_B, 2 * HEAD_DIM), vb)
    return x, win_state, kv_rows, ext[:, S:]

def setup_inputs(seed: int = 0) -> dict:
    key = jax.random.key(seed)
    ks = jax.random.split(key, 32)
    f32 = jnp.float32
    n_pages = PAST_LEN // PAGE_SIZE
    n_used = DEC_BATCH * n_pages
    n_pool = n_used + n_used // 4
    win_len = min(WIN_MAX, PAST_LEN)

    def nrm(k, shape, scale=1.0):
        return jax.random.normal(k, shape, f32) * scale

    col = jnp.arange(3 * MIX_WIDTH)
    is_v = ((col >= 2 * WIDTH_A) & (col < 3 * WIDTH_A)) | (col >= 3 * WIDTH_A + 2 * WIDTH_B)
    w_in = nrm(ks[12], (DEPTH, D_MODEL, 3 * MIX_WIDTH), D_MODEL ** -0.5) * jnp.where(is_v, DEEPNORM_BETA, 1.0)
    page_table = jax.random.permutation(ks[9], n_pool)[:n_used].reshape(DEC_BATCH, n_pages).astype(jnp.int32)
    return {
        'x_prompt': nrm(ks[0], (BATCH, SEQ, D_MODEL)),
        'x_sample': nrm(ks[1], (DEC_BATCH, DEC_SEQ, D_MODEL)),
        'cache_win_k': nrm(ks[2], (DEPTH, DEC_BATCH, win_len, N_HEADS_A, HEAD_DIM)),
        'cache_win_v': nrm(ks[3], (DEPTH, DEC_BATCH, win_len, N_HEADS_A, HEAD_DIM)),
        'cache_k': nrm(ks[4], (DEPTH, n_pool, PAGE_SIZE, N_HEADS_B, 2 * HEAD_DIM)),
        'cache_v': nrm(ks[5], (DEPTH, n_pool, PAGE_SIZE, N_HEADS_B, 2 * HEAD_DIM)),
        'state_conv': nrm(ks[6], (DEPTH, DEC_BATCH, CONV_W - 1, 2 * D_FF)),
        'page_table': page_table,
        'c_prompt': nrm(ks[7], (BATCH, D_MODEL)),
        'c_sample': nrm(ks[8], (DEC_BATCH, D_MODEL)),
        'w_ada': nrm(ks[10], (DEPTH, D_MODEL, 6 * D_MODEL), D_MODEL ** -0.5),
        'b_ada': nrm(ks[11], (DEPTH, 6 * D_MODEL), 0.02),
        'w_in': w_in,
        'w_o': nrm(ks[13], (DEPTH, MIX_WIDTH, D_MODEL), MIX_WIDTH ** -0.5 * DEEPNORM_BETA),
        'lambda_q1': nrm(ks[14], (DEPTH, HEAD_DIM), 0.1),
        'lambda_k1': nrm(ks[15], (DEPTH, HEAD_DIM), 0.1),
        'lambda_q2': nrm(ks[16], (DEPTH, HEAD_DIM), 0.1),
        'lambda_k2': nrm(ks[17], (DEPTH, HEAD_DIM), 0.1),
        'subln_g': 1.0 + nrm(ks[18], (DEPTH, 2 * HEAD_DIM), 0.02),
        'ln1_g': 1.0 + nrm(ks[19], (DEPTH, D_MODEL), 0.02),
        'ln1_b': nrm(ks[20], (DEPTH, D_MODEL), 0.02),
        'w_up': nrm(ks[21], (DEPTH, D_MODEL, 2 * D_FF), D_MODEL ** -0.5),
        'b_up': nrm(ks[22], (DEPTH, 2 * D_FF), 0.02),
        'w_conv': nrm(ks[23], (DEPTH, CONV_W, 2 * D_FF), CONV_W ** -0.5),
        'b_conv': nrm(ks[24], (DEPTH, 2 * D_FF), 0.02),
        'w_down': nrm(ks[25], (DEPTH, D_FF, D_MODEL), D_FF ** -0.5 * DEEPNORM_BETA),
        'b_down': nrm(ks[26], (DEPTH, D_MODEL), 0.02),
        'ln2_g': 1.0 + nrm(ks[27], (DEPTH, D_MODEL), 0.02),
        'ln2_b': nrm(ks[28], (DEPTH, D_MODEL), 0.02),
    }

def reference(x_prompt, x_sample, cache_win_k, cache_win_v, cache_k, cache_v, state_conv, page_table,
              c_prompt, c_sample, w_ada, b_ada, w_in, w_o, lambda_q1, lambda_k1, lambda_q2, lambda_k2,
              subln_g, ln1_g, ln1_b, w_up, b_up, w_conv, b_conv, w_down, b_down, ln2_g, ln2_b):
    f32 = jnp.float32
    B, S, _ = x_prompt.shape
    DB, DS, _ = x_sample.shape
    P = page_table.shape[1] * cache_k.shape[2]
    pos_p = jnp.arange(S, dtype=jnp.int32)
    pos_s = P + jnp.arange(DS, dtype=jnp.int32)
    lp = min(WIN_MAX, S)
    hp, hs = x_prompt, x_sample
    wkp_l, wvp_l, wks_l, wvs_l, kp_l, vp_l, ks_l, vs_l, cp_l, cs_l = ([] for _ in range(10))
    for l in range(DEPTH):
        lam_init = 0.8 - 0.6 * math.exp(-0.3 * l)
        lam = (jnp.exp(jnp.sum(lambda_q1[l].astype(f32) * lambda_k1[l].astype(f32)))
               - jnp.exp(jnp.sum(lambda_q2[l].astype(f32) * lambda_k2[l].astype(f32))) + lam_init)
        wts = (w_ada[l], b_ada[l], w_in[l], w_o[l], subln_g[l], ln1_g[l], ln1_b[l], w_up[l], b_up[l],
               w_conv[l], b_conv[l], w_down[l], b_down[l], ln2_g[l], ln2_b[l])

        def attend_a_prompt(q, k, v):
            return dilated_prompt(q, k, v), (k[:, S - lp:], v[:, S - lp:])

        hp, (wkp, wvp), (kp, vp), cp = layer(
            hp, c_prompt, pos_p, jnp.zeros((B, CONV_W - 1, 2 * D_FF), hp.dtype),
            attend_a_prompt, diff_prompt, lam, lam_init, *wts)

        cwk, cwv = cache_win_k[l], cache_win_v[l]
        ck, cv = cache_k[l], cache_v[l]

        def attend_a_sample(q, k, v):
            L = cwk.shape[1]
            kk = jnp.concatenate([cwk.astype(k.dtype), k], 1)
            vv = jnp.concatenate([cwv.astype(v.dtype), v], 1)
            o = dilated_mix(q, kk, vv, L + jnp.arange(DS, dtype=jnp.int32))
            return o, (kk[:, DS:], vv[:, DS:])

        def attend_b_sample(q, k, v, lam_):
            pk = ck[page_table].reshape(DB, P, N_HEADS_B, 2, HEAD_DIM).astype(k.dtype)
            pv = cv[page_table].reshape(DB, P, N_HEADS_B, 2 * HEAD_DIM).astype(v.dtype)
            kk = jnp.concatenate([pk, k], 1)
            vv = jnp.concatenate([pv, v], 1)
            j = jnp.arange(P + DS, dtype=jnp.int32)
            s = jnp.arange(DS, dtype=jnp.int32)
            mask = (j[None, :] < P) | ((j[None, :] - P) <= s[:, None])
            return diff_core(q, kk, vv, mask, lam_)

        hs, (wks, wvs), (ksn, vsn), cs = layer(
            hs, c_sample, pos_s, state_conv[l], attend_a_sample, attend_b_sample, lam, lam_init, *wts)

        wkp_l.append(wkp); wvp_l.append(wvp); wks_l.append(wks); wvs_l.append(wvs)
        kp_l.append(kp); vp_l.append(vp); ks_l.append(ksn); vs_l.append(vsn)
        cp_l.append(cp); cs_l.append(cs)
    return (hp, hs,
            jnp.stack(wkp_l, 0), jnp.stack(wvp_l, 0), jnp.stack(wks_l, 0), jnp.stack(wvs_l, 0),
            jnp.stack(kp_l, 0), jnp.stack(vp_l, 0), jnp.stack(ks_l, 0), jnp.stack(vs_l, 0),
            jnp.stack(cp_l, 0), jnp.stack(cs_l, 0))


_drawn_inputs = setup_inputs


def setup_inputs(seed=0):
    import zlib

    import numpy as np

    out = dict(_drawn_inputs(seed))
    spreads = {}
    factors = {'lambda_q1': 200.0,
     'lambda_k1': 3.403,
     'subln_g': 69.967,
     'ln1_g': 2.741,
     'ln1_b': 2.845,
     'b_up': 3.754,
     'b_conv': 8.0,
     'b_down': 18.325,
     'ln2_g': 29.978,
     'ln2_b': 26.356}
    for name, (base, spread) in spreads.items():
        noise = np.random.default_rng([zlib.crc32(name.encode()), seed]).standard_normal(out[name].shape)
        drawn = base * np.exp(spread * noise) if base else spread * noise
        out[name] = __import__('jax').numpy.asarray(drawn.astype(out[name].dtype))
    for name, factor in factors.items():
        out[name] = (out[name] * factor).astype(out[name].dtype)
    return out
```

```python
from contextlib import ExitStack

import concourse.bass as bass
from concourse import mybir

P = 128
F32 = mybir.dt.float32
I32 = mybir.dt.int32
ALU = mybir.AluOpType
ACT = mybir.ActivationFunctionType
AX_X = mybir.AxisListType.X

D = 1024
KT_D = D // P
SEQ = 512
TP = SEQ // P
DB, DS = 8, 8
NS = DB * DS
NT = SEQ + NS
HALF_NT = NT // 2
PAST = 2048
PAGE = 128
N_PAGES = PAST // PAGE
WID = 512
MAPS = 8
DFF = 2816
FT = DFF // P
CH = 512
N_SLOTS = 4
SLOT = KT_D * CH
NEG = 3.0e38
BIG = 1.0e30
EPS = 1e-5
ALPHA = 2.0 ** 0.25
LAM_INIT = 0.2
C = 1 + DB
A_TILES = 10
B_TILES = N_PAGES

CHUNKS = [("ada", i) for i in range(4)] + [("in", i) for i in range(6)] + [("ada", i) for i in range(4, 12)] \
    + [("o", i) for i in range(2)] + [("up", i) for i in range(11)] + [("down", i) for i in range(6)]
SLOT_OF = [0, 1, 2, 3] + [0, 1, 2] * 2 + [0, 1, 2, 0, 1, 2, 0, 1] + [i % N_SLOTS for i in range(19)]
CHUNK_AT = {c: i for i, c in enumerate(CHUNKS)}


def loads_of_slot(n):
    return sum(SLOT_OF[i] == SLOT_OF[n] for i in range(n + 1))


def chunk_before(n):
    return max((i for i in range(n) if SLOT_OF[i] == SLOT_OF[n]), default=None)


def build(nc, a, o):
    ctx = ExitStack()
    with ctx:
        def sb(name, shape, dt=F32):
            return ctx.enter_context(nc.sbuf_tensor(name, shape, dt))

        def sem(name):
            return ctx.enter_context(nc.semaphore(name))

        wide = [ctx.enter_context(nc.psum_tensor(f"wide{i}", [P, 1024], F32)) for i in range(4)]

        def bk(i):
            return wide[i // 2][:, 512 * (i % 2):512 * (i % 2) + 512]

        ring = sb("ring", [P, N_SLOTS * SLOT])
        x_sb = sb("x_sb", [P, TP + 1, D])
        ht = sb("ht", [P, KT_D, NT])
        mix = sb("mix", [P, TP * D])
        room = sb("room", [P, 19712])
        ident = sb("ident", [P, P])
        perm = sb("perm", [P, P])
        maskt = sb("maskt", [P, 2, SEQ])
        smask = sb("smask", [P, 384])
        sums = sb("sums", [P, 2, P])
        pick = sb("pick", [P, 32])
        colmask = sb("colmask", [P, P])
        sum9 = sb("sum9", [P, C])
        ones = sb("ones", [P, P])
        diff_c = sb("diff_c", [P, 2])
        vec_t = sb("vec_t", [P, 3, P])
        bada = sb("bada", [P, 48])
        mod_t = sb("mod_t", [P, 48, C])
        c_t = sb("c_t", [P, KT_D, C])
        lam_s = sb("lam_s", [P, 8])
        mn = sb("mn", [P, 64])
        rs = sb("rs", [P, 64])
        rcp = sb("rcp", [P, 64])
        rms = sb("rms", [P, 3, 16])
        pages = sb("pages", [1, DB * N_PAGES], I32)
        stat = sb("stat", [P, 2, 6])
        mv = sb("mv", [P, 4])
        g8 = sb("g8", [P, 1])

        def slot(i):
            return ring[:, i * SLOT:(i + 1) * SLOT].rearrange("p (k n) -> p k n", k=KT_D)

        def part(t, at, n):
            return t[:, at:at + n]

        vec_r = room[:, 0:3 * P].rearrange("p (r d) -> p r d", r=3)
        c_r = room[0:C, 512:512 + D]
        c_e = room[0:C, 1536:1536 + D]
        c_s = room[0:C, 2560:2560 + D]
        lam4 = part(room, 3584, 256).rearrange("p (n d) -> p n d", n=4)
        mod_s = ht[:, :, :].rearrange("p k t -> p (k t)")[:, 0:2 * CH].rearrange("p (b n) -> p b n", b=2)
        qtp = part(room, 0, 8192).rearrange("p (n t) -> p n t", n=16)
        kt = part(room, 8192, 4096).rearrange("p (f t) -> p f t", f=8)
        vp = part(room, 12288, 4096).rearrange("p (t m d) -> p t m d", t=TP, m=2)
        tmp_a = part(room, 16384, 1024).rearrange("p (b n) -> p b n", b=2)
        tmp_b = part(room, 17408, 1024).rearrange("p (b n) -> p b n", b=2)
        rope = part(room, 18432, 1280).rearrange("p (t w n) -> p t w n", t=TP + 1, w=2)
        s_m = part(room, 16384, 1024).rearrange("p (b n) -> p b n", b=2)
        p_b = part(room, 17408, 1024).rearrange("p (b n) -> p b n", b=2)
        pt_b = part(room, 18432, 1024).rearrange("p (b n) -> p b n", b=2)
        o_1 = part(room, 19456, 128)
        stage = mix[:, 0:2048].rearrange("p (b n) -> p b n", b=4)
        mixv = mix[:, :].rearrange("p (t d) -> p t d", t=TP)
        keep = 3 * SLOT
        qrep = part(ring, keep, 2048).rearrange("p (m g t) -> p m g t", m=2, g=16)
        k_s = ring[0:NS, keep + 2048:keep + 3072].rearrange("p (m d) -> p m d", m=2)
        v_s = ring[0:NS, keep + 3072:keep + 4096].rearrange("p (m d) -> p m d", m=2)
        NK, NV = 3, 5
        kraw = part(ring, 0, NK * 2048).rearrange("p (b t d) -> p b t d", b=NK, t=4)
        ktg = part(ring, NK * 2048, NK * 2048).rearrange("p (b g n) -> p b g n", b=NK, g=16)
        vg = part(room, 0, NV * 2048).rearrange("p (b i d) -> p b i d", b=NV, i=4)
        o_s = part(room, 10240, 2048).rearrange("p (w d) -> p w d", w=16)
        kn = part(room, 12288, 1024).rearrange("p (b d) -> p b d", b=2)
        ktn = part(room, 13312, 1024).rearrange("p (b g n) -> p b g n", b=2, g=16)
        vn = part(room, 14336, 1024).rearrange("p (b d) -> p b d", b=2)
        p_s = part(room, 15360, 1088).rearrange("p (b n) -> p b n", b=2)
        pt_s = part(room, 16448, 1024).rearrange("p (b n) -> p b n", b=2)
        ptn = part(room, 17472, 256).rearrange("p (b n) -> p b n", b=2)
        sm_s = part(room, 17728, 704).rearrange("p (b n) -> p b n", b=2)
        qbd = part(room, 18432, 1024).rearrange("p (b g i q) -> p b g i q", b=2, g=16, i=4)
        small = part(room, 19456, 256)
        blk = small[:, 0:32]
        blk_t = small[:, 32:64]
        blk_r = small[:, 64:96]
        blk_o = small[:, 96:128]
        rs_s = small[:, 128:160].rearrange("p (h w) -> p h w", h=2)
        l_s = small[:, 160:176]
        ob_t = part(room, 0, 256)
        ob_q = part(room, 256, 256)
        ob_r = part(room, 512, 256)
        gate = mix[:, 0:2048].rearrange("p (s d) -> p s d", s=2)
        gate2 = mix[:, 2048:4096].rearrange("p (s d) -> p s d", s=2)
        ln1 = part(room, 1024, 2048).rearrange("p (w d) -> p w d", w=2)
        y_sb = part(room, 3072, 2048).rearrange("p (b d) -> p b d", b=2)
        st_r = room[0:16, 5120:5120 + 2 * DFF]
        ln2 = part(room, 12672, 3072).rearrange("p (w d) -> p w d", w=3)
        gt = part(room, 0, FT * NT).rearrange("p (f t) -> p f t", f=FT)
        u_b = part(room, 15744, 2 * (NT + 2)).rearrange("p (b n) -> p b n", b=2)
        cv = part(room, 16900, 2 * NT).rearrange("p (b n) -> p b n", b=2)
        ga = part(room, 18052, 2 * NT).rearrange("p (b n) -> p b n", b=2)
        ext = part(room, 19204, 160).rearrange("p (b s t) -> p b s t", b=2, s=DB)
        st_t = mix[:, 0:704].rearrange("p (f r) -> p f r", f=2 * FT)
        u_last = mix[:, 704:704 + 792].rearrange("p (f r) -> p f r", f=2 * FT)
        y3 = part(room, 16900, 1024).rearrange("p (b n) -> p b n", b=2)
        gexp = part(room, 3072, 1024).rearrange("p (g b s) -> p g b s", g=16, b=DB)

        def conv_out(i):
            h = ht[:, :, :].rearrange("p k t -> p (k t)")
            return h[0:18, 512 * i:512 * i + 512] if i < 9 else part(room, 15744, 1024)[0:18, 512 * (i - 9):512 * (i - 8)]

        early = sem("early_loaded")
        tables = sem("tables_loaded")
        x_in = sem("x_loaded")
        w_in_slot = [sem(f"w_loaded_{i}") for i in range(N_SLOTS)]
        w_used = sem("w_used")
        vecs_t = sem("vecs_transposed")
        vecs_c = sem("vecs_copied")
        act_setup = sem("act_setup")
        dve_seq = sem("dve_seq")
        act_seq = sem("act_seq")
        pool_seq = sem("pool_seq")
        c_tr = sem("c_transposed")
        c_cp = sem("c_copied")
        bank6_zero = sem("bank6_zero")
        ada_mm = sem("ada_product")
        ada_ms = sem("ada_rows_copied")
        ada_tt = sem("ada_transposed")
        ada_ok = sem("ada_ready")
        xt_mm = sem("xt_transposed")
        xt_d = sem("xt_taken_dve")
        xt_a = sem("xt_taken_act")
        pj_mm = sem("proj_product")
        pj_d = sem("proj_taken_dve")
        pj_a = sem("proj_taken_act")
        rope_ok = sem("rope_done")
        qk_t = sem("qk_transposed")
        qk_d = sem("qk_taken_dve")
        qk_a = sem("qk_taken_act")
        qzero = sem("qtp_zeroed")
        stg = [sem(f"stage_stored_{i}") for i in range(4)]
        out_sem = sem("rows_stored")
        pa_s = sem("pa_scores")
        pa_min = sem("pa_masked")
        pa_exp = sem("pa_exp")
        pa_t = sem("pa_transposed")
        pa_pt = sem("pa_pt_copied")
        pa_pv = sem("pa_pv")
        pa_o = sem("pa_out_taken")
        rms_sq = sem("rms_sums")
        rms_rt = sem("rms_roots")
        rms_ok = sem("rms_done")
        kg_in = [sem(f"k_group_loaded_{i}") for i in range(NK)]
        vg_in = [sem(f"v_group_loaded_{i}") for i in range(NV)]
        new_in = [sem(f"new_rows_loaded_{i}") for i in range(2)]
        new_zero = sem("new_zeroed")
        kg_t = sem("k_group_turned")
        kn_t = sem("k_new_turned")
        q_bd = sem("q_spread")
        sa_g = sem("sa_group_scored")
        sa_s = sem("sa_scores")
        sa_min = sem("sa_min")
        sa_exp = sem("sa_exp")
        sa_t = sem("sa_transposed")
        sa_pt = sem("sa_pt_copied")
        sa_vg = sem("sa_group_weighted")
        sa_pv = sem("sa_pv")
        sa_o = sem("sa_out_taken")
        sa_l = sem("sa_sums")
        sa_n = sem("sa_normed")
        sa_x = sem("sa_picked")
        sa_fin = sem("sa_placed")
        sa_sq = sem("sa_square_sums")
        sa_q = sem("sa_mean_squares")
        sa_r = sem("sa_roots")
        page_in = sem("pages_loaded")
        mt_mm = sem("mixed_transposed")
        mt_d = sem("mixed_taken")
        gb_mm = sem("gate_spread")
        gb_a = sem("gate_copied")
        ln_in = sem("ln_rows_loaded")
        ln2_in = sem("ln2_rows_loaded")
        wo_mm = sem("wo_product")
        wo_d = sem("wo_taken")
        n_var = sem("norm_variance")
        n_rt = sem("norm_root")
        x1_ok = sem("x1_ready")
        st_in = sem("state_loaded")
        st_mm = sem("state_transposed")
        st_ok = sem("state_ready")
        h2_mm = sem("h2_transposed")
        h2_d = sem("h2_taken_dve")
        h2_a = sem("h2_taken_act")
        up_mm = sem("up_product")
        up_u = sem("up_taken")
        up_c0 = sem("conv_started")
        up_x = sem("ext_ready")
        up_cv = sem("conv_done")
        up_ge = sem("gelu_done")
        up_gt = sem("gated")
        halo = sem("halo_zeroed")
        us_mm = sem("last_rows_transposed")
        us_a = sem("last_rows_copied")
        dn_mm = sem("down_product")
        dn_d = sem("down_taken")
        y_out = sem("y_ready")
        stored = sem("stored")
        copied = sem("window_copied")
        block = ctx.enter_context(nc.Block())

        units = [(s, t) for s in range(6) for t in range(TP + 1)]
        rope_units = [n for n, (s, t) in enumerate(units) if s in (0, 1, 3, 4)]
        v_units = [n for n, (s, t) in enumerate(units) if s in (2, 5)]
        tr_units = [n for n in rope_units if not (units[n][0] in (1, 4) and units[n][1] == TP)]
        pa = [(0, n, qb) for n in range(8) for qb in range(4)] \
            + [(1, 2 * h + c, qb) for h in range(4) for qb in range(4) for c in range(2)]
        NU = len(pa)
        sa = [(m, b) for b in range(DB) for m in range(2)]
        groups = {0: [4, 4, 2], 1: [4, 4, 4, 4]}
        NG = [sum(len(groups[m]) for m, b in sa[:w]) for w in range(17)]

        def d_units(n):
            return sum(k in rope_units for k in range(n + 1))

        def a_units(n):
            return sum(k in v_units for k in range(n + 1))

        last_t, last_store, n_stored = [], [], [0] * 4
        user = [None] * 4
        for r, n in enumerate(rope_units):
            sec, t = units[n]
            last_t.append(None if user[r % 4] is None else tr_units.index(user[r % 4]) + 1)
            last_store.append(n_stored[r % 4])
            if not (sec in (1, 4) and t == TP):
                user[r % 4] = n
                n_stored[r % 4] += sec in (1, 4)

        def up_bank(k):
            return wide[k % 3][:, :].rearrange("p (h t) -> p h t", h=2)[:, :, 0:HALF_NT]

        def slot_count(n):
            return 16 * sum(2 if CHUNKS[i][0] == "up" else 1 for i in range(n + 1) if SLOT_OF[i] == SLOT_OF[n])

        def k_count(m, w, g):
            G = NG[w] + g
            return 64 * (G // NK + 1)

        def v_count(m, w, g):
            G = NG[w] + g
            return 64 * (G // NV + 1)

        @block.sync
        def _(sp):
            def load_chunk(n):
                kind, i = CHUNKS[n]
                if (prev := chunk_before(n)) is not None:
                    sp.wait_ge(w_used, prev + 1)
                s = w_in_slot[SLOT_OF[n]]
                dst = slot(SLOT_OF[n])
                src = a[{"ada": "w_ada", "in": "w_in", "o": "w_o", "up": "w_up", "down": "w_down"}[kind]][0]
                src = src.rearrange("(k p) n -> p k n", p=P)
                if kind == "up":
                    for g in range(2):
                        sp.dma_start(dst[:, :, 256 * g:256 * g + 256],
                                     src[:, :, DFF * g + 256 * i:DFF * g + 256 * i + 256]).then_inc(s, 16)
                elif kind == "down":
                    half, kg = divmod(i, 3)
                    nk = min(8, FT - 8 * kg)
                    sp.dma_start(dst[:, 0:nk, :], src[:, 8 * kg:8 * kg + nk, CH * half:CH * half + CH]).then_inc(s, 16)
                else:
                    sp.dma_start(dst, src[:, :, CH * i:CH * i + CH]).then_inc(s, 16)

            sp.dma_start(ident[:, :], a["ident"]).then_inc(early, 16)
            sp.dma_start(c_r[0:1, :], a["c_prompt"]).then_inc(early, 16)
            sp.dma_start(c_r[1:C, :], a["c_sample"]).then_inc(early, 16)
            rows = lambda name: a[name].rearrange("l (r d) -> (l r) d", d=P)
            conv = a["w_conv"].rearrange("l j (r d) -> (l j) r d", d=P)
            sp.dma_start(vec_r[0:48, 0, :], rows("b_ada")).then_inc(early, 16)
            sp.dma_start(vec_r[48:92, 0, :], rows("b_up")).then_inc(early, 16)
            sp.dma_start(vec_r[92:93, 0, :], a["subln_g"]).then_inc(early, 16)
            sp.dma_start(vec_r[0:44, 1, :], conv[0]).then_inc(early, 16)
            sp.dma_start(vec_r[44:88, 1, :], conv[1]).then_inc(early, 16)
            sp.dma_start(vec_r[0:44, 2, :], conv[2]).then_inc(early, 16)
            sp.dma_start(vec_r[44:88, 2, :], rows("b_conv")).then_inc(early, 16)
            sp.dma_start(sum9[:, :], a["sum9"]).then_inc(early, 16)
            for i, name in enumerate(("lambda_q1", "lambda_k1", "lambda_q2", "lambda_k2")):
                sp.dma_start(lam4[:, i, :], a[name].to_broadcast([P, 64])).then_inc(early, 16)
            load_chunk(0)
            load_chunk(1)
            sp.dma_start(x_sb[0:NS, TP, :], a["x_sample"].rearrange("b s d -> (b s) d")).then_inc(x_in, 16)
            sp.dma_start(x_sb[:, 0:TP, :], a["x_prompt"][0].rearrange("(t p) d -> p t d", p=P)).then_inc(x_in, 16)
            load_chunk(2)
            load_chunk(3)
            for dst, name in ((rope, "rope"), (maskt, "maskt"), (smask, "smask"), (sums, "sums"), (pick, "pick"),
                              (colmask, "colmask"), (ones, "ones"), (diff_c, "diff_c"), (perm, "perm")):
                if name != "rope":
                    dst = dst[:]
                sp.dma_start(dst, a[name]).then_inc(tables, 16)
            sp.dma_start(pages[:, :], a["page_table"].rearrange("b n -> (b n)").rearrange("(o n) -> o n", o=1)).then_inc(page_in, 16)
            for n in range(4, 7):
                load_chunk(n)

            def move_window(i):
                for name, dst in (("cache_win_k", "wks"), ("cache_win_v", "wvs")):
                    sp.dma_start(o[dst][0, i, 0:PAST - DS], a[name][0, i, DS:PAST]).then_inc(copied, 16)

            def flat(ap):
                return ap.rearrange("t h d -> t (h d)")

            n_rope = n_v = 0
            for n, (s, t) in enumerate(units):
                kb_rows = slice(P * t, P * t + P)
                if s in (0, 3):
                    n_rope += 1
                elif s in (1, 4):
                    m = s // 3
                    sp.wait_ge(rope_ok, n_rope + 1)
                    if t < TP:
                        st = n_rope % 4
                        dst = flat((o["wkp"] if m == 0 else o["kkp"])[0, 0])[kb_rows, :]
                        sp.dma_start(dst, stage[:, st, :]).then_inc(stg[st], 16)
                    else:
                        if m == 0:
                            for b in range(DB):
                                sp.dma_start(flat(o["wks"][0, b])[PAST - DS:PAST, :],
                                             k_s[DS * b:DS * b + DS, 0, :]).then_inc(out_sem, 16)
                        else:
                            sp.dma_start(o["kks"][0].rearrange("b s h d -> (b s) (h d)"), k_s[:, 1, :]).then_inc(out_sem, 16)
                    n_rope += 1
                else:
                    m = s // 3
                    n_v += 1
                    sp.wait_ge(pj_a, n_v)
                    if t < TP:
                        dst = flat((o["wvp"] if m == 0 else o["kvp"])[0, 0])[kb_rows, :]
                        sp.dma_start(dst, vp[:, t, m, :]).then_inc(out_sem, 16)
                    elif m == 0:
                        for b in range(DB):
                            sp.dma_start(flat(o["wvs"][0, b])[PAST - DS:PAST, :],
                                         v_s[DS * b:DS * b + DS, 0, :]).then_inc(out_sem, 16)
                    else:
                        sp.dma_start(o["kvs"][0].rearrange("b s h d -> (b s) (h d)"), v_s[:, 1, :]).then_inc(out_sem, 16)
                if t == TP:
                    move_window(s)
                    load_chunk(7 + s)
            for n in range(13, 18):
                load_chunk(n)

            flat_k = {0: a["cache_win_k"][0], 1: a["cache_k"][0]}
            flat_v = {0: a["cache_win_v"][0], 1: a["cache_v"][0]}
            sp.wait_ge(page_in, 16)
            sp.wait_ge(w_used, 18)
            sp.wait_ge(pa_pv, NU)
            sp.wait_ge(pa_o, NU)
            sp.wait_ge(out_sem, 16 * (TP * 2 + 2 * DB + 2))
            sp.wait_ge(new_zero, 1)
            for w, (m, b) in enumerate(sa):
                nw = w % 2
                if w >= 2:
                    sp.wait_ge(kn_t, w - 1)
                    sp.wait_ge(sa_pv, w - 1)
                sp.dma_start(kn[0:DS, nw, :], k_s[DS * b:DS * b + DS, m, :]).then_inc(new_in[nw], 16)
                sp.dma_start(vn[0:DS, nw, :], v_s[DS * b:DS * b + DS, m, :]).then_inc(new_in[nw], 16)
                win_k = flat_k[0][b].rearrange("(g r) h d -> g r (h d)", r=16)
                win_v = flat_v[0][b].rearrange("(g r) h d -> g r (h d)", r=16)
                for g, nt in enumerate(groups[m]):
                    G = NG[w] + g
                    ks, vs = G % NK, G % NV
                    if G >= NK:
                        sp.wait_ge(kg_t, G - NK + 1)
                    if m == 0 and g < 2:
                        sp.dma_start(kraw[:, ks, :, :], win_k[:, 4 * g:4 * g + 4, :]).then_inc(kg_in[ks], 64)
                    elif m == 0:
                        for i in range(4):
                            sp.dma_start(kraw[32 * i:32 * i + 32, ks, 0:2, :],
                                         win_k[96:128, 8 + i:16:4, :]).then_inc(kg_in[ks], 16)
                    else:
                        for t in range(4):
                            pg = sp.value_load(pages[0:1, N_PAGES * b + 4 * g + t:N_PAGES * b + 4 * g + t + 1],
                                               min_val=0, max_val=a["cache_k"].shape[1] - 1)
                            sp.dma_start(kraw[:, ks, t, :], flat_k[1][bass.ds(pg, 1)].rearrange("a p h d -> (a p) (h d)"))\
                                .then_inc(kg_in[ks], 16)
                    if G >= NV:
                        sp.wait_ge(sa_vg, G - NV + 1)
                    if m == 0 and g < 2:
                        for t in range(4):
                            r = 4 * g + t
                            sp.dma_start(vg[32 * t:32 * t + 32, vs, :, :],
                                         win_v[:, r, :].rearrange("(i m) f -> m i f", i=4)).then_inc(vg_in[vs], 16)
                    elif m == 0:
                        for t in range(2):
                            sp.dma_start(vg[32 * t:32 * t + 32, vs, :, :],
                                         win_v[96:128, 8 + 4 * t:12 + 4 * t, :]).then_inc(vg_in[vs], 32)
                    else:
                        for t in range(4):
                            pg = sp.value_load(pages[0:1, N_PAGES * b + 4 * g + t:N_PAGES * b + 4 * g + t + 1],
                                               min_val=0, max_val=a["cache_v"].shape[1] - 1)
                            sp.dma_start(vg[32 * t:32 * t + 32, vs, :, :],
                                         flat_v[1][bass.ds(pg, 1)].rearrange("a (i m) h d -> m (a i) (h d)", i=4))\
                                .then_inc(vg_in[vs], 16)
            for i in range(6, 8):
                move_window(i)

            sp.wait_ge(sa_fin, 2)
            for n in range(18, 22):
                load_chunk(n)
            for i, name in enumerate(("ln1_g", "ln1_b")):
                sp.dma_start(ln1[:, i, :], a[name].to_broadcast([P, D])).then_inc(ln_in, 16)
            for i, name in enumerate(("b_down", "ln2_g", "ln2_b")):
                sp.dma_start(ln2[:, i, :], a[name].to_broadcast([P, D])).then_inc(ln2_in, 16)
            sp.dma_start(st_r, a["state_conv"][0].rearrange("b j f -> (b j) f")).then_inc(st_in, 16)
            for n in range(22, len(CHUNKS)):
                load_chunk(n)
            for i in range(11):
                sp.wait_ge(us_a, i + 1)
                sp.dma_start(o["cp"][0, 0][:, 512 * i:512 * i + 512], conv_out(i)[0:2, :]).then_inc(stored, 16)
                sp.dma_start(o["cs"][0].rearrange("b j f -> (b j) f")[:, 512 * i:512 * i + 512],
                             conv_out(i)[2:18, :]).then_inc(stored, 16)
            for t in range(TP + 1):
                sp.wait_ge(y_out, t + 1)
                if t < TP:
                    sp.dma_start(o["yp"][0, P * t:P * t + P, :], x_sb[:, t, :]).then_inc(stored, 16)
                else:
                    sp.dma_start(o["ys"].rearrange("b s d -> (b s) d"), x_sb[0:NS, t, :]).then_inc(stored, 16)
            sp.wait_ge(stored, 16 * (22 + TP + 1))
            sp.wait_ge(copied, 16 * 2 * DB)
            sp.wait_ge(out_sem, 16 * (TP * 2 + 2 * DB + 2))
            for st in range(4):
                sp.wait_ge(stg[st], 16 * n_stored[st])

        @block.gpsimd
        def _(pool):
            pool.wait_ge(c_tr, 1)
            pool.wait_ge(vecs_c, 1)
            nc.gpsimd.memset(qtp, 0.0).then_inc(qzero, 1)
            for r, n in enumerate(rope_units):
                s, t = units[n]
                sample_k = s in (1, 4) and t == TP
                pool.wait_ge(pj_d, r + 1)
                if not sample_k and r >= 4:
                    if (prev := last_t[r]) is not None:
                        pool.wait_ge(qk_t, prev)
                    if (q := last_store[r]) > 0:
                        pool.wait_ge(stg[r % 4], 16 * q)
                rows = P if t < TP else NS
                dst = k_s[:, s // 3, :] if sample_k else stage[0:rows, r % 4, :]
                nc.gpsimd.tensor_tensor(dst, tmp_a[0:rows, r % 2, :], tmp_b[0:rows, r % 2, :], ALU.add)\
                    .then_inc(rope_ok, 1)
            pool.wait_ge(pa_pv, NU)
            pool.wait_ge(pa_o, NU)
            nc.gpsimd.memset(kn, 0.0).then_inc(pool_seq, 1)
            nc.gpsimd.memset(ktn, 0.0).then_inc(pool_seq, 1)
            nc.gpsimd.memset(small, 0.0).then_inc(pool_seq, 1)
            nc.gpsimd.memset(qbd, 0.0).then_inc(new_zero, 1)
            pool.wait_ge(new_zero, 1)
            pool.wait_ge(qk_d, len(tr_units) - 2 * TP)
            for w, (m, b) in enumerate(sa):
                if w >= 2:
                    pool.wait_ge(sa_s, w - 1)
                for i in range(4):
                    last = nc.gpsimd.tensor_copy(qbd[32 * i:32 * i + 32, w % 2, :, i, :],
                                                 qrep[32 * i:32 * i + 32, m, :, DS * b:DS * b + DS])
                last.then_inc(q_bd, 1)
            pool.wait_ge(sa_fin, 2)
            nc.gpsimd.memset(u_b[:, :, 0:2], 0.0).then_inc(halo, 1)
            pool.wait_ge(st_ok, 11)
            for k in range(2 * FT):
                f = k // 2 + FT * (k % 2)
                if k >= 2:
                    pool.wait_ge(up_cv, k - 1)
                else:
                    pool.wait_ge(sa_fin, 2)
                nc.gpsimd.tensor_copy(ext[:, k % 2, :, 0:2], st_t[:, f, :].rearrange("p (b j) -> p b j", b=DB))
                pool.wait_ge(up_u, k + 1)
                u3 = u_b[:, k % 2, 2 + SEQ:2 + NT].rearrange("p (b s) -> p b s", b=DB)
                nc.gpsimd.tensor_copy(ext[:, k % 2, :, 2:2 + DS], u3)
                nc.gpsimd.tensor_copy(u_last[:, f, 2:18].rearrange("p (b j) -> p b j", b=DB), u3[:, :, DS - 2:DS])
                nc.gpsimd.tensor_copy(u_last[:, f, 0:2], u_b[:, k % 2, SEQ:SEQ + 2]).then_inc(up_x, 1)

        @block.scalar
        def _(act):
            act.wait_ge(early, 16 * 15)
            nc.scalar.activation(c_e, c_r, ACT.Exp, scale=-1.0).then_inc(act_setup, 1)
            act.wait_ge(dve_seq, 2)
            nc.scalar.activation(lam_s[:, 2:4], lam_s[:, 0:2], ACT.Exp).then_inc(act_setup, 1)
            act.wait_ge(ada_ok, 4)
            for f in range(1, KT_D, 2):
                act.wait_ge(xt_mm, f + 2)
                nc.scalar.activation(ht[:, f, 0:SEQ], bk(f % 4), ACT.Identity, bias=mod_t[:, f, 0:1],
                                     scale=mod_t[:, 8 + f, 0:1]).then_inc(xt_a, 1)
            jobs = []
            for n, (s, t) in enumerate(units):
                if n in v_units:
                    jobs.append((n, "v", n))
                if n in tr_units and s in (0, 3) and t < TP:
                    jobs.append((n + 2.5, "q", n))
            act.wait_ge(qzero, 1)
            for _, what, n in sorted(jobs):
                s, t = units[n]
                rows = P if t < TP else NS
                if what == "v":
                    act.wait_ge(pj_mm, n + 1)
                    dst = vp[:, t, s // 3, :] if t < TP else v_s[:, s // 3, :]
                    nc.scalar.activation(dst, bk(n % 4)[0:rows, :], ACT.Copy).then_inc(pj_a, 1)
                else:
                    k = tr_units.index(n)
                    act.wait_ge(qk_t, k + 1)
                    src = bk(4 + k % 2).rearrange("p (f t) -> p f t", f=4)
                    m0 = 8 * (s // 3)
                    for h in range(2):
                        last = nc.scalar.activation(qtp[64 * h:64 * h + 64, m0 + h:m0 + 8:2, P * t:P * t + P],
                                                    src[64 * h:64 * h + 64], ACT.Copy)
                    last.then_inc(qk_a, 1)
            for u, (m, n, qb) in enumerate(pa):
                act.wait_ge(pa_min, u + 1)
                if u >= 2:
                    act.wait_ge(pa_t, u - 1)
                w = P * (qb + 1)
                nc.scalar.activation(p_b[:, u % 2, 0:w], s_m[:, u % 2, 0:w], ACT.Exp, bias=mn[:, u:u + 1], scale=-1.0,
                                     accum_out=rs[:, u:u + 1]).then_inc(pa_exp, 1)
            act.wait_ge(rms_sq, 1)
            nc.scalar.activation(rms[:, 1, :], rms[:, 0, :], ACT.Sqrt).then_inc(rms_rt, 1)
            for w, (m, b) in enumerate(sa):
                n = 32 * sum(groups[m]) + 32
                act.wait_ge(sa_min, w + 1)
                for h in range(2):
                    if w >= 1:
                        act.wait_ge(sa_t, 2 * (w - 1) + h + 1)
                    src = sm_s[:, h, 0:n] if m == 0 else wide[h][:, 0:n]
                    nc.scalar.activation(p_s[:, h, 0:n], src, ACT.Exp, bias=blk_o[:, h:h + 1], scale=-1.0,
                                         accum_out=rs_s[:, h, w:w + 1]).then_inc(sa_exp, 1)
                act.wait_ge(sa_pv, w + 1)
                nc.scalar.activation(o_s[:, w, :], bk(6)[:, 0:P], ACT.Copy).then_inc(sa_o, 1)
            act.wait_ge(sa_q, 1)
            nc.scalar.activation(ob_q, ob_q, ACT.Sqrt).then_inc(sa_r, 1)
            act.wait_ge(mt_d, 8)
            for j in range(8):
                act.wait_ge(gb_mm, j + 1)
                which, kind, half = j // 4, (j // 2) % 2, j % 2
                g = gate if which == 0 else gate2
                rows = P if kind == 0 else NS
                nc.scalar.activation(g[0:rows, kind, CH * half:CH * half + CH], bk(4 + j % 2)[0:rows, :], ACT.Copy)\
                    .then_inc(gb_a, 1)
            for t in range(TP + 1):
                act.wait_ge(n_var, t + 1)
                nc.scalar.activation(mv[:, 2:3], mv[:, 1:2], ACT.Sqrt).then_inc(n_rt, 1)
            for f in range(1, KT_D, 2):
                act.wait_ge(h2_mm, f + 2)
                nc.scalar.activation(ht[:, f, 0:SEQ], bk(f % 4), ACT.Identity, bias=mod_t[:, 24 + f, 0:1],
                                     scale=mod_t[:, 32 + f, 0:1]).then_inc(h2_a, 1)
            act.wait_ge(halo, 1)
            for k in range(2 * FT):
                f = k // 2 + FT * (k % 2)
                act.wait_ge(up_mm, k + 1)
                if k >= 2:
                    act.wait_ge(up_x, k - 1)
                    act.wait_ge(up_cv, k - 1)
                pair = up_bank(k)
                nc.scalar.activation(u_b[:, k % 2, 2:2 + NT].rearrange("p (h t) -> p h t", h=2), pair, ACT.Identity,
                                     bias=vec_t[:, 0, 48 + f:49 + f]).then_inc(up_u, 1)
                act.wait_ge(up_u, k + 1)
                if k >= 2:
                    if k % 2 == 0:
                        act.wait_ge(up_ge, k // 2)
                    else:
                        act.wait_ge(up_gt, k // 2)
                nc.scalar.activation(cv[:, k % 2, :], u_b[:, k % 2, 2:2 + NT], ACT.Identity,
                                     bias=vec_t[:, 2, 44 + f:45 + f], scale=vec_t[:, 2, f:f + 1]).then_inc(up_c0, 1)
                if k % 2 == 1:
                    act.wait_ge(up_cv, k)
                    if k >= 5:
                        act.wait_ge(up_gt, k // 2 - 1)
                    nc.scalar.activation(ga[:, (k // 2) % 2, :], cv[:, 0, :], ACT.Gelu).then_inc(up_ge, 1)
            for i in range(11):
                act.wait_ge(us_mm, i + 1)
                if i == 9:
                    act.wait_ge(up_gt, FT)
                nc.scalar.activation(conv_out(i), bk(6 + i % 2)[0:18, :], ACT.Copy).then_inc(us_a, 1)
            for t in range(TP + 1):
                act.wait_ge(n_var, TP + 2 + t)
                nc.scalar.activation(mv[:, 2:3], mv[:, 1:2], ACT.Sqrt).then_inc(n_rt, 1)


        @block.vector
        def _(dve):
            steps = [0]

            def then(ins):
                steps[0] += 1
                ins.then_inc(dve_seq, 1)
                dve.wait_ge(dve_seq, steps[0])

            dve.wait_ge(early, 16 * 15)
            for i in range(2):
                then(nc.vector.tensor_tensor_reduce(out=lam4[:, 2 * i, :], in0=lam4[:, 2 * i, :], in1=lam4[:, 2 * i + 1, :],
                                                    scale=1.0, scalar=0.0, op0=ALU.mult, op1=ALU.add,
                                                    accum_out=lam_s[:, i:i + 1]))
            nc.vector.memset(bk(6), 0.0).then_inc(bank6_zero, 1)
            dve.wait_ge(vecs_t, 1)
            nc.vector.tensor_copy(vec_t[:, 0, 0:93], bk(0)[:, 0:93])
            then(nc.vector.tensor_copy(vec_t[:, 1:3, 0:88], bk(0)[:, P:3 * P].rearrange("p (r d) -> p r d", r=2)[:, :, 0:88]))
            nc.vector.tensor_copy(bada[:, :], vec_t[:, 0, 0:48])
            then(nc.vector.tensor_scalar(g8[:, :], vec_t[:, 0, 92:93], 1.0 - LAM_INIT, None, ALU.mult))
            for at in (8, 32):
                then(nc.vector.tensor_scalar(bada[:, at:at + 8], bada[:, at:at + 8], 1.0, None, ALU.add))
            nc.vector.memset(lam_s[:, 7:8], 0.0).then_inc(vecs_c, 1)
            dve.wait_ge(act_setup, 1)
            then(nc.vector.tensor_scalar(c_e, c_e, 1.0, None, ALU.add))
            then(nc.vector.reciprocal(c_e, c_e))
            nc.vector.tensor_tensor(c_s, c_r, c_e, ALU.mult).then_inc(c_cp, 1)
            dve.wait_ge(c_tr, 1)
            nc.vector.tensor_copy(c_t[:, :, :], bk(1)[:, 0:128].rearrange("p (k r) -> p k r", k=8)[:, :, 0:C]).then_inc(c_cp, 1)
            dve.wait_ge(act_setup, 2)
            then(nc.vector.tensor_tensor(lam_s[:, 4:5], lam_s[:, 3:4], lam_s[:, 2:3], ALU.subtract))
            then(nc.vector.tensor_scalar(lam_s[:, 5:6], lam_s[:, 4:5], -LAM_INIT, None, ALU.add))

            def ada(ch):
                dve.wait_ge(ada_mm, ch + 1)
                if ch >= 2:
                    dve.wait_ge(ada_tt, ch - 1)
                nc.vector.tensor_copy(mod_s[:, ch % 2, :], bk(6)).then_inc(ada_ms, 1)
                dve.wait_ge(ada_tt, ch + 1)
                nc.vector.tensor_tensor(mod_t[:, 4 * ch:4 * ch + 4, :],
                                        bk(7)[:, 0:64].rearrange("p (c r) -> p c r", c=4)[:, :, 0:C],
                                        bada[:, 4 * ch:4 * ch + 4][:, :, None].to_broadcast([P, 4, C]), ALU.add)\
                    .then_inc(ada_ok, 1)

            def modulate(mm, done, first, shift, scale):
                dve.wait_ge(mm, 1)
                src = bk(4).rearrange("p (f b s) -> p f b s", f=KT_D, b=DB)
                dst = ht[:, :, SEQ:NT].rearrange("p f (b s) -> p f b s", b=DB)
                col = lambda at: mod_t[:, at:at + 8, 1:C][:, :, :, None].to_broadcast([P, KT_D, DB, DS])
                then(nc.vector.tensor_tensor(dst, src, col(scale), ALU.mult))
                nc.vector.tensor_tensor(dst, dst, col(shift), ALU.add).then_inc(done, 1)
                for f in range(0, KT_D, 2):
                    dve.wait_ge(mm, f + 2)
                    nc.vector.tensor_scalar(ht[:, f, 0:SEQ], bk(f % 4), mod_t[:, scale + f, 0:1],
                                            mod_t[:, shift + f, 0:1], ALU.mult, ALU.add).then_inc(done, 1)

            for ch in range(4):
                ada(ch)
            dve.wait_ge(ada_ok, 4)
            modulate(xt_mm, xt_d, True, 0, 8)

            jobs = [(n, "rope", n) for n in rope_units]
            jobs += [(n + 2.5, "t", n) for n in tr_units if not (units[n][0] in (0, 3) and units[n][1] < TP)]
            dve.wait_ge(tables, 16 * 9)
            for _, what, n in sorted(jobs):
                s, t = units[n]
                rows = P if t < TP else NS
                if what == "rope":
                    r = rope_units.index(n)
                    dve.wait_ge(pj_mm, n + 1)
                    if r >= 2:
                        dve.wait_ge(rope_ok, r - 1)
                    src = bk(n % 4)[0:rows].rearrange("p (h d) -> p h d", h=MAPS)
                    w = 0 if s in (0, 3) else 1
                    tb = tmp_b[0:rows, r % 2, :].rearrange("p (h d) -> p h d", h=MAPS)
                    ta = tmp_a[0:rows, r % 2, :].rearrange("p (h d) -> p h d", h=MAPS)
                    tab = lambda x, k: rope[0:rows, t, w, x:x + k][:, None, :].to_broadcast([rows, MAPS, k])
                    nc.vector.tensor_tensor(ta, src, tab(0, 64), ALU.mult)
                    nc.vector.tensor_tensor(tb[:, :, 0:32], src[:, :, 32:64], tab(64, 32), ALU.mult)
                    nc.vector.tensor_tensor(tb[:, :, 32:64], src[:, :, 0:32], tab(96, 32), ALU.mult).then_inc(pj_d, 1)
                else:
                    k = tr_units.index(n)
                    dve.wait_ge(qk_t, k + 1)
                    src = bk(4 + k % 2).rearrange("p (f t) -> p f t", f=4)
                    if t < TP:
                        nc.vector.tensor_copy(kt[:, 4 * (s // 3):4 * (s // 3) + 4, P * t:P * t + P], src).then_inc(qk_d, 1)
                    else:
                        for i in range(4):
                            for g in range(4):
                                last = nc.vector.tensor_copy(
                                    qrep[32 * i:32 * i + 32, s // 3, g:16:4, :],
                                    bk(4 + k % 2)[32 * g:32 * g + 32, 0:4 * NS].rearrange("p (f t) -> p f t", f=4))
                        last.then_inc(qk_d, 1)

            for st in range(4):
                dve.wait_ge(stg[st], 16 * n_stored[st])
            for s in range(NU + 3):
                if s < NU:
                    m, n, qb = pa[s]
                    w = P * (qb + 1)
                    dve.wait_ge(pa_s, s + 1)
                    if s >= 2:
                        dve.wait_ge(pa_exp, s - 1)
                    else:
                        dve.wait_ge(rope_ok, len(rope_units))
                    nc.vector.tensor_tensor_reduce(out=s_m[:, s % 2, 0:w], in0=bk(s % 2)[:, 0:w],
                                                   in1=maskt[:, m, SEQ - w:SEQ], scale=1.0, scalar=NEG, op0=ALU.add,
                                                   op1=ALU.min, accum_out=mn[:, s:s + 1]).then_inc(pa_min, 1)
                if 0 <= (x := s - 2) < NU:
                    w = P * (pa[x][2] + 1)
                    dve.wait_ge(pa_t, x + 1)
                    if x >= 2:
                        dve.wait_ge(pa_pv, x - 1)
                    nc.vector.tensor_copy(pt_b[:, x % 2, 0:w], bk(2 + x % 2)[:, 0:w]).then_inc(pa_pt, 1)
                if 0 <= (x := s - 3) < NU:
                    m, n, qb = pa[x]
                    dve.wait_ge(pa_exp, x + 1)
                    then(nc.vector.reciprocal(rcp[:, x:x + 1], rs[:, x:x + 1]))
                    dve.wait_ge(pa_pv, x + 1)
                    src = bk(4 + x % 2)
                    if m == 0:
                        nc.vector.tensor_scalar(mixv[:, qb, 64 * n:64 * n + 64], src[:, 64 * (n % 2):64 * (n % 2) + 64],
                                                rcp[:, x:x + 1], None, ALU.mult).then_inc(pa_o, 1)
                    elif n % 2 == 0:
                        nc.vector.tensor_scalar(o_1, src[:, 0:P], rcp[:, x:x + 1], None, ALU.mult).then_inc(pa_o, 1)
                        dve.wait_ge(pa_o, x + 1)
                    else:
                        then(nc.vector.tensor_scalar(rcp[:, x:x + 1], rcp[:, x:x + 1], lam_s[:, 5:6], None, ALU.mult))
                        nc.vector.scalar_tensor_tensor(out=mixv[:, qb, WID + 64 * (n - 1):WID + 64 * (n + 1)],
                                                       in0=src[:, 0:P], scalar=rcp[:, x:x + 1], in1=o_1,
                                                       op0=ALU.mult, op1=ALU.add).then_inc(pa_o, 1)
                if s < NU and s % 8 == 7:
                    ada(4 + s // 8)
            dve.wait_ge(pa_o, NU)
            sq = s_m[:, 0, :]
            for t in range(TP):
                mb = mixv[:, t, WID:D]
                then(nc.vector.tensor_tensor(sq, mb, mb, ALU.mult))
                then(nc.vector.tensor_reduce(rms[:, 2, 4 * t:4 * t + 4], sq.rearrange("p (h d) -> p h d", h=4), AX_X, ALU.add))
            nc.vector.tensor_scalar(rms[:, 0, :], rms[:, 2, :], 1.0 / P, EPS, ALU.mult, ALU.add).then_inc(rms_sq, 1)
            dve.wait_ge(rms_rt, 1)
            then(nc.vector.reciprocal(rms[:, 2, :], rms[:, 1, :]))
            for t in range(TP):
                mb = mixv[:, t, WID:D].rearrange("p (h d) -> p h d", h=4)
                last = nc.vector.tensor_tensor(mb, mb, rms[:, 2, 4 * t:4 * t + 4][:, :, None].to_broadcast([P, 4, P]), ALU.mult)
            last.then_inc(rms_ok, 1)

            dve.wait_ge(new_zero, 1)
            for w, (m, b) in enumerate(sa):
                n = 32 * sum(groups[m])
                for g, nt in enumerate(groups[m]):
                    G = NG[w] + g
                    dve.wait_ge(kg_in[G % NK], k_count(m, w, g))
                    if G >= NK:
                        dve.wait_ge(sa_g, G - NK + 1)
                    for t in range(nt):
                        last = nc.vector.transpose(ktg[:, G % NK, :, 32 * t:32 * t + 32],
                                                   kraw[:, G % NK, t, :].rearrange("p (g d) -> p g d", d=32))
                    last.then_inc(kg_t, 1)
                dve.wait_ge(new_in[w % 2], 32 * (w // 2 + 1))
                if w >= 2:
                    dve.wait_ge(sa_s, w - 1)
                nc.vector.transpose(ktn[0:32, w % 2, :, :], kn[0:32, w % 2, :].rearrange("p (g d) -> p g d", d=32))\
                    .then_inc(kn_t, 1)
                dve.wait_ge(sa_s, w + 1)
                if w >= 1:
                    dve.wait_ge(sa_exp, 2 * w)
                for h in range(2):
                    if m == 0:
                        then(nc.vector.tensor_tensor_reduce(out=sm_s[:, h, 0:n + 32], in0=wide[h][:, 0:n + 32],
                                                            in1=smask[:, 0:n + 32], scale=1.0, scalar=NEG,
                                                            op0=ALU.add, op1=ALU.min, accum_out=blk[:, h:h + 1]))
                    else:
                        then(nc.vector.tensor_tensor(wide[h][:, n:n + 32], wide[h][:, n:n + 32], smask[:, 352:384], ALU.add))
                        then(nc.vector.tensor_reduce(blk[:, h:h + 1], wide[h][:, 0:n + 32], AX_X, ALU.min))
                then(nc.vector.transpose(blk_t, blk))
                then(nc.vector.tensor_reduce(small[:, 176:184], blk_t.rearrange("p (i q) -> p q i", i=4), AX_X, ALU.min))
                then(nc.vector.tensor_copy(blk_r.rearrange("p (i q) -> p i q", i=4),
                                           small[:, 176:184][:, None, :].to_broadcast([P, 4, DS])))
                nc.vector.transpose(blk_o, blk_r).then_inc(sa_min, 1)
                full = P * (n // P)
                for h in range(2):
                    dve.wait_ge(sa_t, 2 * w + h + 1)
                    if w >= 1:
                        dve.wait_ge(sa_pv, w)
                    if m == 0:
                        nc.vector.tensor_copy(pt_s[0:64, h, full:full + P], bk(4 + h)[0:64, full:full + P])
                    nc.vector.tensor_copy(pt_s[:, h, 0:full], bk(4 + h)[:, 0:full]).then_inc(sa_pt, 1)
                nc.vector.tensor_copy(ptn[0:32, :, :], bk(7)[0:32, 0:2 * P].rearrange("p (h c) -> p h c", h=2)).then_inc(sa_pt, 1)
            dve.wait_ge(sa_l, 1)
            then(nc.vector.reciprocal(l_s, bk(0)[:, 0:16]))
            then(nc.vector.tensor_scalar(lam_s[:, 6:7], diff_c[:, 1:2], lam_s[:, 5:6], diff_c[:, 0:1], ALU.mult, ALU.add))
            l_b = l_s.rearrange("p (b m) -> p b m", m=2)
            then(nc.vector.tensor_scalar(l_b[:, :, 1], l_b[:, :, 1], lam_s[:, 6:7], None, ALU.mult))
            dve.wait_ge(sa_o, 16)
            then(nc.vector.tensor_tensor(o_s, o_s, l_s[:, :, None].to_broadcast([P, 16, P]), ALU.mult))
            o_a = o_s.rearrange("p (b m) d -> p b m d", m=2)[:, :, 0, :]
            nc.vector.tensor_tensor(o_a, o_a, colmask[:, None, :].to_broadcast([P, DB, P]), ALU.mult).then_inc(sa_n, 1)
            dve.wait_ge(sa_x, 1)
            tok = lambda f: ht[:, f:f + 4, SEQ:NT].rearrange("p j (b q) -> p j b q", b=DB)
            bjq = lambda ap: ap.rearrange("p (b j q) -> p j b q", b=DB, j=4)
            jbq = lambda ap: ap.rearrange("p (j b q) -> p j b q", b=DB, j=4)
            nc.vector.tensor_copy(tok(0), bjq(bk(1)[:, 0:256])).then_inc(sa_fin, 1)
            then(nc.vector.tensor_copy(jbq(ob_t), bjq(bk(2)[:, 0:256])))
            nc.vector.tensor_tensor(ob_q, ob_t, ob_t, ALU.mult).then_inc(sa_n, 1)
            dve.wait_ge(sa_sq, 1)
            nc.vector.tensor_scalar(ob_q, bk(3)[:, 0:256], 1.0 / P, EPS, ALU.mult, ALU.add).then_inc(sa_q, 1)
            dve.wait_ge(sa_r, 1)
            then(nc.vector.reciprocal(ob_r, ob_q))
            then(nc.vector.tensor_tensor(ob_t, ob_t, ob_r, ALU.mult))
            nc.vector.tensor_scalar(tok(4), jbq(ob_t), g8[:, 0:1], None, ALU.mult).then_inc(sa_fin, 1)

            dve.wait_ge(ada_ok, 12)
            for g, at in enumerate((16, 40)):
                last = nc.vector.tensor_copy(gexp[:, 8 * g:8 * g + 8], mod_t[:, at:at + 8, 1:C][:, :, :, None]
                                             .to_broadcast([P, 8, DB, DS]))
            last.then_inc(mt_d, 1)
            for f in range(KT_D):
                dve.wait_ge(mt_mm, f + 1)
                if f < 4:
                    nc.vector.tensor_copy(ht[:, f, 0:SEQ], bk(f % 4)).then_inc(mt_d, 1)
                else:
                    nc.vector.tensor_scalar(ht[:, f, 0:SEQ], bk(f % 4), g8[:, 0:1], None, ALU.mult).then_inc(mt_d, 1)

            def norm(t, rows, g_row, b_row, k):
                x = x_sb[0:rows, t, :]
                for h in range(2):
                    then(nc.vector.bn_stats(stat[0:rows, h, :], x[:, 512 * h:512 * h + 512]))
                then(nc.vector.bn_aggr(mv[0:rows, 0:2], stat[0:rows, :, :].rearrange("p h s -> p (h s)")))
                nc.vector.tensor_scalar(mv[0:rows, 1:2], mv[0:rows, 1:2], EPS, None, ALU.add).then_inc(n_var, 1)
                dve.wait_ge(n_rt, k + 1)
                then(nc.vector.reciprocal(mv[0:rows, 3:4], mv[0:rows, 2:3]))
                then(nc.vector.tensor_scalar(x, x, mv[0:rows, 0:1], mv[0:rows, 3:4], ALU.subtract, ALU.mult))
                then(nc.vector.tensor_tensor(x, x, g_row[0:rows], ALU.mult))
                return nc.vector.tensor_tensor(x, x, b_row[0:rows], ALU.add)

            dve.wait_ge(gb_a, 4)
            dve.wait_ge(gb_mm, 8)
            dve.wait_ge(ln_in, 32)
            for t in range(TP + 1):
                rows, kind = (P, 0) if t < TP else (NS, 1)
                for half in range(2):
                    j = 2 * t + half
                    dve.wait_ge(wo_mm, j + 1)
                    nc.vector.tensor_tensor(y_sb[0:rows, t % 2, 512 * half:512 * half + 512], bk(j % 4)[0:rows],
                                            gate[0:rows, kind, 512 * half:512 * half + 512], ALU.mult).then_inc(wo_d, 1)
                dve.wait_ge(wo_d, 2 * t + 2)
                x = x_sb[0:rows, t, :]
                then(nc.vector.scalar_tensor_tensor(out=x, in0=x, scalar=ALPHA, in1=y_sb[0:rows, t % 2, :],
                                                    op0=ALU.mult, op1=ALU.add))
                norm(t, rows, ln1[:, 0, :], ln1[:, 1, :], t).then_inc(x1_ok, 1)
            for i in range(11):
                dve.wait_ge(st_mm, i + 1)
                nc.vector.tensor_copy(st_t[:, 4 * i:4 * i + 4, :],
                                      bk(6 + i % 2)[:, 0:64].rearrange("p (f r) -> p f r", f=4)).then_inc(st_ok, 1)
            modulate(h2_mm, h2_d, False, 24, 32)

            for k in range(2 * FT):
                f = k // 2 + FT * (k % 2)
                tap = lambda j: vec_t[:, 1, 44 * j + f:44 * j + f + 1]
                c_p, c_sm = cv[:, k % 2, 0:SEQ], cv[:, k % 2, SEQ:NT].rearrange("p (b s) -> p b s", b=DB)
                dve.wait_ge(up_c0, k + 1)
                then(nc.vector.scalar_tensor_tensor(out=c_p, in0=u_b[:, k % 2, 1:1 + SEQ], scalar=tap(1), in1=c_p,
                                                    op0=ALU.mult, op1=ALU.add))
                nc.vector.scalar_tensor_tensor(out=c_p, in0=u_b[:, k % 2, 0:SEQ], scalar=tap(0), in1=c_p,
                                               op0=ALU.mult, op1=ALU.add)
                dve.wait_ge(up_x, k + 1)
                then(nc.vector.scalar_tensor_tensor(out=c_sm, in0=ext[:, k % 2, :, 1:1 + DS], scalar=tap(1), in1=c_sm,
                                                    op0=ALU.mult, op1=ALU.add))
                nc.vector.scalar_tensor_tensor(out=c_sm, in0=ext[:, k % 2, :, 0:DS], scalar=tap(0), in1=c_sm,
                                               op0=ALU.mult, op1=ALU.add).then_inc(up_cv, 1)
                if k % 2 == 1:
                    dve.wait_ge(up_ge, k // 2 + 1)
                    dve.wait_ge(up_cv, k + 1)
                    nc.vector.tensor_tensor(gt[:, k // 2, :], ga[:, (k // 2) % 2, :], cv[:, 1, :], ALU.mult).then_inc(up_gt, 1)

            dve.wait_ge(ln2_in, 48)
            dve.wait_ge(gb_a, 8)
            dve.wait_ge(up_gt, FT)
            for j in range(2 * (TP + 1)):
                half, t = divmod(j, TP + 1)
                rows, kind = (P, 0) if t < TP else (NS, 1)
                cols = slice(512 * half, 512 * half + 512)
                dve.wait_ge(dn_mm, j + 1)
                y = y3[0:rows, j % 2, :]
                nc.vector.tensor_tensor(y, bk(j % 6)[0:rows], ln2[0:rows, 0, cols], ALU.add).then_inc(dn_d, 1)
                dve.wait_ge(dn_d, j + 1)
                then(nc.vector.tensor_tensor(y, y, gate2[0:rows, kind, cols], ALU.mult))
                x = x_sb[0:rows, t, cols]
                then(nc.vector.scalar_tensor_tensor(out=x, in0=x, scalar=ALPHA, in1=y, op0=ALU.mult, op1=ALU.add))
                if half:
                    norm(t, rows, ln2[:, 1, :], ln2[:, 2, :], TP + 1 + t).then_inc(y_out, 1)

        @block.tensor
        def _(pe):
            def landed(n):
                pe.wait_ge(w_in_slot[SLOT_OF[n]], slot_count(n))

            pe.wait_ge(early, 16 * 15)
            for r, k in enumerate((93, 88, 88)):
                last = nc.tensor.transpose(bk(0)[:, P * r:P * r + k], vec_r[0:k, r, :], ident[0:k, 0:k])
            last.then_inc(vecs_t, 1)
            pe.wait_ge(c_cp, 1)
            for k in range(KT_D):
                last = nc.tensor.transpose(bk(1)[:, 16 * k:16 * k + C], c_s[:, P * k:P * k + P], ident[0:C, 0:C])
            last.then_inc(c_tr, 1)

            def ada(ch):
                n = CHUNK_AT[("ada", ch)]
                landed(n)
                if ch:
                    pe.wait_ge(ada_ms, ch)
                for k in range(KT_D):
                    j = k % 4
                    last = nc.tensor.matmul(bk(6)[32 * j:32 * j + C, :], c_t[:, k, :], slot(SLOT_OF[n])[:, k, :],
                                            start=(k < 4), stop=(k >= 4))
                last.then_inc(ada_mm, 1)
                pe.wait_ge(ada_mm, ch + 1)
                pe.wait_ge(ada_ms, ch + 1)
                pe.sem_inc(w_used, 1)
                if ch:
                    pe.wait_ge(ada_ok, ch)
                for c in range(4):
                    last = nc.tensor.matmul(bk(7)[:, 16 * c:16 * c + C], mod_s[:, ch % 2, P * c:P * c + P], sum9[:, :],
                                            start=True, stop=True)
                last.then_inc(ada_tt, 1)

            pe.wait_ge(bank6_zero, 1)
            pe.wait_ge(c_cp, 2)
            for ch in range(4):
                ada(ch)

            def turn_x(mm, taken_d, taken_a):
                for f in range(KT_D):
                    last = nc.tensor.transpose(bk(4)[:, NS * f:NS * f + NS], x_sb[0:NS, TP, P * f:P * f + P], ident[0:NS, 0:NS])
                last.then_inc(mm, 1)
                for f in range(KT_D):
                    if f >= 4:
                        if f % 2 == 0:
                            pe.wait_ge(taken_d, (f - 4) // 2 + 2)
                        else:
                            pe.wait_ge(taken_a, (f - 4) // 2 + 1)
                    for t in range(TP):
                        last = nc.tensor.transpose(bk(f % 4)[:, P * t:P * t + P], x_sb[:, t, P * f:P * f + P], ident[:, :])
                    last.then_inc(mm, 1)

            pe.wait_ge(x_in, 32)
            turn_x(xt_mm, xt_d, xt_a)
            pe.wait_ge(xt_d, 5)
            pe.wait_ge(xt_a, 4)

            for n in range(len(units) + 3):
                if n < len(units):
                    s, t = units[n]
                    ch = CHUNK_AT[("in", s)]
                    if t == 0:
                        landed(ch)
                    if n >= 4:
                        if n - 4 in rope_units:
                            pe.wait_ge(pj_d, d_units(n - 4))
                        else:
                            pe.wait_ge(pj_a, a_units(n - 4))
                    rows = P if t < TP else NS
                    for k in range(KT_D):
                        last = nc.tensor.matmul(bk(n % 4)[0:rows, :], ht[:, k, P * t:P * t + rows], slot(SLOT_OF[ch])[:, k, :],
                                                start=(k == 0), stop=(k == KT_D - 1))
                    last.then_inc(pj_mm, 1)
                    if t == TP:
                        pe.wait_ge(pj_mm, n + 1)
                        pe.sem_inc(w_used, 1)
                if (n - 2) in tr_units:
                    s, t = units[n - 2]
                    k = tr_units.index(n - 2)
                    r = rope_units.index(n - 2)
                    pe.wait_ge(rope_ok, r + 1)
                    if k >= 2:
                        s2, t2 = units[tr_units[k - 2]]
                        by_act = [x for x in tr_units[:k - 1] if units[x][0] in (0, 3) and units[x][1] < TP]
                        if s2 in (0, 3) and t2 < TP:
                            pe.wait_ge(qk_a, len(by_act))
                        else:
                            pe.wait_ge(qk_d, k - 1 - len(by_act))
                    rows = P if t < TP else NS
                    for f in range(4):
                        last = nc.tensor.transpose(bk(4 + k % 2)[:, rows * f:rows * f + rows],
                                                   stage[0:rows, r % 4, P * f:P * f + P], ident[0:rows, 0:rows])
                    last.then_inc(qk_t, 1)

            pe.wait_ge(qk_a, 2 * TP)
            pe.wait_ge(qk_d, len(tr_units) - 2 * TP)
            pe.wait_ge(pj_a, len(v_units))
            pe.wait_ge(pj_d, len(rope_units))
            for s in range(NU + 3):
                if s < NU:
                    m, n, qb = pa[s]
                    w = P * (qb + 1)
                    if s >= 2:
                        pe.wait_ge(pa_min, s - 1)
                    nc.tensor.matmul(bk(s % 2)[:, 0:w], qtp[:, 8 * m + n, P * qb:P * qb + P], kt[:, 4 * m + n // 2, 0:w],
                                     start=True, stop=True).then_inc(pa_s, 1)
                if 0 <= (x := s - 2) < NU:
                    pe.wait_ge(pa_exp, x + 1)
                    if x >= 2:
                        pe.wait_ge(pa_pt, x - 1)
                    for kb in range(pa[x][2] + 1):
                        last = nc.tensor.transpose(bk(2 + x % 2)[:, P * kb:P * kb + P], p_b[:, x % 2, P * kb:P * kb + P], ident[:, :])
                    last.then_inc(pa_t, 1)
                if 0 <= (x := s - 3) < NU:
                    m, n, qb = pa[x]
                    pe.wait_ge(pa_pt, x + 1)
                    if x >= 2:
                        pe.wait_ge(pa_o, x - 1)
                    for kb in range(qb + 1):
                        last = nc.tensor.matmul(bk(4 + x % 2)[:, 0:P], pt_b[:, x % 2, P * kb:P * kb + P],
                                                vp[:, kb, m, P * (n // 2):P * (n // 2) + P], start=(kb == 0), stop=(kb == qb))
                    last.then_inc(pa_pv, 1)
                if s < NU and s % 8 == 7:
                    ada(4 + s // 8)

            pe.wait_ge(pa_min, NU)
            pe.wait_ge(pa_o, NU)
            pe.wait_ge(ada_ok, 12)
            for w, (m, b) in enumerate(sa):
                n = 32 * sum(groups[m])
                pe.wait_ge(q_bd, w + 1)
                if w >= 1:
                    pe.wait_ge(sa_min, w)
                    pe.wait_ge(sa_exp, 2 * w)

                def score(h, keys, at, nk):
                    for d in range(2):
                        for nn in range(4):
                            g = 2 * (4 * h + nn) + d
                            last = nc.tensor.matmul(wide[h][32 * nn:32 * nn + 32, at:at + nk],
                                                    qbd[:, w % 2, g].rearrange("p i q -> p (i q)"), keys[:, g, 0:nk],
                                                    start=(d == 0), stop=(d == 1), skip_group_check=True)
                    return last

                for g, nt in enumerate(groups[m]):
                    G = NG[w] + g
                    pe.wait_ge(kg_t, G + 1)
                    score(0, ktg[:, G % NK], P * g, 32 * nt)
                    score(1, ktg[:, G % NK], P * g, 32 * nt).then_inc(sa_g, 1)
                pe.wait_ge(kn_t, w + 1)
                score(0, ktn[:, w % 2], n, 32)
                score(1, ktn[:, w % 2], n, 32).then_inc(sa_s, 1)
                for h in range(2):
                    pe.wait_ge(sa_exp, 2 * w + h + 1)
                    if w >= 1:
                        pe.wait_ge(sa_pt, 3 * w)
                    for u in range((n + P - 1) // P):
                        k = min(P, n - P * u)
                        nc.tensor.transpose(bk(4 + h)[0:k, P * u:P * u + P], p_s[:, h, P * u:P * u + k], perm[:, :])
                    nc.tensor.transpose(bk(7)[0:32, P * h:P * h + P], p_s[:, h, n:n + 32], perm[:, :]).then_inc(sa_t, 1)
                pe.wait_ge(sa_pt, 3 * w + 3)
                if w >= 1:
                    pe.wait_ge(sa_o, w)
                for g, nt in enumerate(groups[m]):
                    G = NG[w] + g
                    pe.wait_ge(vg_in[G % NV], v_count(m, w, g))
                    k = 32 * nt
                    for i in range(4):
                        for j in range(4):
                            at = P * g + 32 * i + 16 * (j % 2)
                            last = nc.tensor.matmul(bk(6)[32 * j:32 * j + 16, 0:P], pt_s[0:k, j // 2, at:at + 16],
                                                    vg[0:k, G % NV, i, P * j:P * j + P], start=(g == 0 and i == 0),
                                                    stop=False, skip_group_check=True)
                    last.then_inc(sa_vg, 1)
                pe.wait_ge(new_in[w % 2], 32 * (w // 2 + 1))
                for j in range(4):
                    at = 16 * (j % 2)
                    last = nc.tensor.matmul(bk(6)[32 * j:32 * j + 16, 0:P], ptn[0:DS, j // 2, at:at + 16],
                                            vn[0:DS, w % 2, P * j:P * j + P], start=False, stop=True, skip_group_check=True)
                last.then_inc(sa_pv, 1)
            pe.wait_ge(sa_exp, 32)
            for h in range(2):
                last = nc.tensor.matmul(bk(0)[:, 0:16], sums[:, h, :], rs_s[:, h, :], start=(h == 0), stop=(h == 1))
            last.then_inc(sa_l, 1)
            pe.wait_ge(sa_n, 1)
            for w, (m, b) in enumerate(sa):
                last = nc.tensor.matmul(bk(1 + m)[:, 32 * b:32 * b + 32], o_s[:, w, :], pick[:, :], start=True, stop=True)
            last.then_inc(sa_x, 1)
            pe.wait_ge(sa_n, 2)
            nc.tensor.matmul(bk(3)[:, 0:256], ones[:, :], ob_q, start=True, stop=True).then_inc(sa_sq, 1)

            pe.wait_ge(sa_fin, 2)
            pe.wait_ge(rms_ok, 1)
            for f in range(KT_D):
                if f >= 4:
                    pe.wait_ge(mt_d, f - 2)
                for t in range(TP):
                    last = nc.tensor.transpose(bk(f % 4)[:, P * t:P * t + P], mixv[:, t, P * f:P * f + P], ident[:, :])
                last.then_inc(mt_mm, 1)
            pe.wait_ge(mt_d, 9)
            for j in range(8):
                which, kind, half = j // 4, (j // 2) % 2, j % 2
                rows = P if kind == 0 else NS
                if j >= 2:
                    pe.wait_ge(gb_a, j - 1)
                for c in range(4):
                    f = 4 * half + c
                    col = mod_t[:, (16, 40)[which] + f, 0:1].to_broadcast([P, P]) if kind == 0 else \
                        gexp[:, 8 * which + f].rearrange("p b s -> p (b s)")
                    last = nc.tensor.matmul(bk(4 + j % 2)[0:rows, P * c:P * c + P], col, ident[:, :], start=True, stop=True)
                last.then_inc(gb_mm, 1)
            for j in range(2 * (TP + 1)):
                t, half = divmod(j, 2)
                rows = P if t < TP else NS
                n = CHUNK_AT[("o", half)]
                if t == 0:
                    landed(n)
                if j >= 4:
                    pe.wait_ge(wo_d, j - 3)
                for k in range(KT_D):
                    last = nc.tensor.matmul(bk(j % 4)[0:rows, :], ht[:, k, P * t:P * t + rows], slot(SLOT_OF[n])[:, k, :],
                                            start=(k == 0), stop=(k == KT_D - 1))
                last.then_inc(wo_mm, 1)
            pe.wait_ge(wo_mm, 2 * TP + 2)
            pe.sem_inc(w_used, 2)
            pe.wait_ge(st_in, 16)
            pe.wait_ge(wo_d, 2 * TP + 2)
            for i in range(11):
                if i >= 2:
                    pe.wait_ge(st_ok, i - 1)
                for c in range(4):
                    last = nc.tensor.transpose(bk(6 + i % 2)[:, 16 * c:16 * c + 16], st_r[:, 512 * i + P * c:512 * i + P * c + P],
                                               ident[0:16, 0:16])
                last.then_inc(st_mm, 1)
            pe.wait_ge(x1_ok, TP + 1)
            turn_x(h2_mm, h2_d, h2_a)
            pe.wait_ge(h2_d, 5)
            pe.wait_ge(h2_a, 4)
            for k in range(2 * FT):
                f, g = divmod(k, 2)
                n = CHUNK_AT[("up", f // 2)]
                if k % 4 == 0:
                    landed(n)
                if k >= 3:
                    pe.wait_ge(up_u, k - 2)
                at = 256 * g + P * (f % 2)
                for kk in range(KT_D):
                    for h in range(2):
                        last = nc.tensor.matmul(up_bank(k)[:, h, :], slot(SLOT_OF[n])[:, kk, at:at + P],
                                                ht[:, kk, HALF_NT * h:HALF_NT * h + HALF_NT],
                                                start=(kk == 0), stop=(kk == KT_D - 1))
                last.then_inc(up_mm, 1)
                if k % 4 == 3:
                    pe.wait_ge(up_mm, k + 1)
                    pe.sem_inc(w_used, 1)
            for i in range(11):
                if i == 0:
                    pe.wait_ge(up_x, 2 * FT)
                if i >= 2:
                    pe.wait_ge(us_a, i - 1)
                for c in range(4):
                    last = nc.tensor.transpose(bk(6 + i % 2)[0:18, P * c:P * c + P], u_last[:, 4 * i + c, :], ident[:, :])
                last.then_inc(us_mm, 1)
            pe.wait_ge(up_gt, FT)
            pe.wait_ge(up_u, 2 * FT)
            for j in range(2 * (TP + 1)):
                half, t = divmod(j, TP + 1)
                rows = P if t < TP else NS
                if j >= 6:
                    pe.wait_ge(dn_d, j - 5)
                for f in range(FT):
                    n = CHUNK_AT[("down", 3 * half + f // 8)]
                    if f % 8 == 0 and t == 0:
                        landed(n)
                    last = nc.tensor.matmul(bk(j % 6)[0:rows, :], gt[:, f, P * t:P * t + rows], slot(SLOT_OF[n])[:, f % 8, :],
                                            start=(f == 0), stop=(f == FT - 1))
                    if f % 8 == 7 and t == TP:
                        last.then_inc(w_used, 1)
                last.then_inc(dn_mm, 1)
                if t == TP:
                    pe.wait_ge(dn_mm, j + 1)
                    pe.sem_inc(w_used, 1)


def constants():
    import numpy as np

    f32 = np.float32
    c = {"ident": np.eye(P, dtype=f32), "ones": np.ones((P, P), f32)}
    half = 32
    inv = (f32(1.0) / (f32(10000.0) ** (np.arange(half, dtype=f32) / f32(half)))).astype(f32)
    pos = np.zeros((TP + 1, P), f32)
    pos[:TP] = np.arange(SEQ).reshape(TP, P)
    pos[TP, :NS] = PAST + np.arange(NS) % DS
    ang = (pos[:, :, None] * inv).astype(f32)
    cos, sin = np.cos(ang), np.sin(ang)
    k_tab = np.concatenate([cos, cos, -sin, sin], -1)
    c["rope"] = np.stack([k_tab * f32(-0.125), k_tab], 2).transpose(1, 0, 2, 3).astype(f32).copy()

    def penalty(dist):
        n = sum(((dist >= 0) & (dist <= w) & (dist % d == 0)).astype(int) for w, d in ((128, 1), (512, 4), (2048, 16)))
        return np.where(n > 0, -np.log(np.maximum(n, 1)), BIG).astype(f32)

    dist = np.arange(P)[:, None] + (SEQ - P) - np.arange(SEQ)[None, :]
    c["maskt"] = np.stack([penalty(dist), np.where(dist >= 0, 0, BIG).astype(f32)], 1)
    i = (np.arange(P) // 8) % 4
    q = np.arange(P) % 8
    m = np.arange(32)
    cols = [16 * (32 * i[:, None] + m) + t for t in range(8)] + [16 * (96 + m[None, :]) + 8 + 4 * x + i[:, None] for x in range(2)]
    sm = np.concatenate([penalty(PAST + q[:, None] - k) for k in cols], 1)
    here = (i[:, None] == 0) & (m[None, :] < DS) & (m[None, :] <= q[:, None])
    c["smask"] = np.concatenate([sm, np.where(here, penalty(q[:, None] - m[None, :]), f32(BIG)),
                                 np.where(here, f32(0), f32(BIG))], 1).astype(f32)
    sums = np.zeros((2, P, P), f32)
    for h in range(2):
        for r in range(P):
            for out in range(P):
                j, n2 = out // 32, min((out % 32) // 8, 1)
                sums[h, r, out] = 4 * h + r // 32 == 2 * j + n2 and r % 8 == out % 8
    c["sums"] = sums.transpose(1, 0, 2).copy()
    r = np.arange(P)
    c["pick"] = ((r[:, None] // 32 == np.arange(32)[None, :] // 8) & (r[:, None] % 8 == np.arange(32)[None, :] % 8)
                 & (r[:, None] % 32 < 16)).astype(f32)
    c["colmask"] = ((np.arange(P)[None, :] // 64) == ((r[:, None] % 32) // 8)).astype(f32)
    c["sum9"] = (r[:, None] % 32 == np.arange(C)[None, :]).astype(f32)
    c["diff_c"] = np.stack([(r % 32 // 8 != 1), (r % 32 // 8 == 1)], 1).astype(f32)
    perm = np.zeros((P, P), f32)
    for n in range(4):
        for i_ in range(4):
            for q_ in range(8):
                perm[32 * n + 8 * i_ + q_, 32 * i_ + 8 * n + q_] = 1
    c["perm"] = perm
    return c


_OUTS = [("yp", (1, SEQ, D)), ("ys", (DB, DS, D)),
         ("wkp", (1, 1, SEQ, 8, 64)), ("wvp", (1, 1, SEQ, 8, 64)),
         ("wks", (1, DB, PAST, 8, 64)), ("wvs", (1, DB, PAST, 8, 64)),
         ("kkp", (1, 1, SEQ, 4, 128)), ("kvp", (1, 1, SEQ, 4, 128)),
         ("kks", (1, DB, DS, 4, 128)), ("kvs", (1, DB, DS, 4, 128)),
         ("cp", (1, 1, 2, 2 * DFF)), ("cs", (1, DB, 2, 2 * DFF))]


def kernel(**inputs):
    import numpy as _np
    import concourse.bacc as _bacc
    from concourse.bass_utils import run_bass_kernel_spmd as _run

    nc = _bacc.Bacc("TRN2", target_bir_lowering=False, num_devices=1, dynamic_dma_scratch_size=1024)
    arrays, ins, outs = {}, {}, {}
    for name, value in {**inputs, **constants()}.items():
        value = _np.ascontiguousarray(value)
        arrays[f"in_{name}"] = value
        ins[name] = nc.dram_tensor(f"in_{name}", value.shape, mybir.dt.from_np(value.dtype), kind="ExternalInput").ap()
    for name, shape in _OUTS:
        outs[name] = nc.dram_tensor(f"out_{name}", shape, F32, kind="ExternalOutput").ap()
    build(nc, ins, outs)
    r = _run(nc, [arrays], core_ids=[0])
    return tuple(r.results[0][f"out_{name}"] for name, _ in _OUTS)
```

```python
from contextlib import ExitStack

import concourse.bass as bass
from concourse import mybir

P = 128
F32 = mybir.dt.float32
F32R = mybir.dt.float32r
I32 = mybir.dt.int32
ALU = mybir.AluOpType
ACT = mybir.ActivationFunctionType
AX_X = mybir.AxisListType.X

D = 1024
KT_D = D // P
SEQ = 512
TP = SEQ // P
DB, DS = 8, 8
NS = DB * DS
NT = SEQ + NS
HALF_NT = NT // 2
PAST = 2048
PAGE = 128
N_PAGES = PAST // PAGE
WID = 512
MAPS = 8
DFF = 2816
FT = DFF // P
CH = 512
N_SLOTS = 4
SLOT = KT_D * CH
NEG = 3.0e38
BIG = 1.0e30
EPS = 1e-5
ALPHA = 2.0 ** 0.25
LAM_INIT = 0.2
C = 1 + DB
A_TILES = 10
B_TILES = N_PAGES

CHUNKS = [("ada", i) for i in range(4)] + [("in", i) for i in range(6)] + [("ada", i) for i in range(4, 12)] \
    + [("o", i) for i in range(2)] + [("up", i) for i in range(11)] + [("down", i) for i in range(6)]
SLOT_OF = [0, 1, 2, 3] + [0, 1] * 3 + [0, 1, 2, 0, 1, 2, 0, 1] + [i % 2 for i in range(19)]
CHUNK_AT = {c: i for i, c in enumerate(CHUNKS)}


def loads_of_slot(n):
    return sum(SLOT_OF[i] == SLOT_OF[n] for i in range(n + 1))


def chunk_before(n):
    return max((i for i in range(n) if SLOT_OF[i] == SLOT_OF[n]), default=None)


FIRST_LATE = CHUNK_AT[("o", 0)]
PIECES = [(n, k) for n in range(FIRST_LATE, len(CHUNKS)) for k in range(0, 6 if CHUNKS[n] in (("down", 2), ("down", 5)) else 8, 2)]


def pieces_through(n):
    return sum(c <= n for c, k in PIECES)


def build(nc, a, o, spill):
    ctx = ExitStack()
    with ctx:
        def sb(name, shape, dt=F32):
            return ctx.enter_context(nc.sbuf_tensor(name, shape, dt))

        def sem(name):
            return ctx.enter_context(nc.semaphore(name))

        wide = [ctx.enter_context(nc.psum_tensor(f"wide{i}", [P, 1024], F32)) for i in range(4)]

        def bk(i):
            return wide[i // 2][:, 512 * (i % 2):512 * (i % 2) + 512]

        shared = (("ring", [P, N_SLOTS * SLOT]), ("x_sb", [P, TP + 1, D]), ("ht", [P, KT_D, NT]), ("room", [P, 19712]))
        with ExitStack() as once:
            ring, x_sb, ht, room = (once.enter_context(nc.sbuf_tensor(name, shape, F32)) for name, shape in shared)
        ring_r, x_r, ht_r, room_r = (sb(name + "_r", shape, F32R) for name, shape in shared)
        mix = sb("mix", [P, TP * D])
        ident = sb("ident", [P, P])
        perm = sb("perm", [P, P])
        maskt = sb("maskt", [P, 2, SEQ])
        smask = sb("smask", [P, 384])
        sums = sb("sums", [P, 2, P])
        pick = sb("pick", [P, 32])
        colmask = sb("colmask", [P, P])
        sum9 = sb("sum9", [P, C])
        ones = sb("ones", [P, P])
        diff_c = sb("diff_c", [P, 2])
        vec_t = sb("vec_t", [P, 3, P])
        bada = sb("bada", [P, 48])
        mod_t = sb("mod_t", [P, 48, C])
        c_t = sb("c_t", [P, KT_D, C])
        lam_s = sb("lam_s", [P, 8])
        mn = sb("mn", [P, 64])
        rs = sb("rs", [P, 64])
        rcp = sb("rcp", [P, 64])
        rms = sb("rms", [P, 3, 16])
        pages = sb("pages", [1, DB * N_PAGES], I32)
        stat = sb("stat", [P, 2, 6])
        mv = sb("mv", [P, 4])
        g8 = sb("g8", [P, 1])

        def slot(i, t=ring):
            return t[:, i * SLOT:(i + 1) * SLOT].rearrange("p (k n) -> p k n", k=KT_D)

        def part(t, at, n):
            return t[:, at:at + n]

        def pair_of(n, k, cols=slice(0, CH)):
            high = slot(2 if n < FIRST_LATE else 2 + SLOT_OF[n], ring_r)
            return high[:, k, cols], slot(SLOT_OF[n], ring_r)[:, k, cols]

        vec_r = room[:, 0:3 * P].rearrange("p (r d) -> p r d", r=3)
        c_r = room[0:C, 512:512 + D]
        c_e = room[0:C, 1536:1536 + D]
        c_s = room[0:C, 2560:2560 + D]
        lam4 = part(room, 3584, 256).rearrange("p (n d) -> p n d", n=4)
        mod_s = ht[:, :, :].rearrange("p k t -> p (k t)")[:, 0:2 * CH].rearrange("p (b n) -> p b n", b=2)
        qtp = part(room, 0, 8192).rearrange("p (n t) -> p n t", n=16)
        kt = part(room, 8192, 4096).rearrange("p (f t) -> p f t", f=8)
        vp = part(room, 12288, 4096).rearrange("p (t m d) -> p t m d", t=TP, m=2)
        tmp_a = part(room, 16384, 1024).rearrange("p (b n) -> p b n", b=2)
        tmp_b = part(room, 17408, 1024).rearrange("p (b n) -> p b n", b=2)
        rope = part(room, 18432, 1280).rearrange("p (t w n) -> p t w n", t=TP + 1, w=2)
        s_m = part(room, 16384, 1024).rearrange("p (b n) -> p b n", b=2)
        p_b = part(room, 17408, 1024).rearrange("p (b n) -> p b n", b=2)
        pt_b = part(room, 18432, 1024).rearrange("p (b n) -> p b n", b=2)
        o_1 = part(room, 19456, 128)
        ht_high_r = x_r[:, :, :].rearrange("p t d -> p (t d)")[:, 0:KT_D * NT].rearrange("p (k t) -> p k t", k=KT_D)
        mt_high_r = part(room_r, 12672, KT_D * NT).rearrange("p (k t) -> p k t", k=KT_D)
        stage = mix[:, 0:2048].rearrange("p (b n) -> p b n", b=4)
        mixv = mix[:, :].rearrange("p (t d) -> p t d", t=TP)
        keep = 3 * SLOT
        qrep = part(ring, keep, 2048).rearrange("p (m g t) -> p m g t", m=2, g=16)
        k_s = ring[0:NS, keep + 2048:keep + 3072].rearrange("p (m d) -> p m d", m=2)
        v_s = ring[0:NS, keep + 3072:keep + 4096].rearrange("p (m d) -> p m d", m=2)
        NK, NV = 3, 5
        kraw = part(ring, 0, NK * 2048).rearrange("p (b t d) -> p b t d", b=NK, t=4)
        ktg = part(ring, NK * 2048, NK * 2048).rearrange("p (b g n) -> p b g n", b=NK, g=16)
        vg = part(room, 0, NV * 2048).rearrange("p (b i d) -> p b i d", b=NV, i=4)
        o_s = part(room, 10240, 2048).rearrange("p (w d) -> p w d", w=16)
        kn = part(room, 12288, 1024).rearrange("p (b d) -> p b d", b=2)
        ktn = part(room, 13312, 1024).rearrange("p (b g n) -> p b g n", b=2, g=16)
        vn = part(room, 14336, 1024).rearrange("p (b d) -> p b d", b=2)
        p_s = part(room, 15360, 1088).rearrange("p (b n) -> p b n", b=2)
        pt_s = part(room, 16448, 1024).rearrange("p (b n) -> p b n", b=2)
        ptn = part(room, 17472, 256).rearrange("p (b n) -> p b n", b=2)
        sm_s = part(room, 17728, 704).rearrange("p (b n) -> p b n", b=2)
        qbd = part(room, 18432, 1024).rearrange("p (b g i q) -> p b g i q", b=2, g=16, i=4)
        small = part(room, 19456, 256)
        blk = small[:, 0:32]
        blk_t = small[:, 32:64]
        blk_r = small[:, 64:96]
        blk_o = small[:, 96:128]
        rs_s = small[:, 128:160].rearrange("p (h w) -> p h w", h=2)
        l_s = small[:, 160:176]
        ob_t = part(room, 0, 256)
        ob_q = part(room, 256, 256)
        ob_r = part(room, 512, 256)
        gate = mix[:, 0:2048].rearrange("p (s d) -> p s d", s=2)
        gate2 = mix[:, 2048:4096].rearrange("p (s d) -> p s d", s=2)
        ln1 = part(room, 1024, 2048).rearrange("p (w d) -> p w d", w=2)
        y_sb = part(room, 3072, 2048).rearrange("p (b d) -> p b d", b=2)
        st_r = room[0:16, 5120:5120 + 2 * DFF]
        ln2 = part(room, 12672, 3072).rearrange("p (w d) -> p w d", w=3)
        gt = part(room, 0, FT * NT).rearrange("p (f t) -> p f t", f=FT)
        u_b = part(room, 15744, 2 * (NT + 2)).rearrange("p (b n) -> p b n", b=2)
        cv = part(room, 16900, 2 * NT).rearrange("p (b n) -> p b n", b=2)
        ga = part(room, 18052, 2 * NT).rearrange("p (b n) -> p b n", b=2)
        ext = part(room, 19204, 160).rearrange("p (b s t) -> p b s t", b=2, s=DB)
        st_t = mix[:, 0:704].rearrange("p (f r) -> p f r", f=2 * FT)
        u_last = mix[:, 704:704 + 792].rearrange("p (f r) -> p f r", f=2 * FT)
        ht_flat = ht[:, :, :].rearrange("p k t -> p (k t)")
        NG_BUF = 6
        g_high_r = ht_r[:, :, :].rearrange("p k t -> p (k t)")[:, 0:NG_BUF * NT].rearrange("p (b t) -> p b t", b=NG_BUF)
        g_rest_r = part(room_r, 15744, NG_BUF * NT).rearrange("p (b t) -> p b t", b=NG_BUF)
        y3 = part(room, 15744 + NG_BUF * NT, CH)
        gexp = part(room, 3072, 1024).rearrange("p (g b s) -> p g b s", g=16, b=DB)

        def conv_out(i):
            at = NG_BUF * NT + CH * (i % 2)
            return ht_flat[0:18, at:at + CH]

        early = sem("early_loaded")
        tables = sem("tables_loaded")
        x_in = sem("x_loaded")
        w_in_slot = [sem(f"w_loaded_{i}") for i in range(N_SLOTS)]
        w_used = sem("w_used")
        vecs_t = sem("vecs_transposed")
        vecs_c = sem("vecs_copied")
        act_setup = sem("act_setup")
        dve_seq = sem("dve_seq")
        act_seq = sem("act_seq")
        pool_seq = sem("pool_seq")
        c_tr = sem("c_transposed")
        c_cp = sem("c_copied")
        bank6_zero = sem("bank6_zero")
        ada_mm = sem("ada_product")
        ada_ms = sem("ada_rows_copied")
        ada_tt = sem("ada_transposed")
        ada_ok = sem("ada_ready")
        xt_mm = sem("xt_transposed")
        xt_d = sem("xt_taken_dve")
        xt_a = sem("xt_taken_act")
        pj_mm = sem("proj_product")
        pj_d = sem("proj_taken_dve")
        pj_a = sem("proj_taken_act")
        rope_ok = sem("rope_done")
        qk_t = sem("qk_transposed")
        qk_d = sem("qk_taken_dve")
        qk_a = sem("qk_taken_act")
        qzero = sem("qtp_zeroed")
        stg = [sem(f"stage_stored_{i}") for i in range(4)]
        out_sem = sem("rows_stored")
        pa_s = sem("pa_scores")
        pa_min = sem("pa_masked")
        pa_exp = sem("pa_exp")
        pa_t = sem("pa_transposed")
        pa_pt = sem("pa_pt_copied")
        pa_pv = sem("pa_pv")
        pa_o = sem("pa_out_taken")
        rms_sq = sem("rms_sums")
        rms_rt = sem("rms_roots")
        rms_ok = sem("rms_done")
        kg_in = [sem(f"k_group_loaded_{i}") for i in range(NK)]
        vg_in = [sem(f"v_group_loaded_{i}") for i in range(NV)]
        new_in = [sem(f"new_rows_loaded_{i}") for i in range(2)]
        new_zero = sem("new_zeroed")
        kg_t = sem("k_group_turned")
        kn_t = sem("k_new_turned")
        q_bd = sem("q_spread")
        sa_g = sem("sa_group_scored")
        sa_s = sem("sa_scores")
        sa_min = sem("sa_min")
        sa_exp = sem("sa_exp")
        sa_t = sem("sa_transposed")
        sa_pt = sem("sa_pt_copied")
        sa_vg = sem("sa_group_weighted")
        sa_pv = sem("sa_pv")
        sa_o = sem("sa_out_taken")
        sa_l = sem("sa_sums")
        sa_n = sem("sa_normed")
        sa_x = sem("sa_picked")
        sa_fin = sem("sa_placed")
        sa_sq = sem("sa_square_sums")
        sa_q = sem("sa_mean_squares")
        sa_r = sem("sa_roots")
        page_in = sem("pages_loaded")
        mt_mm = sem("mixed_transposed")
        mt_d = sem("mixed_taken")
        gb_mm = sem("gate_spread")
        gb_a = sem("gate_copied")
        ln_in = sem("ln_rows_loaded")
        ln2_in = sem("ln2_rows_loaded")
        wo_mm = sem("wo_product")
        wo_d = sem("wo_taken")
        n_var = sem("norm_variance")
        n_rt = sem("norm_root")
        x1_ok = sem("x1_ready")
        st_in = sem("state_loaded")
        st_mm = sem("state_transposed")
        st_ok = sem("state_ready")
        h2_mm = sem("h2_transposed")
        h2_d = sem("h2_taken_dve")
        h2_a = sem("h2_taken_act")
        up_mm = sem("up_product")
        up_u = sem("up_taken")
        up_c0 = sem("conv_started")
        up_x = sem("ext_ready")
        up_cv = sem("conv_done")
        up_ge = sem("gelu_done")
        up_gt = sem("gated")
        halo = sem("halo_zeroed")
        us_mm = sem("last_rows_transposed")
        us_a = sem("last_rows_copied")
        dn_mm = sem("down_product")
        dn_d = sem("down_taken")
        y_out = sem("y_ready")
        stored = sem("stored")
        conv_st = [sem(f"conv_state_stored_{i}") for i in range(2)]
        x_back = sem("x_reloaded")
        spilled = sem("x1_spilled")
        x1_back = sem("x1_reloaded")
        win_high = sem("w_in_high")
        win_pool = sem("w_in_rest_pool")
        win_dve = sem("w_in_rest_dve")
        win_free = sem("w_in_slice_used")
        wl_high = sem("late_weights_high")
        wl_rest = sem("late_weights_rest")
        ht_rest = sem("ht_rest")
        mt_hi = sem("mixed_high")
        g_split = sem("gated_split")
        g_used = sem("gated_used")
        gb2 = sem("gated_bias")
        copied = sem("window_copied")
        block = ctx.enter_context(nc.Block())

        units = [(s, t) for s in range(6) for t in range(TP + 1)]
        rope_units = [n for n, (s, t) in enumerate(units) if s in (0, 1, 3, 4)]
        v_units = [n for n, (s, t) in enumerate(units) if s in (2, 5)]
        tr_units = [n for n in rope_units if not (units[n][0] in (1, 4) and units[n][1] == TP)]
        pa = [(0, n, qb) for n in range(8) for qb in range(4)] \
            + [(1, 2 * h + c, qb) for h in range(4) for qb in range(4) for c in range(2)]
        NU = len(pa)
        sa = [(m, b) for b in range(DB) for m in range(2)]
        groups = {0: [4, 4, 2], 1: [4, 4, 4, 4]}
        NG = [sum(len(groups[m]) for m, b in sa[:w]) for w in range(17)]

        def d_units(n):
            return sum(k in rope_units for k in range(n + 1))

        def a_units(n):
            return sum(k in v_units for k in range(n + 1))

        last_t, last_store, n_stored = [], [], [0] * 4
        user = [None] * 4
        for r, n in enumerate(rope_units):
            sec, t = units[n]
            last_t.append(None if user[r % 4] is None else tr_units.index(user[r % 4]) + 1)
            last_store.append(n_stored[r % 4])
            if not (sec in (1, 4) and t == TP):
                user[r % 4] = n
                n_stored[r % 4] += sec in (1, 4)

        def up_bank(k):
            return wide[k % 3][:, :].rearrange("p (h t) -> p h t", h=2)[:, :, 0:HALF_NT]

        def slot_count(n):
            return 16 * sum(2 if CHUNKS[i][0] == "up" else 1 for i in range(n + 1) if SLOT_OF[i] == SLOT_OF[n])

        def k_count(m, w, g):
            G = NG[w] + g
            return 64 * (G // NK + 1)

        def v_count(m, w, g):
            G = NG[w] + g
            return 64 * (G // NV + 1)

        flat_k = {0: a["cache_win_k"][0], 1: a["cache_k"][0]}
        flat_v = {0: a["cache_win_v"][0], 1: a["cache_v"][0]}

        @block.sync
        def _(sp):
            def load_chunk(n):
                kind, i = CHUNKS[n]
                if (prev := chunk_before(n)) is not None and CHUNKS[prev][0] == "down":
                    half, kg = divmod(CHUNKS[prev][1], 3)
                    sp.wait_ge(g_used, FT * half + min(FT, 8 * kg + 8))
                elif prev is not None:
                    sp.wait_ge(w_used, prev + 1)
                if CHUNKS[n] == ("ada", 6):
                    sp.wait_ge(w_used, CHUNK_AT[("in", 5)] + 1)
                s = w_in_slot[SLOT_OF[n]]
                dst = slot(SLOT_OF[n])
                src = a[{"ada": "w_ada", "in": "w_in", "o": "w_o", "up": "w_up", "down": "w_down"}[kind]][0]
                src = src.rearrange("(k p) n -> p k n", p=P)
                if kind == "up":
                    for g in range(2):
                        sp.dma_start(dst[:, :, 256 * g:256 * g + 256],
                                     src[:, :, DFF * g + 256 * i:DFF * g + 256 * i + 256]).then_inc(s, 16)
                elif kind == "down":
                    half, kg = divmod(i, 3)
                    nk = min(8, FT - 8 * kg)
                    sp.dma_start(dst[:, 0:nk, :], src[:, 8 * kg:8 * kg + nk, CH * half:CH * half + CH]).then_inc(s, 16)
                else:
                    sp.dma_start(dst, src[:, :, CH * i:CH * i + CH]).then_inc(s, 16)

            sp.dma_start(ident[:, :], a["ident"]).then_inc(early, 16)
            sp.dma_start(c_r[0:1, :], a["c_prompt"]).then_inc(early, 16)
            sp.dma_start(c_r[1:C, :], a["c_sample"]).then_inc(early, 16)
            rows = lambda name: a[name].rearrange("l (r d) -> (l r) d", d=P)
            conv = a["w_conv"].rearrange("l j (r d) -> (l j) r d", d=P)
            sp.dma_start(vec_r[0:48, 0, :], rows("b_ada")).then_inc(early, 16)
            sp.dma_start(vec_r[48:92, 0, :], rows("b_up")).then_inc(early, 16)
            sp.dma_start(vec_r[92:93, 0, :], a["subln_g"]).then_inc(early, 16)
            sp.dma_start(vec_r[0:44, 1, :], conv[0]).then_inc(early, 16)
            sp.dma_start(vec_r[44:88, 1, :], conv[1]).then_inc(early, 16)
            sp.dma_start(vec_r[0:44, 2, :], conv[2]).then_inc(early, 16)
            sp.dma_start(vec_r[44:88, 2, :], rows("b_conv")).then_inc(early, 16)
            sp.dma_start(sum9[:, :], a["sum9"]).then_inc(early, 16)
            for i, name in enumerate(("lambda_q1", "lambda_k1", "lambda_q2", "lambda_k2")):
                sp.dma_start(lam4[:, i, :], a[name].to_broadcast([P, 64])).then_inc(early, 16)
            load_chunk(0)
            load_chunk(1)
            sp.dma_start(x_sb[0:NS, TP, :], a["x_sample"].rearrange("b s d -> (b s) d")).then_inc(x_in, 16)
            sp.dma_start(x_sb[:, 0:TP, :], a["x_prompt"][0].rearrange("(t p) d -> p t d", p=P)).then_inc(x_in, 16)
            load_chunk(2)
            load_chunk(3)
            for dst, name in ((rope, "rope"), (maskt, "maskt"), (smask, "smask"), (sums, "sums"), (pick, "pick"),
                              (colmask, "colmask"), (ones, "ones"), (diff_c, "diff_c"), (perm, "perm")):
                if name != "rope":
                    dst = dst[:]
                sp.dma_start(dst, a[name]).then_inc(tables, 16)
            sp.dma_start(pages[:, :], a["page_table"].rearrange("b n -> (b n)").rearrange("(o n) -> o n", o=1)).then_inc(page_in, 16)
            for n in range(4, 6):
                load_chunk(n)

            def move_window(i):
                for name, dst in (("cache_win_k", "wks"), ("cache_win_v", "wvs")):
                    sp.dma_start(o[dst][0, i, 0:PAST - DS], a[name][0, i, DS:PAST]).then_inc(copied, 16)

            def flat(ap):
                return ap.rearrange("t h d -> t (h d)")

            n_rope = n_v = 0
            for n, (s, t) in enumerate(units):
                kb_rows = slice(P * t, P * t + P)
                if s in (0, 3):
                    n_rope += 1
                elif s in (1, 4):
                    m = s // 3
                    sp.wait_ge(rope_ok, n_rope + 1)
                    if t < TP:
                        st = n_rope % 4
                        dst = flat((o["wkp"] if m == 0 else o["kkp"])[0, 0])[kb_rows, :]
                        sp.dma_start(dst, stage[:, st, :]).then_inc(stg[st], 16)
                    else:
                        if m == 0:
                            for b in range(DB):
                                sp.dma_start(flat(o["wks"][0, b])[PAST - DS:PAST, :],
                                             k_s[DS * b:DS * b + DS, 0, :]).then_inc(out_sem, 16)
                        else:
                            sp.dma_start(o["kks"][0].rearrange("b s h d -> (b s) (h d)"), k_s[:, 1, :]).then_inc(out_sem, 16)
                    n_rope += 1
                else:
                    m = s // 3
                    n_v += 1
                    sp.wait_ge(pj_a, n_v)
                    if t < TP:
                        dst = flat((o["wvp"] if m == 0 else o["kvp"])[0, 0])[kb_rows, :]
                        sp.dma_start(dst, vp[:, t, m, :]).then_inc(out_sem, 16)
                    elif m == 0:
                        for b in range(DB):
                            sp.dma_start(flat(o["wvs"][0, b])[PAST - DS:PAST, :],
                                         v_s[DS * b:DS * b + DS, 0, :]).then_inc(out_sem, 16)
                    else:
                        sp.dma_start(o["kvs"][0].rearrange("b s h d -> (b s) (h d)"), v_s[:, 1, :]).then_inc(out_sem, 16)
                if t == TP:
                    move_window(s)
                    load_chunk(6 + s)
            sp.wait_ge(w_used, CHUNK_AT[("in", 5)] + 1)
            sp.dma_start(x_sb[0:NS, TP, :], a["x_sample"].rearrange("b s d -> (b s) d")).then_inc(x_back, 16)
            sp.dma_start(x_sb[:, 0:TP, :], a["x_prompt"][0].rearrange("(t p) d -> p t d", p=P)).then_inc(x_back, 16)
            for n in range(12, 18):
                load_chunk(n)

            sp.wait_ge(page_in, 16)
            sp.wait_ge(w_used, 18)
            sp.wait_ge(new_zero, 1)
            for w, (m, b) in enumerate(sa):
                win_k = flat_k[0][b].rearrange("(g r) h d -> g r (h d)", r=16)
                for g, nt in enumerate(groups[m]):
                    G = NG[w] + g
                    ks = G % NK
                    if G >= NK:
                        sp.wait_ge(kg_t, G - NK + 1)
                    if m == 0 and g < 2:
                        sp.dma_start(kraw[:, ks, :, :], win_k[:, 4 * g:4 * g + 4, :]).then_inc(kg_in[ks], 64)
                    elif m == 0:
                        for i in range(4):
                            sp.dma_start(kraw[32 * i:32 * i + 32, ks, 0:2, :],
                                         win_k[96:128, 8 + i:16:4, :]).then_inc(kg_in[ks], 16)
                    else:
                        for t in range(4):
                            pg = sp.value_load(pages[0:1, N_PAGES * b + 4 * g + t:N_PAGES * b + 4 * g + t + 1],
                                               min_val=0, max_val=a["cache_k"].shape[1] - 1)
                            sp.dma_start(kraw[:, ks, t, :], flat_k[1][bass.ds(pg, 1)].rearrange("a p h d -> (a p) (h d)"))\
                                .then_inc(kg_in[ks], 16)
                nw = w % 2
                if w >= 2:
                    sp.wait_ge(kn_t, w - 1)
                    sp.wait_ge(sa_pv, w - 1)
                sp.dma_start(kn[0:DS, nw, :], k_s[DS * b:DS * b + DS, m, :]).then_inc(new_in[nw], 16)
                sp.dma_start(vn[0:DS, nw, :], v_s[DS * b:DS * b + DS, m, :]).then_inc(new_in[nw], 16)

            sp.wait_ge(sa_fin, 2)
            for n in range(FIRST_LATE, FIRST_LATE + 2):
                load_chunk(n)
            for i, name in enumerate(("ln1_g", "ln1_b")):
                sp.dma_start(ln1[:, i, :], a[name].to_broadcast([P, D])).then_inc(ln_in, 16)
            sp.dma_start(st_r, a["state_conv"][0].rearrange("b j f -> (b j) f")).then_inc(st_in, 16)
            for n in range(FIRST_LATE + 2, FIRST_LATE + 4):
                load_chunk(n)
            for i, name in enumerate(("b_down", "ln2_g", "ln2_b")):
                sp.dma_start(ln2[:, i, :], a[name].to_broadcast([P, D])).then_inc(ln2_in, 16)
            for t in range(TP + 1):
                sp.wait_ge(x1_ok, t + 1)
                rows = P if t < TP else NS
                sp.dma_start(spill[P * t:P * t + rows, :], x_sb[0:rows, t, :]).then_inc(spilled, 16)
            for n in range(FIRST_LATE + 4, FIRST_LATE + 13):
                load_chunk(n)
                if n < FIRST_LATE + 6:
                    move_window(6 + n - FIRST_LATE - 4)
            load_chunk(FIRST_LATE + 13)
            sp.wait_ge(spilled, 16 * (TP + 1))
            sp.wait_ge(up_mm, 2 * FT)
            sp.dma_start(x_sb[:, 0:TP, :], spill[0:SEQ, :].rearrange("(t p) d -> p t d", p=P)).then_inc(x1_back, 16)
            sp.dma_start(x_sb[0:NS, TP, :], spill[SEQ:NT, :]).then_inc(x1_back, 16)
            load_chunk(FIRST_LATE + 14)
            for i in range(11):
                sp.wait_ge(us_a, i + 1)
                sp.dma_start(o["cp"][0, 0][:, CH * i:CH * i + CH], conv_out(i)[0:2, :]).then_inc(conv_st[i % 2], 16)
                sp.dma_start(o["cs"][0].rearrange("b j f -> (b j) f")[:, CH * i:CH * i + CH],
                             conv_out(i)[2:18, :]).then_inc(conv_st[i % 2], 16)
            for n in range(FIRST_LATE + 15, len(CHUNKS)):
                load_chunk(n)
            for t in range(TP + 1):
                sp.wait_ge(y_out, t + 1)
                if t < TP:
                    sp.dma_start(o["yp"][0, P * t:P * t + P, :], x_sb[:, t, :]).then_inc(stored, 16)
                else:
                    sp.dma_start(o["ys"].rearrange("b s d -> (b s) d"), x_sb[0:NS, t, :]).then_inc(stored, 16)
            sp.wait_ge(stored, 16 * (TP + 1))
            sp.wait_ge(conv_st[0], 32 * 6)
            sp.wait_ge(conv_st[1], 32 * 5)
            sp.wait_ge(copied, 16 * 2 * DB)
            sp.wait_ge(out_sem, 16 * (TP * 2 + 2 * DB + 2))
            for st in range(4):
                sp.wait_ge(stg[st], 16 * n_stored[st])

        @block.gpsimd
        def _(pool):
            pool.wait_ge(c_tr, 1)
            pool.wait_ge(vecs_c, 1)
            nc.gpsimd.memset(qtp, 0.0).then_inc(qzero, 1)
            jobs = [(n, "rope", r) for r, n in enumerate(rope_units)]
            jobs += [(5 * c - 1.4, "split", c) for c in range(6)]
            for _, what, r in sorted(jobs):
                if what == "split":
                    n = CHUNK_AT[("in", r)]
                    for k in range(0, KT_D, 2):
                        pool.wait_ge(win_high, 4 * r + k // 2 + 1)
                        w = slot(SLOT_OF[n])[:, k, :]
                        high, rest = pair_of(n, k)
                        nc.gpsimd.tensor_tensor(rest, w, high.bitcast(F32), ALU.subtract).then_inc(win_pool, 1)
                    continue
                s, t = units[rope_units[r]]
                sample_k = s in (1, 4) and t == TP
                pool.wait_ge(pj_d, r + 1)
                if not sample_k and r >= 4:
                    if (prev := last_t[r]) is not None:
                        pool.wait_ge(qk_t, prev)
                    if (q := last_store[r]) > 0:
                        pool.wait_ge(stg[r % 4], 16 * q)
                rows = P if t < TP else NS
                dst = k_s[:, s // 3, :] if sample_k else stage[0:rows, r % 4, :]
                nc.gpsimd.tensor_tensor(dst, tmp_a[0:rows, r % 2, :], tmp_b[0:rows, r % 2, :], ALU.add)\
                    .then_inc(rope_ok, 1)
            pool.wait_ge(pa_pv, NU)
            pool.wait_ge(pa_o, NU)
            nc.gpsimd.memset(kn, 0.0).then_inc(pool_seq, 1)
            nc.gpsimd.memset(ktn, 0.0).then_inc(pool_seq, 1)
            nc.gpsimd.memset(small, 0.0).then_inc(pool_seq, 1)
            nc.gpsimd.memset(qbd, 0.0).then_inc(new_zero, 1)
            pool.wait_ge(new_zero, 1)
            pool.wait_ge(qk_d, len(tr_units) - 2 * TP)
            for w, (m, b) in enumerate(sa):
                if w >= 2:
                    pool.wait_ge(sa_s, w - 1)
                for i in range(4):
                    last = nc.gpsimd.tensor_copy(qbd[32 * i:32 * i + 32, w % 2, :, i, :],
                                                 qrep[32 * i:32 * i + 32, m, :, DS * b:DS * b + DS])
                last.then_inc(q_bd, 1)
            def rest_of_piece(q):
                n, k = PIECES[q]
                pool.wait_ge(wl_high, q + 1)
                w = slot(SLOT_OF[n])[:, k:k + 2, :]
                high, rest = pair_of(n, slice(k, k + 2))
                nc.gpsimd.tensor_tensor(rest, w, high.bitcast(F32), ALU.subtract).then_inc(wl_rest, 1)

            for q in range(12):
                rest_of_piece(q)
            pool.wait_ge(wo_mm, 2 * TP + 2)
            nc.gpsimd.memset(u_b[:, :, 0:2], 0.0).then_inc(halo, 1)
            pool.wait_ge(st_ok, 11)
            for k in range(2 * FT):
                f = k // 2 + FT * (k % 2)
                if k >= 2:
                    pool.wait_ge(up_cv, k - 1)
                rest_of_piece(12 + k)
                nc.gpsimd.tensor_copy(ext[:, k % 2, :, 0:2], st_t[:, f, :].rearrange("p (b j) -> p b j", b=DB))
                pool.wait_ge(up_u, k + 1)
                u3 = u_b[:, k % 2, 2 + SEQ:2 + NT].rearrange("p (b s) -> p b s", b=DB)
                nc.gpsimd.tensor_copy(ext[:, k % 2, :, 2:2 + DS], u3)
                nc.gpsimd.tensor_copy(u_last[:, f, 2:18].rearrange("p (b j) -> p b j", b=DB), u3[:, :, DS - 2:DS])
                nc.gpsimd.tensor_copy(u_last[:, f, 0:2], u_b[:, k % 2, SEQ:SEQ + 2]).then_inc(up_x, 1)
            for q in range(12 + 2 * FT, len(PIECES)):
                rest_of_piece(q)

        @block.scalar
        def _(act):
            act.wait_ge(early, 16 * 15)
            nc.scalar.activation(c_e, c_r, ACT.Exp, scale=-1.0).then_inc(act_setup, 1)
            act.wait_ge(dve_seq, 2)
            nc.scalar.activation(lam_s[:, 2:4], lam_s[:, 0:2], ACT.Exp).then_inc(act_setup, 1)
            act.wait_ge(ada_ok, 4)
            for f in range(1, KT_D, 2):
                act.wait_ge(xt_mm, f + 2)
                nc.scalar.activation(ht[:, f, 0:SEQ], bk(f % 4), ACT.Identity, bias=mod_t[:, f, 0:1],
                                     scale=mod_t[:, 8 + f, 0:1]).then_inc(xt_a, 1)
            jobs = []
            for n, (s, t) in enumerate(units):
                if n in v_units:
                    jobs.append((n, "v", n))
                if n in tr_units and s in (0, 3) and t < TP:
                    jobs.append((n + 2.5, "q", n))
            act.wait_ge(qzero, 1)
            for _, what, n in sorted(jobs):
                s, t = units[n]
                rows = P if t < TP else NS
                if what == "v":
                    act.wait_ge(pj_mm, n + 1)
                    dst = vp[:, t, s // 3, :] if t < TP else v_s[:, s // 3, :]
                    nc.scalar.activation(dst, bk(n % 4)[0:rows, :], ACT.Copy).then_inc(pj_a, 1)
                else:
                    k = tr_units.index(n)
                    act.wait_ge(qk_t, k + 1)
                    src = bk(4 + k % 2).rearrange("p (f t) -> p f t", f=4)
                    m0 = 8 * (s // 3)
                    for h in range(2):
                        last = nc.scalar.activation(qtp[64 * h:64 * h + 64, m0 + h:m0 + 8:2, P * t:P * t + P],
                                                    src[64 * h:64 * h + 64], ACT.Copy)
                    last.then_inc(qk_a, 1)
            for u, (m, n, qb) in enumerate(pa):
                act.wait_ge(pa_min, u + 1)
                if u >= 2:
                    act.wait_ge(pa_t, u - 1)
                w = P * (qb + 1)
                nc.scalar.activation(p_b[:, u % 2, 0:w], s_m[:, u % 2, 0:w], ACT.Exp, bias=mn[:, u:u + 1], scale=-1.0,
                                     accum_out=rs[:, u:u + 1]).then_inc(pa_exp, 1)
            act.wait_ge(rms_sq, 1)
            nc.scalar.activation(rms[:, 1, :], rms[:, 0, :], ACT.Sqrt).then_inc(rms_rt, 1)
            def load_values(w):
                m, b = sa[w]
                win_v = flat_v[0][b].rearrange("(g r) h d -> g r (h d)", r=16)
                for g, nt in enumerate(groups[m]):
                    G = NG[w] + g
                    vs = G % NV
                    if G >= NV:
                        act.wait_ge(sa_vg, G - NV + 1)
                    if m == 0 and g < 2:
                        for t in range(4):
                            act.dma_start(vg[32 * t:32 * t + 32, vs, :, :],
                                          win_v[:, 4 * g + t, :].rearrange("(i m) f -> m i f", i=4)).then_inc(vg_in[vs], 16)
                    elif m == 0:
                        for t in range(2):
                            act.dma_start(vg[32 * t:32 * t + 32, vs, :, :],
                                          win_v[96:128, 8 + 4 * t:12 + 4 * t, :]).then_inc(vg_in[vs], 32)
                    else:
                        for t in range(4):
                            pg = act.value_load(pages[0:1, N_PAGES * b + 4 * g + t:N_PAGES * b + 4 * g + t + 1],
                                                min_val=0, max_val=a["cache_v"].shape[1] - 1)
                            act.dma_start(vg[32 * t:32 * t + 32, vs, :, :],
                                          flat_v[1][bass.ds(pg, 1)].rearrange("a (i m) h d -> m (a i) (h d)", i=4))\
                                .then_inc(vg_in[vs], 16)

            act.wait_ge(page_in, 16)
            act.wait_ge(pa_pv, NU)
            act.wait_ge(pa_o, NU)
            act.wait_ge(out_sem, 16 * (TP * 2 + 2 * DB + 2))
            load_values(0)
            for w, (m, b) in enumerate(sa):
                n = 32 * sum(groups[m]) + 32
                act.wait_ge(sa_min, w + 1)
                for h in range(2):
                    if w >= 1:
                        act.wait_ge(sa_t, 2 * (w - 1) + h + 1)
                    src = sm_s[:, h, 0:n] if m == 0 else wide[h][:, 0:n]
                    nc.scalar.activation(p_s[:, h, 0:n], src, ACT.Exp, bias=blk_o[:, h:h + 1], scale=-1.0,
                                         accum_out=rs_s[:, h, w:w + 1]).then_inc(sa_exp, 1)
                if w + 1 < len(sa):
                    load_values(w + 1)
                act.wait_ge(sa_pv, w + 1)
                nc.scalar.activation(o_s[:, w, :], bk(6)[:, 0:P], ACT.Copy).then_inc(sa_o, 1)
            act.wait_ge(sa_q, 1)
            nc.scalar.activation(ob_q, ob_q, ACT.Sqrt).then_inc(sa_r, 1)
            act.wait_ge(mt_d, 8)
            for j in range(8):
                act.wait_ge(gb_mm, j + 1)
                which, kind, half = j // 4, (j // 2) % 2, j % 2
                g = gate if which == 0 else gate2
                rows = P if kind == 0 else NS
                nc.scalar.activation(g[0:rows, kind, CH * half:CH * half + CH], bk(4 + j % 2)[0:rows, :], ACT.Copy)\
                    .then_inc(gb_a, 1)
            for t in range(TP + 1):
                act.wait_ge(n_var, t + 1)
                nc.scalar.activation(mv[:, 2:3], mv[:, 1:2], ACT.Sqrt).then_inc(n_rt, 1)
            for f in range(1, KT_D, 2):
                act.wait_ge(h2_mm, f + 2)
                nc.scalar.activation(ht[:, f, 0:SEQ], bk(f % 4), ACT.Identity, bias=mod_t[:, 24 + f, 0:1],
                                     scale=mod_t[:, 32 + f, 0:1]).then_inc(h2_a, 1)
            act.wait_ge(halo, 1)
            for k in range(2 * FT):
                f = k // 2 + FT * (k % 2)
                act.wait_ge(up_mm, k + 1)
                if k >= 2:
                    act.wait_ge(up_x, k - 1)
                    act.wait_ge(up_cv, k - 1)
                pair = up_bank(k)
                nc.scalar.activation(u_b[:, k % 2, 2:2 + NT].rearrange("p (h t) -> p h t", h=2), pair, ACT.Identity,
                                     bias=vec_t[:, 0, 48 + f:49 + f]).then_inc(up_u, 1)
                act.wait_ge(up_u, k + 1)
                if k >= 2:
                    if k % 2 == 0:
                        act.wait_ge(up_ge, k // 2)
                    else:
                        act.wait_ge(up_gt, k // 2)
                nc.scalar.activation(cv[:, k % 2, :], u_b[:, k % 2, 2:2 + NT], ACT.Identity,
                                     bias=vec_t[:, 2, 44 + f:45 + f], scale=vec_t[:, 2, f:f + 1]).then_inc(up_c0, 1)
                if k % 2 == 1:
                    act.wait_ge(up_cv, k)
                    if k >= 5:
                        act.wait_ge(up_gt, k // 2 - 1)
                    nc.scalar.activation(ga[:, (k // 2) % 2, :], cv[:, 0, :], ACT.Gelu).then_inc(up_ge, 1)
            for i in range(11):
                act.wait_ge(us_mm, i + 1)
                if i >= 2:
                    act.wait_ge(conv_st[i % 2], 32 * (i // 2))
                nc.scalar.activation(conv_out(i), bk(6 + i % 2)[0:18, :], ACT.Copy).then_inc(us_a, 1)
            for t in range(TP + 1):
                act.wait_ge(n_var, TP + 2 + t)
                nc.scalar.activation(mv[:, 2:3], mv[:, 1:2], ACT.Sqrt).then_inc(n_rt, 1)


        @block.vector
        def _(dve):
            steps = [0]

            def then(ins):
                steps[0] += 1
                ins.then_inc(dve_seq, 1)
                dve.wait_ge(dve_seq, steps[0])

            dve.wait_ge(early, 16 * 15)
            for i in range(2):
                then(nc.vector.tensor_tensor_reduce(out=lam4[:, 2 * i, :], in0=lam4[:, 2 * i, :], in1=lam4[:, 2 * i + 1, :],
                                                    scale=1.0, scalar=0.0, op0=ALU.mult, op1=ALU.add,
                                                    accum_out=lam_s[:, i:i + 1]))
            nc.vector.memset(bk(6), 0.0).then_inc(bank6_zero, 1)
            dve.wait_ge(vecs_t, 1)
            nc.vector.tensor_copy(vec_t[:, 0, 0:93], bk(0)[:, 0:93])
            then(nc.vector.tensor_copy(vec_t[:, 1:3, 0:88], bk(0)[:, P:3 * P].rearrange("p (r d) -> p r d", r=2)[:, :, 0:88]))
            nc.vector.tensor_copy(bada[:, :], vec_t[:, 0, 0:48])
            then(nc.vector.tensor_scalar(g8[:, :], vec_t[:, 0, 92:93], 1.0 - LAM_INIT, None, ALU.mult))
            for at in (8, 32):
                then(nc.vector.tensor_scalar(bada[:, at:at + 8], bada[:, at:at + 8], 1.0, None, ALU.add))
            nc.vector.memset(lam_s[:, 7:8], 0.0).then_inc(vecs_c, 1)
            dve.wait_ge(act_setup, 1)
            then(nc.vector.tensor_scalar(c_e, c_e, 1.0, None, ALU.add))
            then(nc.vector.reciprocal(c_e, c_e))
            nc.vector.tensor_tensor(c_s, c_r, c_e, ALU.mult).then_inc(c_cp, 1)
            dve.wait_ge(c_tr, 1)
            nc.vector.tensor_copy(c_t[:, :, :], bk(1)[:, 0:128].rearrange("p (k r) -> p k r", k=8)[:, :, 0:C]).then_inc(c_cp, 1)
            dve.wait_ge(act_setup, 2)
            then(nc.vector.tensor_tensor(lam_s[:, 4:5], lam_s[:, 3:4], lam_s[:, 2:3], ALU.subtract))
            then(nc.vector.tensor_scalar(lam_s[:, 5:6], lam_s[:, 4:5], -LAM_INIT, None, ALU.add))

            def ada(ch):
                dve.wait_ge(ada_mm, ch + 1)
                if ch >= 2:
                    dve.wait_ge(ada_tt, ch - 1)
                nc.vector.tensor_copy(mod_s[:, ch % 2, :], bk(6)).then_inc(ada_ms, 1)
                dve.wait_ge(ada_tt, ch + 1)
                nc.vector.tensor_tensor(mod_t[:, 4 * ch:4 * ch + 4, :],
                                        bk(7)[:, 0:64].rearrange("p (c r) -> p c r", c=4)[:, :, 0:C],
                                        bada[:, 4 * ch:4 * ch + 4][:, :, None].to_broadcast([P, 4, C]), ALU.add)\
                    .then_inc(ada_ok, 1)

            def high_of_piece(q):
                n, k = PIECES[q]
                dve.wait_ge(w_in_slot[SLOT_OF[n]], slot_count(n))
                nc.vector.tensor_copy(pair_of(n, slice(k, k + 2))[0], slot(SLOT_OF[n])[:, k:k + 2, :]).then_inc(wl_high, 1)

            def split_ht(k, high):
                then(nc.vector.tensor_copy(high[:, k, :], ht[:, k, :]))
                nc.vector.tensor_tensor(ht_r[:, k, :], ht[:, k, :], high[:, k, :].bitcast(F32), ALU.subtract).then_inc(ht_rest, 1)

            def modulate(mm, done, first, shift, scale):
                dve.wait_ge(mm, 1)
                src = bk(4).rearrange("p (f b s) -> p f b s", f=KT_D, b=DB)
                dst = ht[:, :, SEQ:NT].rearrange("p f (b s) -> p f b s", b=DB)
                col = lambda at: mod_t[:, at:at + 8, 1:C][:, :, :, None].to_broadcast([P, KT_D, DB, DS])
                then(nc.vector.tensor_tensor(dst, src, col(scale), ALU.mult))
                nc.vector.tensor_tensor(dst, dst, col(shift), ALU.add).then_inc(done, 1)
                for f in range(0, KT_D, 2):
                    dve.wait_ge(mm, f + 2)
                    nc.vector.tensor_scalar(ht[:, f, 0:SEQ], bk(f % 4), mod_t[:, scale + f, 0:1],
                                            mod_t[:, shift + f, 0:1], ALU.mult, ALU.add).then_inc(done, 1)

            def split_in(c, k):
                n = CHUNK_AT[("in", c)]
                if k == 0:
                    dve.wait_ge(w_in_slot[SLOT_OF[n]], slot_count(n))
                if c:
                    dve.wait_ge(win_free, 8 * (c - 1) + k + 1)
                w = slot(SLOT_OF[n])[:, k, :]
                high, rest = pair_of(n, k)
                if k % 2 == 0:
                    nc.vector.tensor_copy(high, w).then_inc(win_high, 1)
                else:
                    then(nc.vector.tensor_copy(high, w))
                    nc.vector.tensor_tensor(rest, w, high.bitcast(F32), ALU.subtract).then_inc(win_dve, 1)

            for ch in range(4):
                ada(ch)
            dve.wait_ge(ada_ok, 4)
            for k in range(KT_D):
                split_in(0, k)
            modulate(xt_mm, xt_d, True, 0, 8)
            dve.wait_ge(xt_mm, 9)
            dve.wait_ge(xt_d, 5)
            for k in range(KT_D):
                if k % 2:
                    dve.wait_ge(xt_a, k // 2 + 1)
                split_ht(k, ht_high_r)

            jobs = [(n, "rope", n) for n in rope_units]
            jobs += [(n + 2.5, "t", n) for n in tr_units if not (units[n][0] in (0, 3) and units[n][1] < TP)]
            jobs += [(5 * c - 1.4, "split", c) for c in range(1, 6)]
            dve.wait_ge(tables, 16 * 9)
            for _, what, n in sorted(jobs):
                if what == "split":
                    for k in range(KT_D):
                        split_in(n, k)
                    continue
                s, t = units[n]
                rows = P if t < TP else NS
                if what == "rope":
                    r = rope_units.index(n)
                    dve.wait_ge(pj_mm, n + 1)
                    if r >= 2:
                        dve.wait_ge(rope_ok, r - 1)
                    src = bk(n % 4)[0:rows].rearrange("p (h d) -> p h d", h=MAPS)
                    w = 0 if s in (0, 3) else 1
                    tb = tmp_b[0:rows, r % 2, :].rearrange("p (h d) -> p h d", h=MAPS)
                    ta = tmp_a[0:rows, r % 2, :].rearrange("p (h d) -> p h d", h=MAPS)
                    tab = lambda x, k: rope[0:rows, t, w, x:x + k][:, None, :].to_broadcast([rows, MAPS, k])
                    nc.vector.tensor_tensor(ta, src, tab(0, 64), ALU.mult)
                    nc.vector.tensor_tensor(tb[:, :, 0:32], src[:, :, 32:64], tab(64, 32), ALU.mult)
                    nc.vector.tensor_tensor(tb[:, :, 32:64], src[:, :, 0:32], tab(96, 32), ALU.mult).then_inc(pj_d, 1)
                else:
                    k = tr_units.index(n)
                    dve.wait_ge(qk_t, k + 1)
                    src = bk(4 + k % 2).rearrange("p (f t) -> p f t", f=4)
                    if t < TP:
                        nc.vector.tensor_copy(kt[:, 4 * (s // 3):4 * (s // 3) + 4, P * t:P * t + P], src).then_inc(qk_d, 1)
                    else:
                        for i in range(4):
                            for g in range(4):
                                last = nc.vector.tensor_copy(
                                    qrep[32 * i:32 * i + 32, s // 3, g:16:4, :],
                                    bk(4 + k % 2)[32 * g:32 * g + 32, 0:4 * NS].rearrange("p (f t) -> p f t", f=4))
                        last.then_inc(qk_d, 1)

            for st in range(4):
                dve.wait_ge(stg[st], 16 * n_stored[st])
            for s in range(NU + 3):
                if s < NU:
                    m, n, qb = pa[s]
                    w = P * (qb + 1)
                    dve.wait_ge(pa_s, s + 1)
                    if s >= 2:
                        dve.wait_ge(pa_exp, s - 1)
                    else:
                        dve.wait_ge(rope_ok, len(rope_units))
                    nc.vector.tensor_tensor_reduce(out=s_m[:, s % 2, 0:w], in0=bk(s % 2)[:, 0:w],
                                                   in1=maskt[:, m, SEQ - w:SEQ], scale=1.0, scalar=NEG, op0=ALU.add,
                                                   op1=ALU.min, accum_out=mn[:, s:s + 1]).then_inc(pa_min, 1)
                if 0 <= (x := s - 2) < NU:
                    w = P * (pa[x][2] + 1)
                    dve.wait_ge(pa_t, x + 1)
                    if x >= 2:
                        dve.wait_ge(pa_pv, x - 1)
                    nc.vector.tensor_copy(pt_b[:, x % 2, 0:w], bk(2 + x % 2)[:, 0:w]).then_inc(pa_pt, 1)
                if 0 <= (x := s - 3) < NU:
                    m, n, qb = pa[x]
                    dve.wait_ge(pa_exp, x + 1)
                    then(nc.vector.reciprocal(rcp[:, x:x + 1], rs[:, x:x + 1]))
                    dve.wait_ge(pa_pv, x + 1)
                    src = bk(4 + x % 2)
                    if m == 0:
                        nc.vector.tensor_scalar(mixv[:, qb, 64 * n:64 * n + 64], src[:, 64 * (n % 2):64 * (n % 2) + 64],
                                                rcp[:, x:x + 1], None, ALU.mult).then_inc(pa_o, 1)
                    elif n % 2 == 0:
                        nc.vector.tensor_scalar(o_1, src[:, 0:P], rcp[:, x:x + 1], None, ALU.mult).then_inc(pa_o, 1)
                        dve.wait_ge(pa_o, x + 1)
                    else:
                        then(nc.vector.tensor_scalar(rcp[:, x:x + 1], rcp[:, x:x + 1], lam_s[:, 5:6], None, ALU.mult))
                        nc.vector.scalar_tensor_tensor(out=mixv[:, qb, WID + 64 * (n - 1):WID + 64 * (n + 1)],
                                                       in0=src[:, 0:P], scalar=rcp[:, x:x + 1], in1=o_1,
                                                       op0=ALU.mult, op1=ALU.add).then_inc(pa_o, 1)
                if s < NU and s % 8 == 7:
                    ada(4 + s // 8)
            dve.wait_ge(pa_o, NU)
            sq = s_m[:, 0, :]
            for t in range(TP):
                mb = mixv[:, t, WID:D]
                then(nc.vector.tensor_tensor(sq, mb, mb, ALU.mult))
                then(nc.vector.tensor_reduce(rms[:, 2, 4 * t:4 * t + 4], sq.rearrange("p (h d) -> p h d", h=4), AX_X, ALU.add))
            nc.vector.tensor_scalar(rms[:, 0, :], rms[:, 2, :], 1.0 / P, EPS, ALU.mult, ALU.add).then_inc(rms_sq, 1)
            dve.wait_ge(rms_rt, 1)
            then(nc.vector.reciprocal(rms[:, 2, :], rms[:, 1, :]))
            for t in range(TP):
                mb = mixv[:, t, WID:D].rearrange("p (h d) -> p h d", h=4)
                last = nc.vector.tensor_tensor(mb, mb, rms[:, 2, 4 * t:4 * t + 4][:, :, None].to_broadcast([P, 4, P]), ALU.mult)
            last.then_inc(rms_ok, 1)

            dve.wait_ge(new_zero, 1)
            def turn_keys(w, g):
                m, b = sa[w]
                G = NG[w] + g
                dve.wait_ge(kg_in[G % NK], k_count(m, w, g))
                if G >= NK:
                    dve.wait_ge(sa_g, G - NK + 1)
                for t in range(groups[m][g]):
                    last = nc.vector.transpose(ktg[:, G % NK, :, 32 * t:32 * t + 32],
                                               kraw[:, G % NK, t, :].rearrange("p (g d) -> p g d", d=32))
                last.then_inc(kg_t, 1)

            def turn_new(w):
                dve.wait_ge(new_in[w % 2], 32 * (w // 2 + 1))
                if w >= 2:
                    dve.wait_ge(sa_s, w - 1)
                nc.vector.transpose(ktn[0:32, w % 2, :, :], kn[0:32, w % 2, :].rearrange("p (g d) -> p g d", d=32))\
                    .then_inc(kn_t, 1)

            for g in range(len(groups[0])):
                turn_keys(0, g)
            turn_new(0)
            for w, (m, b) in enumerate(sa):
                n = 32 * sum(groups[m])
                dve.wait_ge(sa_s, w + 1)
                if w >= 1:
                    dve.wait_ge(sa_exp, 2 * w)
                for h in range(2):
                    if m == 0:
                        then(nc.vector.tensor_tensor_reduce(out=sm_s[:, h, 0:n + 32], in0=wide[h][:, 0:n + 32],
                                                            in1=smask[:, 0:n + 32], scale=1.0, scalar=NEG,
                                                            op0=ALU.add, op1=ALU.min, accum_out=blk[:, h:h + 1]))
                    else:
                        then(nc.vector.tensor_tensor(wide[h][:, n:n + 32], wide[h][:, n:n + 32], smask[:, 352:384], ALU.add))
                        then(nc.vector.tensor_reduce(blk[:, h:h + 1], wide[h][:, 0:n + 32], AX_X, ALU.min))
                then(nc.vector.transpose(blk_t, blk))
                then(nc.vector.tensor_reduce(small[:, 176:184], blk_t.rearrange("p (i q) -> p q i", i=4), AX_X, ALU.min))
                then(nc.vector.tensor_copy(blk_r.rearrange("p (i q) -> p i q", i=4),
                                           small[:, 176:184][:, None, :].to_broadcast([P, 4, DS])))
                nc.vector.transpose(blk_o, blk_r).then_inc(sa_min, 1)
                if w + 1 < len(sa):
                    turn_keys(w + 1, 0)
                full = P * (n // P)
                for h in range(2):
                    dve.wait_ge(sa_t, 2 * w + h + 1)
                    if w >= 1:
                        dve.wait_ge(sa_pv, w)
                    if m == 0:
                        nc.vector.tensor_copy(pt_s[0:64, h, full:full + P], bk(4 + h)[0:64, full:full + P])
                    nc.vector.tensor_copy(pt_s[:, h, 0:full], bk(4 + h)[:, 0:full]).then_inc(sa_pt, 1)
                nc.vector.tensor_copy(ptn[0:32, :, :], bk(7)[0:32, 0:2 * P].rearrange("p (h c) -> p h c", h=2)).then_inc(sa_pt, 1)
                if w + 1 < len(sa):
                    for g in range(1, len(groups[sa[w + 1][0]])):
                        turn_keys(w + 1, g)
                    turn_new(w + 1)
            dve.wait_ge(sa_l, 1)
            then(nc.vector.reciprocal(l_s, bk(0)[:, 0:16]))
            then(nc.vector.tensor_scalar(lam_s[:, 6:7], diff_c[:, 1:2], lam_s[:, 5:6], diff_c[:, 0:1], ALU.mult, ALU.add))
            l_b = l_s.rearrange("p (b m) -> p b m", m=2)
            then(nc.vector.tensor_scalar(l_b[:, :, 1], l_b[:, :, 1], lam_s[:, 6:7], None, ALU.mult))
            dve.wait_ge(sa_o, 16)
            then(nc.vector.tensor_tensor(o_s, o_s, l_s[:, :, None].to_broadcast([P, 16, P]), ALU.mult))
            o_a = o_s.rearrange("p (b m) d -> p b m d", m=2)[:, :, 0, :]
            nc.vector.tensor_tensor(o_a, o_a, colmask[:, None, :].to_broadcast([P, DB, P]), ALU.mult).then_inc(sa_n, 1)
            dve.wait_ge(sa_x, 1)
            tok = lambda f: ht[:, f:f + 4, SEQ:NT].rearrange("p j (b q) -> p j b q", b=DB)
            bjq = lambda ap: ap.rearrange("p (b j q) -> p j b q", b=DB, j=4)
            jbq = lambda ap: ap.rearrange("p (j b q) -> p j b q", b=DB, j=4)
            nc.vector.tensor_copy(tok(0), bjq(bk(1)[:, 0:256])).then_inc(sa_fin, 1)
            then(nc.vector.tensor_copy(jbq(ob_t), bjq(bk(2)[:, 0:256])))
            nc.vector.tensor_tensor(ob_q, ob_t, ob_t, ALU.mult).then_inc(sa_n, 1)
            dve.wait_ge(sa_sq, 1)
            nc.vector.tensor_scalar(ob_q, bk(3)[:, 0:256], 1.0 / P, EPS, ALU.mult, ALU.add).then_inc(sa_q, 1)
            dve.wait_ge(sa_r, 1)
            then(nc.vector.reciprocal(ob_r, ob_q))
            then(nc.vector.tensor_tensor(ob_t, ob_t, ob_r, ALU.mult))
            nc.vector.tensor_scalar(tok(4), jbq(ob_t), g8[:, 0:1], None, ALU.mult).then_inc(sa_fin, 1)

            dve.wait_ge(ada_ok, 12)
            for g, at in enumerate((16, 40)):
                last = nc.vector.tensor_copy(gexp[:, 8 * g:8 * g + 8], mod_t[:, at:at + 8, 1:C][:, :, :, None]
                                             .to_broadcast([P, 8, DB, DS]))
            last.then_inc(mt_d, 1)
            for q in range(8):
                high_of_piece(q)
            for f in range(KT_D):
                dve.wait_ge(mt_mm, f + 1)
                if f < 4:
                    nc.vector.tensor_copy(ht[:, f, 0:SEQ], bk(f % 4)).then_inc(mt_d, 1)
                else:
                    nc.vector.tensor_scalar(ht[:, f, 0:SEQ], bk(f % 4), g8[:, 0:1], None, ALU.mult).then_inc(mt_d, 1)
                dve.wait_ge(mt_d, f + 2)
                split_ht(f, mt_high_r)

            def norm(t, rows, g_row, b_row, k):
                x = x_sb[0:rows, t, :]
                for h in range(2):
                    then(nc.vector.bn_stats(stat[0:rows, h, :], x[:, 512 * h:512 * h + 512]))
                then(nc.vector.bn_aggr(mv[0:rows, 0:2], stat[0:rows, :, :].rearrange("p h s -> p (h s)")))
                nc.vector.tensor_scalar(mv[0:rows, 1:2], mv[0:rows, 1:2], EPS, None, ALU.add).then_inc(n_var, 1)
                dve.wait_ge(n_rt, k + 1)
                then(nc.vector.reciprocal(mv[0:rows, 3:4], mv[0:rows, 2:3]))
                then(nc.vector.tensor_scalar(x, x, mv[0:rows, 0:1], mv[0:rows, 3:4], ALU.subtract, ALU.mult))
                then(nc.vector.tensor_tensor(x, x, g_row[0:rows], ALU.mult))
                return nc.vector.tensor_tensor(x, x, b_row[0:rows], ALU.add)

            dve.wait_ge(gb_a, 4)
            dve.wait_ge(gb_mm, 8)
            dve.wait_ge(ln_in, 32)
            dve.wait_ge(x_back, 32)
            for t in range(TP + 1):
                rows, kind = (P, 0) if t < TP else (NS, 1)
                for half in range(2):
                    j = 2 * t + half
                    dve.wait_ge(wo_mm, j + 1)
                    nc.vector.tensor_tensor(y_sb[0:rows, t % 2, 512 * half:512 * half + 512], bk(j % 4)[0:rows],
                                            gate[0:rows, kind, 512 * half:512 * half + 512], ALU.mult).then_inc(wo_d, 1)
                dve.wait_ge(wo_d, 2 * t + 2)
                x = x_sb[0:rows, t, :]
                then(nc.vector.scalar_tensor_tensor(out=x, in0=x, scalar=ALPHA, in1=y_sb[0:rows, t % 2, :],
                                                    op0=ALU.mult, op1=ALU.add))
                norm(t, rows, ln1[:, 0, :], ln1[:, 1, :], t).then_inc(x1_ok, 1)
            for i in range(11):
                dve.wait_ge(st_mm, i + 1)
                nc.vector.tensor_copy(st_t[:, 4 * i:4 * i + 4, :],
                                      bk(6 + i % 2)[:, 0:64].rearrange("p (f r) -> p f r", f=4)).then_inc(st_ok, 1)
            for q in range(8, 12):
                high_of_piece(q)
            modulate(h2_mm, h2_d, False, 24, 32)
            dve.wait_ge(h2_mm, 9)
            dve.wait_ge(h2_d, 5)
            dve.wait_ge(spilled, 16 * (TP + 1))
            for k in range(KT_D):
                if k % 2:
                    dve.wait_ge(h2_a, k // 2 + 1)
                split_ht(k, ht_high_r)

            for k in range(2 * FT):
                f = k // 2 + FT * (k % 2)
                tap = lambda j: vec_t[:, 1, 44 * j + f:44 * j + f + 1]
                c_p, c_sm = cv[:, k % 2, 0:SEQ], cv[:, k % 2, SEQ:NT].rearrange("p (b s) -> p b s", b=DB)
                high_of_piece(12 + k)
                dve.wait_ge(up_c0, k + 1)
                then(nc.vector.scalar_tensor_tensor(out=c_p, in0=u_b[:, k % 2, 1:1 + SEQ], scalar=tap(1), in1=c_p,
                                                    op0=ALU.mult, op1=ALU.add))
                nc.vector.scalar_tensor_tensor(out=c_p, in0=u_b[:, k % 2, 0:SEQ], scalar=tap(0), in1=c_p,
                                               op0=ALU.mult, op1=ALU.add)
                dve.wait_ge(up_x, k + 1)
                then(nc.vector.scalar_tensor_tensor(out=c_sm, in0=ext[:, k % 2, :, 1:1 + DS], scalar=tap(1), in1=c_sm,
                                                    op0=ALU.mult, op1=ALU.add))
                nc.vector.scalar_tensor_tensor(out=c_sm, in0=ext[:, k % 2, :, 0:DS], scalar=tap(0), in1=c_sm,
                                               op0=ALU.mult, op1=ALU.add).then_inc(up_cv, 1)
                if k % 2 == 1:
                    dve.wait_ge(up_ge, k // 2 + 1)
                    dve.wait_ge(up_cv, k + 1)
                    nc.vector.tensor_tensor(gt[:, k // 2, :], ga[:, (k // 2) % 2, :], cv[:, 1, :], ALU.mult).then_inc(up_gt, 1)

            def split_gated(z):
                f, b = z % FT, z % NG_BUF
                if z >= NG_BUF:
                    dve.wait_ge(g_used, z - NG_BUF + 1)
                then(nc.vector.tensor_copy(g_high_r[:, b, :], gt[:, f, :]))
                nc.vector.tensor_tensor(g_rest_r[:, b, :], gt[:, f, :], g_high_r[:, b, :].bitcast(F32), ALU.subtract)\
                    .then_inc(g_split, 1)

            def add_half(half, t):
                rows, kind = (P, 0) if t < TP else (NS, 1)
                cols = slice(CH * half, CH * half + CH)
                j = (TP + 1) * half + t
                dve.wait_ge(dn_mm, j + 1)
                nc.vector.tensor_tensor(y3[0:rows], bk(j % 8)[0:rows], gate2[0:rows, kind, cols], ALU.mult).then_inc(dn_d, 1)
                dve.wait_ge(dn_d, j + 1)
                x = x_sb[0:rows, t, cols]
                then(nc.vector.tensor_tensor(x, x, y3[0:rows], ALU.add))

            dve.wait_ge(up_gt, FT)
            for z in range(NG_BUF):
                split_gated(z)
            q = 12 + 2 * FT
            starts = [FT * half + 8 * kg for half in range(2) for kg in range(3)][1:]
            piece_at = {z: sum(n == CHUNK_AT[("down", 1 + i)] for n, k in PIECES) for i, z in enumerate(starts)}
            dve.wait_ge(ln2_in, 48)
            dve.wait_ge(gb_a, 8)
            dve.wait_ge(x1_back, 32)
            pre = []
            for t in range(TP + 1):
                pre += [(0, t), (1, t)]
            for z in range(NG_BUF, 2 * FT):
                split_gated(z)
                for _ in range(min(2, piece_at.get(z, 0))):
                    high_of_piece(q)
                    q += 1
                for _ in range(max(0, piece_at.get(z - 1, 0) - 2)):
                    high_of_piece(q)
                    q += 1
                if pre:
                    half, t = pre.pop(0)
                    rows, kind = (P, 0) if t < TP else (NS, 1)
                    cols = slice(CH * half, CH * half + CH)
                    then(nc.vector.tensor_tensor(y3[0:rows], gate2[0:rows, kind, cols], ln2[0:rows, 0, cols], ALU.mult))
                    x = x_sb[0:rows, t, cols]
                    then(nc.vector.scalar_tensor_tensor(out=x, in0=x, scalar=ALPHA, in1=y3[0:rows], op0=ALU.mult, op1=ALU.add))
                if z == FT + NG_BUF - 1:
                    add_half(0, 0)
                    add_half(0, 1)
                elif FT + NG_BUF <= z < FT + NG_BUF + TP - 1:
                    add_half(0, z - FT - NG_BUF + 2)
            for t in range(TP + 1):
                add_half(1, t)
                norm(t, P if t < TP else NS, ln2[:, 1, :], ln2[:, 2, :], TP + 1 + t).then_inc(y_out, 1)

        @block.tensor
        def _(pe):
            def landed(n):
                pe.wait_ge(w_in_slot[SLOT_OF[n]], slot_count(n))

            pe.wait_ge(early, 16 * 15)
            for r, k in enumerate((93, 88, 88)):
                last = nc.tensor.transpose(bk(0)[:, P * r:P * r + k], vec_r[0:k, r, :], ident[0:k, 0:k])
            last.then_inc(vecs_t, 1)
            pe.wait_ge(c_cp, 1)
            for k in range(KT_D):
                last = nc.tensor.transpose(bk(1)[:, 16 * k:16 * k + C], c_s[:, P * k:P * k + P], ident[0:C, 0:C])
            last.then_inc(c_tr, 1)

            def ada(ch):
                n = CHUNK_AT[("ada", ch)]
                landed(n)
                if ch:
                    pe.wait_ge(ada_ms, ch)
                for k in range(KT_D):
                    j = k % 4
                    last = nc.tensor.matmul(bk(6)[32 * j:32 * j + C, :], c_t[:, k, :], slot(SLOT_OF[n])[:, k, :],
                                            start=(k < 4), stop=(k >= 4))
                last.then_inc(ada_mm, 1)
                pe.wait_ge(ada_mm, ch + 1)
                pe.wait_ge(ada_ms, ch + 1)
                pe.sem_inc(w_used, 1)
                if ch:
                    pe.wait_ge(ada_ok, ch)
                for c in range(4):
                    last = nc.tensor.matmul(bk(7)[:, 16 * c:16 * c + C], mod_s[:, ch % 2, P * c:P * c + P], sum9[:, :],
                                            start=True, stop=True)
                last.then_inc(ada_tt, 1)

            pe.wait_ge(bank6_zero, 1)
            pe.wait_ge(c_cp, 2)
            for ch in range(4):
                ada(ch)

            def turn_x(mm, taken_d, taken_a):
                for f in range(KT_D):
                    last = nc.tensor.transpose(bk(4)[:, NS * f:NS * f + NS], x_sb[0:NS, TP, P * f:P * f + P], ident[0:NS, 0:NS])
                last.then_inc(mm, 1)
                for f in range(KT_D):
                    if f >= 4:
                        if f % 2 == 0:
                            pe.wait_ge(taken_d, (f - 4) // 2 + 2)
                        else:
                            pe.wait_ge(taken_a, (f - 4) // 2 + 1)
                    for t in range(TP):
                        last = nc.tensor.transpose(bk(f % 4)[:, P * t:P * t + P], x_sb[:, t, P * f:P * f + P], ident[:, :])
                    last.then_inc(mm, 1)

            pe.wait_ge(x_in, 32)
            turn_x(xt_mm, xt_d, xt_a)
            pe.wait_ge(xt_d, 5)
            pe.wait_ge(xt_a, 4)

            def product(out, left, right, first, last):
                nc.tensor.matmul(out, left[0], right[0], start=first, stop=False)
                nc.tensor.matmul(out, left[0], right[1], start=False, stop=False)
                return nc.tensor.matmul(out, left[1], right[0], start=False, stop=last)

            for n in range(len(units) + 3):
                if n < len(units):
                    s, t = units[n]
                    ch = CHUNK_AT[("in", s)]
                    if n >= 4:
                        if n - 4 in rope_units:
                            pe.wait_ge(pj_d, d_units(n - 4))
                        else:
                            pe.wait_ge(pj_a, a_units(n - 4))
                    rows = P if t < TP else NS
                    for k in range(KT_D):
                        if t == 0:
                            if k % 2 == 0:
                                pe.wait_ge(win_pool, 4 * s + k // 2 + 1)
                            else:
                                pe.wait_ge(win_dve, 4 * s + k // 2 + 1)
                        if n == 0:
                            pe.wait_ge(ht_rest, k + 1)
                        cols = slice(P * t, P * t + rows)
                        last = product(bk(n % 4)[0:rows, :], (ht_high_r[:, k, cols], ht_r[:, k, cols]),
                                       pair_of(ch, k), k == 0, k == KT_D - 1)
                        if t == TP and k < KT_D - 1:
                            last.then_inc(win_free, 1)
                    last.then_inc(pj_mm, 1)
                    if t == TP:
                        pe.wait_ge(pj_mm, n + 1)
                        pe.sem_inc(win_free, 1)
                        pe.sem_inc(w_used, 1)
                if (n - 2) in tr_units:
                    s, t = units[n - 2]
                    k = tr_units.index(n - 2)
                    r = rope_units.index(n - 2)
                    pe.wait_ge(rope_ok, r + 1)
                    if k >= 2:
                        s2, t2 = units[tr_units[k - 2]]
                        by_act = [x for x in tr_units[:k - 1] if units[x][0] in (0, 3) and units[x][1] < TP]
                        if s2 in (0, 3) and t2 < TP:
                            pe.wait_ge(qk_a, len(by_act))
                        else:
                            pe.wait_ge(qk_d, k - 1 - len(by_act))
                    rows = P if t < TP else NS
                    for f in range(4):
                        last = nc.tensor.transpose(bk(4 + k % 2)[:, rows * f:rows * f + rows],
                                                   stage[0:rows, r % 4, P * f:P * f + P], ident[0:rows, 0:rows])
                    last.then_inc(qk_t, 1)

            pe.wait_ge(qk_a, 2 * TP)
            pe.wait_ge(qk_d, len(tr_units) - 2 * TP)
            pe.wait_ge(pj_a, len(v_units))
            pe.wait_ge(pj_d, len(rope_units))
            for s in range(NU + 3):
                if s < NU:
                    m, n, qb = pa[s]
                    w = P * (qb + 1)
                    if s >= 2:
                        pe.wait_ge(pa_min, s - 1)
                    nc.tensor.matmul(bk(s % 2)[:, 0:w], qtp[:, 8 * m + n, P * qb:P * qb + P], kt[:, 4 * m + n // 2, 0:w],
                                     start=True, stop=True).then_inc(pa_s, 1)
                if 0 <= (x := s - 2) < NU:
                    pe.wait_ge(pa_exp, x + 1)
                    if x >= 2:
                        pe.wait_ge(pa_pt, x - 1)
                    for kb in range(pa[x][2] + 1):
                        last = nc.tensor.transpose(bk(2 + x % 2)[:, P * kb:P * kb + P], p_b[:, x % 2, P * kb:P * kb + P], ident[:, :])
                    last.then_inc(pa_t, 1)
                if 0 <= (x := s - 3) < NU:
                    m, n, qb = pa[x]
                    pe.wait_ge(pa_pt, x + 1)
                    if x >= 2:
                        pe.wait_ge(pa_o, x - 1)
                    for kb in range(qb + 1):
                        last = nc.tensor.matmul(bk(4 + x % 2)[:, 0:P], pt_b[:, x % 2, P * kb:P * kb + P],
                                                vp[:, kb, m, P * (n // 2):P * (n // 2) + P], start=(kb == 0), stop=(kb == qb))
                    last.then_inc(pa_pv, 1)
                if s < NU and s % 8 == 7:
                    ada(4 + s // 8)

            pe.wait_ge(pa_min, NU)
            pe.wait_ge(pa_o, NU)
            pe.wait_ge(ada_ok, 12)
            def score(w, h, keys, at, nk):
                for d in range(2):
                    for nn in range(4):
                        g = 2 * (4 * h + nn) + d
                        last = nc.tensor.matmul(wide[h][32 * nn:32 * nn + 32, at:at + nk],
                                                qbd[:, w % 2, g].rearrange("p i q -> p (i q)"), keys[:, g, 0:nk],
                                                start=(d == 0), stop=(d == 1), skip_group_check=True)
                return last

            def score_group(w, g):
                m, b = sa[w]
                G = NG[w] + g
                if g == 0:
                    pe.wait_ge(q_bd, w + 1)
                    if w >= 1:
                        pe.wait_ge(sa_min, w)
                        pe.wait_ge(sa_exp, 2 * w)
                pe.wait_ge(kg_t, G + 1)
                score(w, 0, ktg[:, G % NK], P * g, 32 * groups[m][g])
                score(w, 1, ktg[:, G % NK], P * g, 32 * groups[m][g]).then_inc(sa_g, 1)

            def score_new(w):
                n = 32 * sum(groups[sa[w][0]])
                pe.wait_ge(kn_t, w + 1)
                score(w, 0, ktn[:, w % 2], n, 32)
                score(w, 1, ktn[:, w % 2], n, 32).then_inc(sa_s, 1)

            def weigh_group(w, g):
                m, b = sa[w]
                G = NG[w] + g
                pe.wait_ge(vg_in[G % NV], v_count(m, w, g))
                k = 32 * groups[m][g]
                for i in range(4):
                    for j in range(4):
                        at = P * g + 32 * i + 16 * (j % 2)
                        last = nc.tensor.matmul(bk(6)[32 * j:32 * j + 16, 0:P], pt_s[0:k, j // 2, at:at + 16],
                                                vg[0:k, G % NV, i, P * j:P * j + P], start=(g == 0 and i == 0),
                                                stop=False, skip_group_check=True)
                last.then_inc(sa_vg, 1)

            for g in range(len(groups[0])):
                score_group(0, g)
            score_new(0)
            for w, (m, b) in enumerate(sa):
                n = 32 * sum(groups[m])
                for h in range(2):
                    pe.wait_ge(sa_exp, 2 * w + h + 1)
                    if w >= 1:
                        pe.wait_ge(sa_pt, 3 * w)
                    for u in range((n + P - 1) // P):
                        k = min(P, n - P * u)
                        nc.tensor.transpose(bk(4 + h)[0:k, P * u:P * u + P], p_s[:, h, P * u:P * u + k], perm[:, :])
                    nc.tensor.transpose(bk(7)[0:32, P * h:P * h + P], p_s[:, h, n:n + 32], perm[:, :]).then_inc(sa_t, 1)
                nxt = groups[sa[w + 1][0]] if w + 1 < len(sa) else []
                for g in range(4):
                    if g < len(nxt):
                        score_group(w + 1, g)
                    if g == 0:
                        pe.wait_ge(sa_pt, 3 * w + 3)
                        if w >= 1:
                            pe.wait_ge(sa_o, w)
                    if g < len(groups[m]):
                        weigh_group(w, g)
                pe.wait_ge(new_in[w % 2], 32 * (w // 2 + 1))
                for j in range(4):
                    at = 16 * (j % 2)
                    last = nc.tensor.matmul(bk(6)[32 * j:32 * j + 16, 0:P], ptn[0:DS, j // 2, at:at + 16],
                                            vn[0:DS, w % 2, P * j:P * j + P], start=False, stop=True, skip_group_check=True)
                last.then_inc(sa_pv, 1)
                if nxt:
                    score_new(w + 1)
            pe.wait_ge(sa_exp, 32)
            for h in range(2):
                last = nc.tensor.matmul(bk(0)[:, 0:16], sums[:, h, :], rs_s[:, h, :], start=(h == 0), stop=(h == 1))
            last.then_inc(sa_l, 1)
            pe.wait_ge(sa_n, 1)
            for w, (m, b) in enumerate(sa):
                last = nc.tensor.matmul(bk(1 + m)[:, 32 * b:32 * b + 32], o_s[:, w, :], pick[:, :], start=True, stop=True)
            last.then_inc(sa_x, 1)
            pe.wait_ge(sa_n, 2)
            nc.tensor.matmul(bk(3)[:, 0:256], ones[:, :], ob_q, start=True, stop=True).then_inc(sa_sq, 1)

            pe.wait_ge(sa_fin, 2)
            pe.wait_ge(rms_ok, 1)
            for f in range(KT_D):
                if f >= 4:
                    pe.wait_ge(mt_d, f - 2)
                for t in range(TP):
                    last = nc.tensor.transpose(bk(f % 4)[:, P * t:P * t + P], mixv[:, t, P * f:P * f + P], ident[:, :])
                last.then_inc(mt_mm, 1)
            pe.wait_ge(mt_d, 9)
            for j in range(8):
                which, kind, half = j // 4, (j // 2) % 2, j % 2
                rows = P if kind == 0 else NS
                if j >= 2:
                    pe.wait_ge(gb_a, j - 1)
                for c in range(4):
                    f = 4 * half + c
                    col = mod_t[:, (16, 40)[which] + f, 0:1].to_broadcast([P, P]) if kind == 0 else \
                        gexp[:, 8 * which + f].rearrange("p b s -> p (b s)")
                    last = nc.tensor.matmul(bk(4 + j % 2)[0:rows, P * c:P * c + P], col, ident[:, :], start=True, stop=True)
                last.then_inc(gb_mm, 1)
            for j in range(2 * (TP + 1)):
                t, half = divmod(j, 2)
                rows = P if t < TP else NS
                n = CHUNK_AT[("o", half)]
                if j >= 4:
                    pe.wait_ge(wo_d, j - 3)
                for k in range(KT_D):
                    if t == 0 and k % 2 == 0:
                        pe.wait_ge(wl_rest, 4 * half + k // 2 + 1)
                    if j == 0:
                        pe.wait_ge(ht_rest, KT_D + k + 1)
                    cols = slice(P * t, P * t + rows)
                    last = product(bk(j % 4)[0:rows, :], (mt_high_r[:, k, cols], ht_r[:, k, cols]),
                                   pair_of(n, k), k == 0, k == KT_D - 1)
                last.then_inc(wo_mm, 1)
            pe.wait_ge(wo_mm, 2 * TP + 2)
            pe.sem_inc(w_used, 2)
            pe.wait_ge(st_in, 16)
            pe.wait_ge(wo_d, 2 * TP + 2)
            for i in range(11):
                if i >= 2:
                    pe.wait_ge(st_ok, i - 1)
                for c in range(4):
                    last = nc.tensor.transpose(bk(6 + i % 2)[:, 16 * c:16 * c + 16], st_r[:, 512 * i + P * c:512 * i + P * c + P],
                                               ident[0:16, 0:16])
                last.then_inc(st_mm, 1)
            pe.wait_ge(x1_ok, TP + 1)
            turn_x(h2_mm, h2_d, h2_a)
            pe.wait_ge(h2_d, 5)
            pe.wait_ge(h2_a, 4)
            for k in range(2 * FT):
                f, g = divmod(k, 2)
                n = CHUNK_AT[("up", f // 2)]
                if k >= 3:
                    pe.wait_ge(up_u, k - 2)
                at = 256 * g + P * (f % 2)
                for kk in range(KT_D):
                    if k % 4 == 0 and kk % 2 == 0:
                        pe.wait_ge(wl_rest, 8 + k + kk // 2 + 1)
                    if k == 0:
                        pe.wait_ge(ht_rest, 2 * KT_D + kk + 1)
                    for h in range(2):
                        cols = slice(HALF_NT * h, HALF_NT * h + HALF_NT)
                        last = product(up_bank(k)[:, h, :], pair_of(n, kk, slice(at, at + P)),
                                       (ht_high_r[:, kk, cols], ht_r[:, kk, cols]), kk == 0, kk == KT_D - 1)
                last.then_inc(up_mm, 1)
                if k % 4 == 3:
                    pe.wait_ge(up_mm, k + 1)
                    pe.sem_inc(w_used, 1)
            for i in range(11):
                if i == 0:
                    pe.wait_ge(up_x, 2 * FT)
                if i >= 2:
                    pe.wait_ge(us_a, i - 1)
                for c in range(4):
                    last = nc.tensor.transpose(bk(6 + i % 2)[0:18, P * c:P * c + P], u_last[:, 4 * i + c, :], ident[:, :])
                last.then_inc(us_mm, 1)
            pe.wait_ge(up_gt, FT)
            pe.wait_ge(up_u, 2 * FT)
            pe.wait_ge(us_a, 11)
            for half in range(2):
                steps = [(f, t) for f in range(16) for t in range(TP + 1)]
                if half == 0:
                    steps += [(f, t) for f in range(16, FT) for t in range(TP + 1)]
                else:
                    steps += [(f, t) for t in range(TP + 1) for f in range(16, FT)]
                for f, t in steps:
                    n = CHUNK_AT[("down", 3 * half + f // 8)]
                    z, j = FT * half + f, (TP + 1) * half + t
                    if t == 0:
                        if f == 0 and half == 0:
                            pe.wait_ge(us_mm, 11)
                        pe.wait_ge(g_split, z + 1)
                        pe.wait_ge(wl_rest, pieces_through(n - 1) + (f % 8) // 2 + 1)
                    if f == 0 and j >= 8:
                        pe.wait_ge(dn_d, j - 7)
                    rows = P if t < TP else NS
                    cols = slice(P * t, P * t + rows)
                    last = product(bk(j % 8)[0:rows, :], (g_high_r[:, z % NG_BUF, cols], g_rest_r[:, z % NG_BUF, cols]),
                                   pair_of(n, f % 8), f == 0, f == FT - 1)
                    if f == FT - 1:
                        last.then_inc(dn_mm, 1)
                    elif t == TP:
                        last.then_inc(g_used, 1)
                if half == 0:
                    pe.wait_ge(dn_mm, TP + 1)
                    pe.sem_inc(g_used, 1)


def constants():
    import numpy as np

    f32 = np.float32
    c = {"ident": np.eye(P, dtype=f32), "ones": np.ones((P, P), f32)}
    half = 32
    inv = (f32(1.0) / (f32(10000.0) ** (np.arange(half, dtype=f32) / f32(half)))).astype(f32)
    pos = np.zeros((TP + 1, P), f32)
    pos[:TP] = np.arange(SEQ).reshape(TP, P)
    pos[TP, :NS] = PAST + np.arange(NS) % DS
    ang = (pos[:, :, None] * inv).astype(f32)
    cos, sin = np.cos(ang), np.sin(ang)
    k_tab = np.concatenate([cos, cos, -sin, sin], -1)
    c["rope"] = np.stack([k_tab * f32(-0.125), k_tab], 2).transpose(1, 0, 2, 3).astype(f32).copy()

    def penalty(dist):
        n = sum(((dist >= 0) & (dist <= w) & (dist % d == 0)).astype(int) for w, d in ((128, 1), (512, 4), (2048, 16)))
        return np.where(n > 0, -np.log(np.maximum(n, 1)), BIG).astype(f32)

    dist = np.arange(P)[:, None] + (SEQ - P) - np.arange(SEQ)[None, :]
    c["maskt"] = np.stack([penalty(dist), np.where(dist >= 0, 0, BIG).astype(f32)], 1)
    i = (np.arange(P) // 8) % 4
    q = np.arange(P) % 8
    m = np.arange(32)
    cols = [16 * (32 * i[:, None] + m) + t for t in range(8)] + [16 * (96 + m[None, :]) + 8 + 4 * x + i[:, None] for x in range(2)]
    sm = np.concatenate([penalty(PAST + q[:, None] - k) for k in cols], 1)
    here = (i[:, None] == 0) & (m[None, :] < DS) & (m[None, :] <= q[:, None])
    c["smask"] = np.concatenate([sm, np.where(here, penalty(q[:, None] - m[None, :]), f32(BIG)),
                                 np.where(here, f32(0), f32(BIG))], 1).astype(f32)
    sums = np.zeros((2, P, P), f32)
    for h in range(2):
        for r in range(P):
            for out in range(P):
                j, n2 = out // 32, min((out % 32) // 8, 1)
                sums[h, r, out] = 4 * h + r // 32 == 2 * j + n2 and r % 8 == out % 8
    c["sums"] = sums.transpose(1, 0, 2).copy()
    r = np.arange(P)
    c["pick"] = ((r[:, None] // 32 == np.arange(32)[None, :] // 8) & (r[:, None] % 8 == np.arange(32)[None, :] % 8)
                 & (r[:, None] % 32 < 16)).astype(f32)
    c["colmask"] = ((np.arange(P)[None, :] // 64) == ((r[:, None] % 32) // 8)).astype(f32)
    c["sum9"] = (r[:, None] % 32 == np.arange(C)[None, :]).astype(f32)
    c["diff_c"] = np.stack([(r % 32 // 8 != 1), (r % 32 // 8 == 1)], 1).astype(f32)
    perm = np.zeros((P, P), f32)
    for n in range(4):
        for i_ in range(4):
            for q_ in range(8):
                perm[32 * n + 8 * i_ + q_, 32 * i_ + 8 * n + q_] = 1
    c["perm"] = perm
    return c


_OUTS = [("yp", (1, SEQ, D)), ("ys", (DB, DS, D)),
         ("wkp", (1, 1, SEQ, 8, 64)), ("wvp", (1, 1, SEQ, 8, 64)),
         ("wks", (1, DB, PAST, 8, 64)), ("wvs", (1, DB, PAST, 8, 64)),
         ("kkp", (1, 1, SEQ, 4, 128)), ("kvp", (1, 1, SEQ, 4, 128)),
         ("kks", (1, DB, DS, 4, 128)), ("kvs", (1, DB, DS, 4, 128)),
         ("cp", (1, 1, 2, 2 * DFF)), ("cs", (1, DB, 2, 2 * DFF))]


def kernel(**inputs):
    import numpy as _np
    import concourse.bacc as _bacc
    from concourse.bass_utils import run_bass_kernel_spmd as _run

    nc = _bacc.Bacc("TRN2", target_bir_lowering=False, num_devices=1, dynamic_dma_scratch_size=1024)
    arrays, ins, outs = {}, {}, {}
    for name, value in {**inputs, **constants()}.items():
        value = _np.ascontiguousarray(value)
        arrays[f"in_{name}"] = value
        ins[name] = nc.dram_tensor(f"in_{name}", value.shape, mybir.dt.from_np(value.dtype), kind="ExternalInput").ap()
    for name, shape in _OUTS:
        outs[name] = nc.dram_tensor(f"out_{name}", shape, F32, kind="ExternalOutput").ap()
    spill = nc.dram_tensor("x1_spill", (NT, D), F32).ap()
    build(nc, ins, outs, spill)
    r = _run(nc, [arrays], core_ids=[0])
    return tuple(r.results[0][f"out_{name}"] for name, _ in _OUTS)
```

```python
from contextlib import ExitStack

import concourse.bass as bass
from concourse import mybir

P = 128
F32 = mybir.dt.float32
F32R = mybir.dt.float32r
I32 = mybir.dt.int32
ALU = mybir.AluOpType
ACT = mybir.ActivationFunctionType
AX_X = mybir.AxisListType.X

D = 1024
KT_D = D // P
SEQ = 512
TP = SEQ // P
DB, DS = 8, 8
NS = DB * DS
NT = SEQ + NS
HALF_NT = NT // 2
PAST = 2048
PAGE = 128
N_PAGES = PAST // PAGE
WID = 512
MAPS = 8
DFF = 2816
FT = DFF // P
CH = 512
N_SLOTS = 4
SLOT = KT_D * CH
NEG = 3.0e38
BIG = 1.0e30
EPS = 1e-5
ALPHA = 2.0 ** 0.25
LAM_INIT = 0.2
C = 1 + DB
A_TILES = 10
B_TILES = N_PAGES

CHUNKS = [("ada", i) for i in range(4)] + [("in", i) for i in range(6)] + [("ada", i) for i in range(4, 12)] \
    + [("o", i) for i in range(2)] + [("up", i) for i in range(11)] + [("down", i) for i in range(6)]
SLOT_OF = [0, 1, 2, 3] + [0, 1] * 3 + [0, 1, 2, 0, 1, 2, 0, 1] + [i % 2 for i in range(19)]
CHUNK_AT = {c: i for i, c in enumerate(CHUNKS)}


def loads_of_slot(n):
    return sum(SLOT_OF[i] == SLOT_OF[n] for i in range(n + 1))


def chunk_before(n):
    return max((i for i in range(n) if SLOT_OF[i] == SLOT_OF[n]), default=None)


FIRST_LATE = CHUNK_AT[("o", 0)]
PIECES = [(n, k) for n in range(FIRST_LATE, len(CHUNKS)) for k in range(0, 6 if CHUNKS[n] in (("down", 2), ("down", 5)) else 8, 2)]


UP0 = range(8, 12)


def piece_count(q):
    return q + 1 - sum(p <= q for p in UP0)


def first_piece(n):
    return min(q for q, (c, k) in enumerate(PIECES) if c == n)


def build(nc, a, o, spill):
    ctx = ExitStack()
    with ctx:
        def sb(name, shape, dt=F32):
            return ctx.enter_context(nc.sbuf_tensor(name, shape, dt))

        def sem(name):
            return ctx.enter_context(nc.semaphore(name))

        wide = [ctx.enter_context(nc.psum_tensor(f"wide{i}", [P, 1024], F32)) for i in range(4)]

        def bk(i):
            return wide[i // 2][:, 512 * (i % 2):512 * (i % 2) + 512]

        shared = (("ring", [P, N_SLOTS * SLOT]), ("x_sb", [P, TP + 1, D]), ("ht", [P, KT_D, NT]), ("room", [P, 19712]))
        with ExitStack() as once:
            ring, x_sb, ht, room = (once.enter_context(nc.sbuf_tensor(name, shape, F32)) for name, shape in shared)
        ring_r, x_r, ht_r, room_r = (sb(name + "_r", shape, F32R) for name, shape in shared)
        mix = sb("mix", [P, TP * D])
        ident = sb("ident", [P, P])
        perm = sb("perm", [P, P])
        maskt = sb("maskt", [P, 2, SEQ])
        smask = sb("smask", [P, 384])
        sums = sb("sums", [P, 2, P])
        pick = sb("pick", [P, 32])
        colmask = sb("colmask", [P, P])
        sum9 = sb("sum9", [P, C])
        ones = sb("ones", [P, P])
        diff_c = sb("diff_c", [P, 2])
        vec_t = sb("vec_t", [P, 3, P])
        bada = sb("bada", [P, 48])
        mod_t = sb("mod_t", [P, 48, C])
        c_t = sb("c_t", [P, KT_D, C])
        lam_s = sb("lam_s", [P, 8])
        mn = sb("mn", [P, 64])
        rs = sb("rs", [P, 64])
        rcp = sb("rcp", [P, 64])
        rms = sb("rms", [P, 3, 16])
        pages = sb("pages", [1, DB * N_PAGES], I32)
        stat = sb("stat", [P, 2, 6])
        mv = sb("mv", [P, 4])
        g8 = sb("g8", [P, 1])
        stat2 = sb("stat2", [P, TP + 1, 2, 6])
        mv2 = sb("mv2", [P, TP + 1, 6])

        def slot(i, t=ring):
            return t[:, i * SLOT:(i + 1) * SLOT].rearrange("p (k n) -> p k n", k=KT_D)

        def part(t, at, n):
            return t[:, at:at + n]

        def pair_of(n, k, cols=slice(0, CH)):
            high = slot(2 if n < FIRST_LATE else 2 + SLOT_OF[n], ring_r)
            return high[:, k, cols], slot(SLOT_OF[n], ring_r)[:, k, cols]

        vec_r = room[:, 0:3 * P].rearrange("p (r d) -> p r d", r=3)
        c_r = room[0:C, 512:512 + D]
        c_e = part(room, 1536, KT_D * C).rearrange("p (k r) -> p k r", k=KT_D)
        lam4 = part(room, 3584, 256).rearrange("p (n d) -> p n d", n=4)
        mod_s = ht[:, :, :].rearrange("p k t -> p (k t)")[:, 6 * NT:6 * NT + 2 * CH].rearrange("p (b n) -> p b n", b=2)
        qtp = part(room, 0, 8192).rearrange("p (n t) -> p n t", n=16)
        kt = part(room, 8192, 4096).rearrange("p (f t) -> p f t", f=8)
        vp = part(room, 12288, 4096).rearrange("p (m t d) -> p t m d", t=TP, m=2)
        tmp_a = part(room, 16384, 1024).rearrange("p (b n) -> p b n", b=2)
        tmp_b = part(room, 17408, 1024).rearrange("p (b n) -> p b n", b=2)
        rope = part(room, 18432, 1280).rearrange("p (t w n) -> p t w n", t=TP + 1, w=2)
        s_m = part(room, 16384, 1024).rearrange("p (b n) -> p b n", b=2)
        p_b = part(room, 17408, 1024).rearrange("p (b n) -> p b n", b=2)
        pt_b = part(room, 18432, 1024).rearrange("p (b n) -> p b n", b=2)
        o_1 = part(room, 19456, 128)
        sq_b = part(room, 19584, 128)
        ht_high_r = x_r[:, :, :].rearrange("p t d -> p (t d)")[:, 0:KT_D * NT].rearrange("p (k t) -> p k t", k=KT_D)
        mt_high_r = part(room_r, 5120, KT_D * NT).rearrange("p (k t) -> p k t", k=KT_D)
        stage = mix[:, 0:2048].rearrange("p (b n) -> p b n", b=4)
        mixv = mix[:, :].rearrange("p (t d) -> p t d", t=TP)
        keep = 3 * SLOT
        qrep = part(ring, keep, 2048).rearrange("p (m g t) -> p m g t", m=2, g=16)
        k_s = ring[0:NS, keep + 2048:keep + 3072].rearrange("p (m d) -> p m d", m=2)
        v_s = ring[0:NS, keep + 3072:keep + 4096].rearrange("p (m d) -> p m d", m=2)
        NK, NV = 3, 4
        kraw = [part(ring, at, 2048).rearrange("p (t d) -> p t d", t=4) for at in (4 * 2048, 5 * 2048, 3 * 2048)]
        ktg = part(ring, 0, NK * 2048).rearrange("p (b g n) -> p b g n", b=NK, g=16)
        x_flat = x_sb[:, :, :].rearrange("p t d -> p (t d)")
        ht_flat = ht[:, :, :].rearrange("p k t -> p (k t)")
        vg = [part(t, at, 2048).rearrange("p (i d) -> p i d", i=4)
              for t, at in ((x_flat, 0), (x_flat, 2048), (room, 0), (room, 2048))]
        qbd = part(x_flat, 4096, 1024).rearrange("p (b g i q) -> p b g i q", b=2, g=16, i=4)
        kn = part(room, 8192, 1024).rearrange("p (b d) -> p b d", b=2)
        ktn = part(room, 9216, 1024).rearrange("p (b g n) -> p b g n", b=2, g=16)
        o_s = part(room, 12288, 2048).rearrange("p (w d) -> p w d", w=16)
        vn = part(ht_flat, 0, 1024).rearrange("p (b d) -> p b d", b=2)
        p_s = part(ht_flat, 1024, 1088).rearrange("p (b n) -> p b n", b=2)
        pt_s = part(ht_flat, 2112, 1024).rearrange("p (b n) -> p b n", b=2)
        sm_s = part(ht_flat, 3136, 640).rearrange("p (b n) -> p b n", b=2)
        sm_n = part(ht_flat, 3776, 64).rearrange("p (b n) -> p b n", b=2)
        ptn = part(ht_flat, 3840, 256).rearrange("p (b n) -> p b n", b=2)
        small = maskt[:, 0, 0:256]
        blk = small[:, 0:32]
        blk_t = small[:, 32:64]
        blk_r = small[:, 64:96]
        blk_o = small[:, 96:128]
        rs_s = small[:, 128:160].rearrange("p (h w) -> p h w", h=2)
        l_s = small[:, 160:176]
        rs_n = small[:, 192:224].rearrange("p (h w) -> p h w", h=2)
        ob_t = part(room, 0, 256)
        ob_q = part(room, 256, 256)
        ob_r = part(room, 512, 256)
        gate = mix[:, 0:2048].rearrange("p (s d) -> p s d", s=2)
        gate2 = mix[:, 2048:4096].rearrange("p (s d) -> p s d", s=2)
        ln1 = part(room, 1024, 2048).rearrange("p (w d) -> p w d", w=2)
        y_sb = part(room, 3072, 2048).rearrange("p (b d) -> p b d", b=2)
        st_r = room[0:16, 12672:12672 + 2 * DFF]
        ln2 = part(room, 12672, 3072).rearrange("p (w d) -> p w d", w=3)
        gt = part(room, 0, FT * NT).rearrange("p (f t) -> p f t", f=FT)
        u_b = part(room, 15744, 2 * (NT + 2)).rearrange("p (b n) -> p b n", b=2)
        cv = part(room, 16900, 2 * NT).rearrange("p (b n) -> p b n", b=2)
        ga = part(room, 18052, 2 * NT).rearrange("p (b n) -> p b n", b=2)
        ext = part(room, 19204, 160).rearrange("p (b s t) -> p b s t", b=2, s=DB)
        st_t = maskt[:, :, :].rearrange("p m t -> p (m t)")[:, 0:704].rearrange("p (f r) -> p f r", f=2 * FT)
        u_last = mix[:, 704:704 + 792].rearrange("p (f r) -> p f r", f=2 * FT)
        NG_BUF = 6
        g_high_r = ht_r[:, :, :].rearrange("p k t -> p (k t)")[:, 0:NG_BUF * NT].rearrange("p (b t) -> p b t", b=NG_BUF)
        g_rest_r = [part(ht_r[:, :, :].rearrange("p k t -> p (k t)"), (NG_BUF + b) * NT, NT) for b in range(2)] \
            + [part(room_r, 15744 + b * NT, NT) for b in range(NG_BUF - 2)]
        y3 = part(room, 15744 + NG_BUF * NT, CH)
        gexp = part(room, 4096, 1024).rearrange("p (g b s) -> p g b s", g=16, b=DB)

        def conv_out(i):
            return mix[0:18, 0:CH] if i % 2 == 0 else mix[0:18, 1536:1536 + CH]

        c_cols = bk(1)[:, 0:P].rearrange("p (k r) -> p k r", k=KT_D)[:, :, 0:C]

        early = sem("early_loaded")
        c_in = sem("c_loaded")
        in0_high = sem("w_in_first_chunk_high")
        lam_dot = sem("lambda_dots")
        tables = sem("tables_loaded")
        rope_in = sem("rope_loaded")
        x_in = sem("x_loaded")
        w_in_slot = [sem(f"w_loaded_{i}") for i in range(N_SLOTS)]
        w_used = sem("w_used")
        vecs_t = sem("vecs_transposed")
        vecs_c = sem("vecs_copied")
        act_setup = sem("act_setup")
        dve_seq = sem("dve_seq")
        c_tr = sem("c_transposed")
        c_cp = sem("c_copied")
        bank6_zero = sem("bank6_zero")
        ada_mm = sem("ada_product")
        ada_ms = sem("ada_rows_copied")
        ada_tt = sem("ada_transposed")
        ada_ok = sem("ada_ready")
        xt_mm = sem("xt_transposed")
        xt_d = sem("xt_taken_dve")
        xt_a = sem("xt_taken_act")
        pj_mm = sem("proj_product")
        pj_d = sem("proj_taken_dve")
        pj_a = sem("proj_taken_act")
        rope_ok = sem("rope_done")
        qk_t = sem("qk_transposed")
        qk_d = sem("qk_taken_dve")
        qk_a = sem("qk_taken_act")
        qzero = sem("qtp_zeroed")
        stg = [sem(f"stage_stored_{i}") for i in range(4)]
        out_sem = sem("rows_stored")
        pa_s = sem("pa_scores")
        pa_min = sem("pa_masked")
        pa_exp = sem("pa_exp")
        pa_t = sem("pa_transposed")
        pa_pt = sem("pa_pt_copied")
        pa_pv = sem("pa_pv")
        pa_o = sem("pa_out_taken")
        rms_sq = sem("rms_sums")
        rms_rt = sem("rms_roots")
        rms_ok = sem("rms_done")
        kg_in = [sem(f"k_group_loaded_{i}") for i in range(NK)]
        vg_in = [sem(f"v_group_loaded_{i}") for i in range(NV)]
        new_in = [sem(f"new_rows_loaded_{i}") for i in range(2)]
        new_zero, qbd_zero = sem("new_zeroed"), sem("queries_zeroed")
        kg_t = sem("k_group_turned")
        kn_t = sem("k_new_turned")
        q_bd = sem("q_spread")
        sa_g = sem("sa_group_scored")
        sa_s = sem("sa_scores")
        sa_min = sem("sa_min")
        sa_exp = sem("sa_exp")
        sa_t = sem("sa_transposed")
        sa_pt = sem("sa_pt_copied")
        sa_vg = sem("sa_group_weighted")
        sa_pv = sem("sa_pv")
        sa_o = sem("sa_out_taken")
        sa_l = sem("sa_sums")
        sa_n = sem("sa_normed")
        sa_x = sem("sa_picked")
        sa_fin = sem("sa_placed")
        sa_sq = sem("sa_square_sums")
        sa_q = sem("sa_mean_squares")
        sa_r = sem("sa_roots")
        page_in = sem("pages_loaded")
        mt_mm = sem("mixed_transposed")
        mt_d = sem("mixed_taken")
        gb_mm = sem("gate_spread")
        gb_a = sem("gate_copied")
        ln_in = sem("ln_rows_loaded")
        ln2_in = sem("ln2_rows_loaded")
        wo_mm = sem("wo_product")
        wo_d = sem("wo_taken")
        n_var = sem("norm_variance")
        n_rt = sem("norm_root")
        x1_ok = sem("x1_ready")
        st_in = sem("state_loaded")
        st_mm = sem("state_transposed")
        st_ok = sem("state_ready")
        h2_mm = sem("h2_transposed")
        h2_d = sem("h2_taken_dve")
        h2_a = sem("h2_taken_act")
        up_mm = sem("up_product")
        up_u = sem("up_taken")
        up_c0 = sem("conv_started")
        up_x = sem("ext_ready")
        up_cv = sem("conv_done")
        up_ge = sem("gelu_done")
        up_gt = sem("gated")
        halo = sem("halo_zeroed")
        us_mm = sem("last_rows_transposed")
        us_a = sem("last_rows_copied")
        dn_mm = sem("down_product")
        dn_d = sem("down_taken")
        y_out = sem("y_ready")
        stored = sem("stored")
        conv_st = [sem(f"conv_state_stored_{i}") for i in range(2)]
        x_back = sem("x_reloaded")
        spilled = sem("x1_spilled")
        spilled_last = sem("x1_last_tile_spilled")
        up0_high = sem("up0_high")
        up0_dve, up0_pool = sem("up0_rest_dve"), sem("up0_rest_pool")
        x1_back = sem("x1_reloaded")
        win_high = sem("w_in_high")
        win_pool = sem("w_in_rest_pool")
        win_dve = sem("w_in_rest_dve")
        win_free = sem("w_in_slice_used")
        wl_high = sem("late_weights_high")
        wl_rest = sem("late_weights_rest")
        wo_high = sem("w_o_high")
        ht_hi = sem("ht_high")
        ht_rest = sem("ht_rest_dve")
        ht_rest_p = sem("ht_rest_pool")
        mt_rest = sem("mt_rest")
        mt_hi = sem("mixed_high")
        g_split = sem("gated_split")
        g_used = sem("gated_used")
        n2_var, n2_rt, n2_fac = sem("norm2_variance"), sem("norm2_root"), sem("norm2_factors")
        n2_scaled, n2_w = sem("norm2_scaled"), sem("norm2_weighted")
        y_last = sem("y_sample_ready")
        copied = sem("window_copied")
        pb_s, pb_min, pb_exp = sem("pb_scores"), sem("pb_masked"), sem("pb_exp")
        pb_t, pb_pt, pb_pv, pb_o = sem("pb_transposed"), sem("pb_pt_copied"), sem("pb_pv"), sem("pb_out_taken")
        sa_ph = sem("sa_pt_copied_act")
        mt_a = sem("mixed_taken_act")
        block = ctx.enter_context(nc.Block())

        WO_TILES = [0, 1, TP, 2, 3]
        st_after = {1: [0, 1], 2: [2, 3], **{j: [j + 1] for j in range(3, 10)}}
        units = [(s, t) for s in range(6) for t in range(TP + 1)]
        rope_units = [n for n, (s, t) in enumerate(units) if s in (0, 1, 3, 4)]
        v_units = [n for n, (s, t) in enumerate(units) if s in (2, 5)]
        tr_units = [n for n in rope_units if not (units[n][0] in (1, 4) and units[n][1] == TP)]
        pa = [(0, n, qb) for n in range(8) for qb in range(4)] \
            + [(1, 2 * h + c, qb) for h in range(4) for qb in range(4) for c in range(2)]
        NU = 32
        pb = pa[NU:]
        sa = [(m, b) for b in range(DB) for m in range(2)]
        groups = {0: [4, 4, 2], 1: [4, 4, 4, 4]}
        NG = [sum(len(groups[m]) for m, b in sa[:w]) for w in range(17)]

        def d_units(n):
            return sum(k in rope_units for k in range(n + 1))

        def a_units(n):
            return sum(k in v_units for k in range(n + 1))

        last_t, last_store, n_stored = [], [], [0] * 4
        user = [None] * 4
        for r, n in enumerate(rope_units):
            sec, t = units[n]
            last_t.append(None if user[r % 4] is None else tr_units.index(user[r % 4]) + 1)
            last_store.append(n_stored[r % 4])
            if not (sec in (1, 4) and t == TP):
                user[r % 4] = n
                n_stored[r % 4] += sec in (1, 4)

        def ht_high_count(phase, k):
            return 9 * phase + (6 if k is None else k + 1 if k < 5 else k + 2)

        def up_bank(k):
            return wide[k % 3][:, :].rearrange("p (h t) -> p h t", h=2)[:, :, 0:HALF_NT]

        def slot_count(n):
            return 16 * sum(2 if CHUNKS[i][0] == "up" else 1 for i in range(n + 1) if SLOT_OF[i] == SLOT_OF[n])

        def k_count(m, w, g):
            G = NG[w] + g
            return 64 * (G // NK + 1)

        def v_count(m, w, g):
            G = NG[w] + g
            return 64 * (G // NV + 1)

        flat_k = {0: a["cache_win_k"][0], 1: a["cache_k"][0]}
        flat_v = {0: a["cache_win_v"][0], 1: a["cache_v"][0]}

        def values_by_act(w, g):
            return w < len(sa) and w > 0 and (g < 2 if sa[w][0] else g == 1)

        def load_new(eng, w):
            m, b = sa[w]
            eng.dma_start(kn[0:DS, w % 2, :], k_s[DS * b:DS * b + DS, m, :]).then_inc(new_in[w % 2], 16)
            eng.dma_start(vn[0:DS, w % 2, :], v_s[DS * b:DS * b + DS, m, :]).then_inc(new_in[w % 2], 16)

        def load_values(eng, w, g):
            m, b = sa[w]
            win_v = flat_v[0][b].rearrange("(g r) h d -> g r (h d)", r=16)
            G = NG[w] + g
            vs = G % NV
            if G >= NV:
                eng.wait_ge(sa_vg, G - NV + 1)
            if m == 0 and g < 2:
                for t in range(4):
                    eng.dma_start(vg[vs][32 * t:32 * t + 32, :, :],
                                  win_v[:, 4 * g + t, :].rearrange("(i m) f -> m i f", i=4)).then_inc(vg_in[vs], 16)
            elif m == 0:
                for t in range(2):
                    eng.dma_start(vg[vs][32 * t:32 * t + 32, :, :],
                                  win_v[96:128, 8 + 4 * t:12 + 4 * t, :]).then_inc(vg_in[vs], 32)
            else:
                for t in range(4):
                    pg = eng.value_load(pages[0:1, N_PAGES * b + 4 * g + t:N_PAGES * b + 4 * g + t + 1],
                                        min_val=0, max_val=a["cache_v"].shape[1] - 1)
                    eng.dma_start(vg[vs][32 * t:32 * t + 32, :, :],
                                  flat_v[1][bass.ds(pg, 1)].rearrange("a (i m) h d -> m (a i) (h d)", i=4))\
                        .then_inc(vg_in[vs], 16)

        @block.sync
        def _(sp):
            def load_chunk(n):
                kind, i = CHUNKS[n]
                if (prev := chunk_before(n)) is not None and CHUNKS[prev][0] == "down":
                    half, kg = divmod(CHUNKS[prev][1], 3)
                    sp.wait_ge(g_used, FT * half + min(FT, 8 * kg + 8))
                elif prev is not None:
                    sp.wait_ge(w_used, prev + 1)
                if CHUNKS[n] == ("ada", 6):
                    sp.wait_ge(w_used, CHUNK_AT[("in", 5)] + 1)
                s = w_in_slot[SLOT_OF[n]]
                dst = slot(SLOT_OF[n])
                src = a[{"ada": "w_ada", "in": "w_in", "o": "w_o", "up": "w_up", "down": "w_down"}[kind]][0]
                src = src.rearrange("(k p) n -> p k n", p=P)
                if kind == "up":
                    for g in range(2):
                        sp.dma_start(dst[:, :, 256 * g:256 * g + 256],
                                     src[:, :, DFF * g + 256 * i:DFF * g + 256 * i + 256]).then_inc(s, 16)
                elif kind == "down":
                    half, kg = divmod(i, 3)
                    nk = min(8, FT - 8 * kg)
                    sp.dma_start(dst[:, 0:nk, :], src[:, 8 * kg:8 * kg + nk, CH * half:CH * half + CH]).then_inc(s, 16)
                else:
                    sp.dma_start(dst, src[:, :, CH * i:CH * i + CH]).then_inc(s, 16)

            sp.dma_start(ident[:, :], a["ident"]).then_inc(c_in, 16)
            sp.dma_start(c_r[0:1, :], a["c_prompt"]).then_inc(c_in, 16)
            sp.dma_start(c_r[1:C, :], a["c_sample"]).then_inc(c_in, 16)
            load_chunk(0)
            rows = lambda name: a[name].rearrange("l (r d) -> (l r) d", d=P)
            conv = a["w_conv"].rearrange("l j (r d) -> (l j) r d", d=P)
            sp.dma_start(vec_r[0:48, 0, :], rows("b_ada")).then_inc(early, 16)
            sp.dma_start(vec_r[48:92, 0, :], rows("b_up")).then_inc(early, 16)
            sp.dma_start(vec_r[92:93, 0, :], a["subln_g"]).then_inc(early, 16)
            sp.dma_start(vec_r[0:44, 1, :], conv[0]).then_inc(early, 16)
            sp.dma_start(vec_r[44:88, 1, :], conv[1]).then_inc(early, 16)
            sp.dma_start(vec_r[0:44, 2, :], conv[2]).then_inc(early, 16)
            sp.dma_start(vec_r[44:88, 2, :], rows("b_conv")).then_inc(early, 16)
            sp.dma_start(sum9[:, :], a["sum9"]).then_inc(early, 16)
            for i, name in enumerate(("lambda_q1", "lambda_k1", "lambda_q2", "lambda_k2")):
                sp.dma_start(lam4[:, i, :], a[name].to_broadcast([P, 64])).then_inc(early, 16)
            load_chunk(1)
            sp.dma_start(x_sb[0:NS, TP, :], a["x_sample"].rearrange("b s d -> (b s) d")).then_inc(x_in, 16)
            sp.dma_start(x_sb[:, 0:TP, :], a["x_prompt"][0].rearrange("(t p) d -> p t d", p=P)).then_inc(x_in, 16)
            load_chunk(2)
            load_chunk(3)
            load_chunk(4)
            sp.dma_start(rope, a["rope"]).then_inc(rope_in, 16)
            load_chunk(5)
            for dst, name in ((maskt, "maskt"), (smask, "smask"), (sums, "sums"), (pick, "pick"),
                              (colmask, "colmask"), (ones, "ones"), (diff_c, "diff_c"), (perm, "perm")):
                sp.dma_start(dst[:], a[name]).then_inc(tables, 16)
            sp.dma_start(pages[:, :], a["page_table"].rearrange("b n -> (b n)").rearrange("(o n) -> o n", o=1)).then_inc(page_in, 16)

            def move_window(i, names=(("cache_win_k", "wks"), ("cache_win_v", "wvs"))):
                for name, dst in names:
                    sp.dma_start(o[dst][0, i, 0:PAST - DS], a[name][0, i, DS:PAST]).then_inc(copied, 16)

            def flat(ap):
                return ap.rearrange("t h d -> t (h d)")

            sp.wait_ge(ada_ok, 4)
            move_window(0)
            n_rope = n_v = 0
            for n, (s, t) in enumerate(units):
                kb_rows = slice(P * t, P * t + P)
                if s in (0, 3):
                    n_rope += 1
                elif s in (1, 4):
                    m = s // 3
                    sp.wait_ge(rope_ok, n_rope + 1)
                    if t < TP:
                        st = n_rope % 4
                        dst = flat((o["wkp"] if m == 0 else o["kkp"])[0, 0])[kb_rows, :]
                        sp.dma_start(dst, stage[:, st, :]).then_inc(stg[st], 16)
                    else:
                        if m == 0:
                            for b in range(DB):
                                sp.dma_start(flat(o["wks"][0, b])[PAST - DS:PAST, :],
                                             k_s[DS * b:DS * b + DS, 0, :]).then_inc(out_sem, 16)
                        else:
                            sp.dma_start(o["kks"][0].rearrange("b s h d -> (b s) (h d)"), k_s[:, 1, :]).then_inc(out_sem, 16)
                    n_rope += 1
                else:
                    m = s // 3
                    n_v += 1
                    sp.wait_ge(pj_a, n_v)
                    if t < TP:
                        dst = flat((o["wvp"] if m == 0 else o["kvp"])[0, 0])[kb_rows, :]
                        sp.dma_start(dst, vp[:, t, m, :]).then_inc(out_sem, 16)
                    elif m == 0:
                        for b in range(DB):
                            sp.dma_start(flat(o["wvs"][0, b])[PAST - DS:PAST, :],
                                         v_s[DS * b:DS * b + DS, 0, :]).then_inc(out_sem, 16)
                    else:
                        sp.dma_start(o["kvs"][0].rearrange("b s h d -> (b s) (h d)"), v_s[:, 1, :]).then_inc(out_sem, 16)
                if t == TP:
                    load_chunk(6 + s)
                    if s < 3:
                        move_window(s + 1)
            for n in range(12, 18):
                load_chunk(n)

            sp.wait_ge(page_in, 16)
            load_values(sp, 0, 0)
            load_values(sp, 0, 1)
            sp.wait_ge(w_used, CHUNK_AT[("ada", 9)] + 1)
            group_list = [(w, g) for w, (m, b) in enumerate(sa) for g in range(len(groups[m]))]

            def values_behind(G):
                if G >= 2 and not values_by_act(*group_list[G]):
                    if G == 2:
                        sp.wait_ge(pa_min, NU)
                    load_values(sp, *group_list[G])

            for w, (m, b) in enumerate(sa):
                win_k = flat_k[0][b].rearrange("(g r) h d -> g r (h d)", r=16)
                for g, nt in enumerate(groups[m]):
                    G = NG[w] + g
                    ks = G % NK
                    if G == 2:
                        sp.wait_ge(w_used, CHUNK_AT[("ada", 11)] + 1)
                    if G >= NK:
                        sp.wait_ge(kg_t, G - NK + 1)
                    if m == 0 and g < 2:
                        sp.dma_start(kraw[ks][:, :, :], win_k[:, 4 * g:4 * g + 4, :]).then_inc(kg_in[ks], 64)
                    elif m == 0:
                        for i in range(4):
                            sp.dma_start(kraw[ks][32 * i:32 * i + 32, 0:2, :],
                                         win_k[96:128, 8 + i:16:4, :]).then_inc(kg_in[ks], 16)
                    else:
                        for t in range(4):
                            pg = sp.value_load(pages[0:1, N_PAGES * b + 4 * g + t:N_PAGES * b + 4 * g + t + 1],
                                               min_val=0, max_val=a["cache_k"].shape[1] - 1)
                            sp.dma_start(kraw[ks][:, t, :], flat_k[1][bass.ds(pg, 1)].rearrange("a p h d -> (a p) (h d)"))\
                                .then_inc(kg_in[ks], 16)
                    if G >= 3:
                        values_behind(G - 3)
                if w >= 2:
                    sp.wait_ge(kn_t, w - 1)
                    sp.wait_ge(sa_pv, w - 1)
                    load_new(sp, w)

            for G in range(len(group_list) - 3, len(group_list)):
                values_behind(G)

            sp.wait_ge(sa_s, len(sa))
            for n in range(FIRST_LATE, FIRST_LATE + 2):
                load_chunk(n)
            sp.wait_ge(sa_pv, len(sa))
            sp.dma_start(x_sb[:, 0:TP, :], a["x_prompt"][0].rearrange("(t p) d -> p t d", p=P)).then_inc(x_back, 16)
            sp.dma_start(x_sb[0:NS, TP, :], a["x_sample"].rearrange("b s d -> (b s) d")).then_inc(x_back, 16)
            sp.wait_ge(sa_fin, 2)
            for i, name in enumerate(("ln1_g", "ln1_b")):
                sp.dma_start(ln1[:, i, :], a[name].to_broadcast([P, D])).then_inc(ln_in, 16)
            sp.dma_start(st_r, a["state_conv"][0].rearrange("b j f -> (b j) f")).then_inc(st_in, 16)
            for i, t in enumerate(WO_TILES):
                if i == TP:
                    load_chunk(FIRST_LATE + 2)
                sp.wait_ge(x1_ok, i + 1)
                rows = P if t < TP else NS
                sp.dma_start(spill[P * t:P * t + rows, :], x_sb[0:rows, t, :]).then_inc(spilled if i < TP else spilled_last, 16)
            load_chunk(FIRST_LATE + 3)
            sp.wait_ge(st_mm, 11)
            for i, name in enumerate(("b_down", "ln2_g", "ln2_b")):
                sp.dma_start(ln2[:, i, :], a[name].to_broadcast([P, D])).then_inc(ln2_in, 16)
            for n in range(FIRST_LATE + 4, FIRST_LATE + 13):
                load_chunk(n)
                if n < FIRST_LATE + 12:
                    i = n - FIRST_LATE - 4
                    move_window(4 + i // 2, ((("cache_win_k", "wks"), ("cache_win_v", "wvs"))[i % 2],))
            load_chunk(FIRST_LATE + 13)
            sp.wait_ge(spilled, 16 * TP)
            sp.wait_ge(spilled_last, 16)
            sp.wait_ge(up_mm, 2 * FT)
            sp.dma_start(x_sb[:, 0:TP, :], spill[0:SEQ, :].rearrange("(t p) d -> p t d", p=P)).then_inc(x1_back, 16)
            sp.dma_start(x_sb[0:NS, TP, :], spill[SEQ:NT, :]).then_inc(x1_back, 16)
            load_chunk(FIRST_LATE + 14)
            for i in range(11):
                if i in (4, 8):
                    load_chunk(FIRST_LATE + 14 + i // 4)
                sp.wait_ge(us_a, i + 1)
                sp.dma_start(o["cp"][0, 0][:, CH * i:CH * i + CH], conv_out(i)[0:2, :]).then_inc(conv_st[i % 2], 16)
                sp.dma_start(o["cs"][0].rearrange("b j f -> (b j) f")[:, CH * i:CH * i + CH],
                             conv_out(i)[2:18, :]).then_inc(conv_st[i % 2], 16)
            for n in range(FIRST_LATE + 17, len(CHUNKS)):
                load_chunk(n)
            for t in range(TP + 1):
                if t < TP:
                    sp.wait_ge(y_out, t + 1)
                    sp.dma_start(o["yp"][0, P * t:P * t + P, :], x_sb[:, t, :]).then_inc(stored, 16)
                else:
                    sp.wait_ge(y_last, 1)
                    sp.dma_start(o["ys"].rearrange("b s d -> (b s) d"), x_sb[0:NS, t, :]).then_inc(stored, 16)
            sp.wait_ge(stored, 16 * (TP + 1))
            sp.wait_ge(conv_st[0], 32 * 6)
            sp.wait_ge(conv_st[1], 32 * 5)
            sp.wait_ge(copied, 16 * 2 * DB)
            sp.wait_ge(out_sem, 16 * (TP * 2 + 2 * DB + 2))
            for st in range(4):
                sp.wait_ge(stg[st], 16 * n_stored[st])

        @block.gpsimd
        def _(pool):
            pool.wait_ge(c_cp, 1)
            pool.wait_ge(vecs_c, 1)
            nc.gpsimd.memset(qtp, 0.0).then_inc(qzero, 1)
            def rest_of_ht(phase):
                if phase == 1:
                    for i in (1, 3):
                        pool.wait_ge(up0_high, i + 1)
                        n, kk = PIECES[UP0[i]]
                        high, rest = pair_of(n, slice(kk, kk + 2))
                        nc.gpsimd.tensor_tensor(rest, slot(SLOT_OF[n])[:, kk:kk + 2, :], high.bitcast(F32), ALU.subtract)\
                            .then_inc(up0_pool, 1)
                for k in range(1, KT_D, 2):
                    pool.wait_ge(ht_hi, ht_high_count(phase, k))
                    nc.gpsimd.tensor_tensor(ht_r[:, k, 0:SEQ], ht[:, k, 0:SEQ], ht_high_r[:, k, 0:SEQ].bitcast(F32),
                                            ALU.subtract).then_inc(ht_rest_p, 1)

            jobs = [(n, "rope", r) for r, n in enumerate(rope_units)]
            jobs += [(5 * c - 1.4, "split", c) for c in range(6)]
            for _, what, r in sorted(jobs):
                if what == "split":
                    n = CHUNK_AT[("in", r)]
                    for k in range(0, KT_D, 2):
                        if r == 0:
                            pool.wait_ge(in0_high, k // 2 + 1)
                        else:
                            pool.wait_ge(win_high, 4 * (r - 1) + k // 2 + 1)
                        w = slot(SLOT_OF[n])[:, k, :]
                        high, rest = pair_of(n, k)
                        nc.gpsimd.tensor_tensor(rest, w, high.bitcast(F32), ALU.subtract).then_inc(win_pool, 1)
                    if r == 0:
                        rest_of_ht(0)
                    continue
                s, t = units[rope_units[r]]
                sample_k = s in (1, 4) and t == TP
                pool.wait_ge(pj_d, r + 1)
                if not sample_k and r >= 4:
                    if (prev := last_t[r]) is not None:
                        pool.wait_ge(qk_t, prev)
                    if (q := last_store[r]) > 0:
                        pool.wait_ge(stg[r % 4], 16 * q)
                rows = P if t < TP else NS
                dst = k_s[:, s // 3, :] if sample_k else stage[0:rows, r % 4, :]
                nc.gpsimd.tensor_tensor(dst, tmp_a[0:rows, r % 2, :], tmp_b[0:rows, r % 2, :], ALU.add)\
                    .then_inc(rope_ok, 1)
            pool.wait_ge(w_used, CHUNK_AT[("in", 5)] + 1)
            nc.gpsimd.memset(qbd, 0.0).then_inc(qbd_zero, 1)
            pool.wait_ge(qbd_zero, 1)
            pool.wait_ge(qk_d, len(tr_units) - 2 * TP)
            for w, (m, b) in enumerate(sa):
                if w >= 2:
                    pool.wait_ge(sa_s, w - 1)
                for i in range(4):
                    last = nc.gpsimd.tensor_copy(qbd[32 * i:32 * i + 32, w % 2, :, i, :],
                                                 qrep[32 * i:32 * i + 32, m, :, DS * b:DS * b + DS])
                last.then_inc(q_bd, 1)
                if w == 1:
                    pool.wait_ge(q_bd, 2)
                    pool.wait_ge(pa_min, NU)
                    for i, place in enumerate((kn, ktn, small)):
                        nc.gpsimd.memset(place, 0.0).then_inc(new_zero, 1)
                        pool.wait_ge(new_zero, i + 1)
            def rest_of_piece(q):
                n, k = PIECES[q]
                if q < 8:
                    pool.wait_ge(wo_high, q + 1)
                else:
                    pool.wait_ge(wl_high, piece_count(q) - 8)
                w = slot(SLOT_OF[n])[:, k:k + 2, :]
                high, rest = pair_of(n, slice(k, k + 2))
                nc.gpsimd.tensor_tensor(rest, w, high.bitcast(F32), ALU.subtract).then_inc(wl_rest, 1)

            for q in range(8):
                rest_of_piece(q)
            pool.wait_ge(st_mm, 11)
            nc.gpsimd.memset(u_b[:, :, 0:2], 0.0).then_inc(halo, 1)
            rest_of_ht(1)
            pool.wait_ge(st_ok, 11)
            for k in range(2 * FT):
                f = k // 2 + FT * (k % 2)
                if k >= 2:
                    pool.wait_ge(up_cv, k - 1)
                rest_of_piece(12 + k)
                nc.gpsimd.tensor_copy(ext[:, k % 2, :, 0:2], st_t[:, f, :].rearrange("p (b j) -> p b j", b=DB))
                pool.wait_ge(up_u, k + 1)
                u3 = u_b[:, k % 2, 2 + SEQ:2 + NT].rearrange("p (b s) -> p b s", b=DB)
                nc.gpsimd.tensor_copy(ext[:, k % 2, :, 2:2 + DS], u3)
                nc.gpsimd.tensor_copy(u_last[:, f, 2:18].rearrange("p (b j) -> p b j", b=DB), u3[:, :, DS - 2:DS])
                nc.gpsimd.tensor_copy(u_last[:, f, 0:2], u_b[:, k % 2, SEQ:SEQ + 2]).then_inc(up_x, 1)
            for q in range(12 + 2 * FT, len(PIECES)):
                rest_of_piece(q)
            for t in range(TP):
                pool.wait_ge(n2_w, t + 1)
                nc.gpsimd.tensor_tensor(x_sb[:, t, :], x_sb[:, t, :], ln2[:, 2, :], ALU.add).then_inc(y_out, 1)

        @block.scalar
        def _(act):
            act.wait_ge(c_tr, 1)
            nc.scalar.activation(c_e, c_cols, ACT.Exp, scale=-1.0).then_inc(act_setup, 1)
            act.wait_ge(lam_dot, 2)
            nc.scalar.activation(lam_s[:, 2:4], lam_s[:, 0:2], ACT.Exp).then_inc(act_setup, 1)
            def high_of_ht(phase, mm, by_dve, by_act, shift, scale, bank):
                if phase == 1:
                    for q in UP0:
                        n, kk = PIECES[q]
                        act.wait_ge(w_in_slot[SLOT_OF[n]], slot_count(n))
                        nc.scalar.activation(pair_of(n, slice(kk, kk + 2))[0], slot(SLOT_OF[n])[:, kk:kk + 2, :], ACT.Copy)\
                            .then_inc(up0_high, 1)
                for f in range(1, KT_D, 2):
                    if phase == 0 and f == 5:
                        act.wait_ge(ada_ok, 4)
                        n = CHUNK_AT[("in", 0)]
                        act.wait_ge(w_in_slot[SLOT_OF[n]], slot_count(n))
                        for k in range(0, KT_D, 2):
                            nc.scalar.activation(pair_of(n, k)[0], slot(SLOT_OF[n])[:, k, :], ACT.Copy).then_inc(in0_high, 1)
                    act.wait_ge(mm, f + 2)
                    nc.scalar.activation(ht[:, f, 0:SEQ], bank(f), ACT.Identity, bias=mod_t[:, shift + f, 0:1],
                                         scale=mod_t[:, scale + f, 0:1]).then_inc(by_act, 1)
                act.wait_ge(mm, 9)
                if phase == 1:
                    act.wait_ge(spilled, 16 * TP)
                for f in range(KT_D):
                    if f == 5:
                        if phase == 1:
                            act.wait_ge(spilled_last, 16)
                        act.wait_ge(by_dve, 1)
                        nc.scalar.activation(ht_high_r[:, :, SEQ:NT], ht[:, :, SEQ:NT], ACT.Copy).then_inc(ht_hi, 1)
                    if f % 2 == 0:
                        act.wait_ge(by_dve, f // 2 + 2)
                    else:
                        act.wait_ge(by_act, f // 2 + 1)
                    nc.scalar.activation(ht_high_r[:, f, 0:SEQ], ht[:, f, 0:SEQ], ACT.Copy).then_inc(ht_hi, 1)

            act.wait_ge(ada_ok, 3)
            high_of_ht(0, xt_mm, xt_d, xt_a, 0, 8, lambda f: bk(f % 4))
            jobs = []
            for n, (s, t) in enumerate(units):
                if n in v_units:
                    jobs.append((n, "v", n))
                if n in tr_units and s in (0, 3) and t < TP:
                    jobs.append((n + 2.5, "q", n))
            act.wait_ge(qzero, 1)
            for _, what, n in sorted(jobs):
                s, t = units[n]
                rows = P if t < TP else NS
                if what == "v":
                    act.wait_ge(pj_mm, n + 1)
                    dst = vp[:, t, s // 3, :] if t < TP else v_s[:, s // 3, :]
                    nc.scalar.activation(dst, bk(n % 4)[0:rows, :], ACT.Copy).then_inc(pj_a, 1)
                else:
                    k = tr_units.index(n)
                    act.wait_ge(qk_t, k + 1)
                    src = bk(4 + k % 2).rearrange("p (f t) -> p f t", f=4)
                    m0 = 8 * (s // 3)
                    for h in range(2):
                        last = nc.scalar.activation(qtp[64 * h:64 * h + 64, m0 + h:m0 + 8:2, P * t:P * t + P],
                                                    src[64 * h:64 * h + 64], ACT.Copy)
                    last.then_inc(qk_a, 1)
            act.wait_ge(page_in, 16)
            for u, (m, n, qb) in enumerate(pa[:NU]):
                act.wait_ge(pa_min, u + 1)
                if u >= 2:
                    act.wait_ge(pa_t, u - 1)
                w = P * (qb + 1)
                nc.scalar.activation(p_b[:, u % 2, 0:w], s_m[:, u % 2, 0:w], ACT.Exp, bias=mn[:, u:u + 1], scale=-1.0,
                                     accum_out=rs[:, u:u + 1]).then_inc(pa_exp, 1)
            act.wait_ge(pa_pv, NU)
            act.wait_ge(pa_o, NU)
            act.wait_ge(out_sem, 16 * (TP * 2 + 2 * DB + 2))
            act.wait_ge(new_zero, 3)
            load_new(act, 0)
            load_new(act, 1)

            def probs_b(y):
                u = NU + y
                act.wait_ge(pb_min, y + 1)
                if y >= 2:
                    act.wait_ge(pb_t, y - 1)
                w = P * (pb[y][2] + 1)
                nc.scalar.activation(p_b[:, y % 2, 0:w], s_m[:, y % 2, 0:w], ACT.Exp, bias=mn[:, u:u + 1], scale=-1.0,
                                     accum_out=rs[:, u:u + 1]).then_inc(pb_exp, 1)

            def copy_b(y):
                act.wait_ge(pb_t, y + 1)
                if y >= 2:
                    act.wait_ge(pb_pv, y - 1)
                w = P * (pb[y][2] + 1)
                nc.scalar.activation(pt_b[:, y % 2, 0:w], bk(6)[:, 0:w], ACT.Copy).then_inc(pb_pt, 1)

            for w, (m, b) in enumerate(sa):
                n = 32 * sum(groups[m])
                act.wait_ge(sa_min, w + 1)
                for h in range(2):
                    if w >= 1:
                        act.wait_ge(sa_t, 2 * (w - 1) + h + 1)
                    src = sm_s[:, h, 0:n] if m == 0 else bk(h)[:, 0:n]
                    nc.scalar.activation(p_s[:, h, 0:n], src, ACT.Exp, bias=blk_o[:, h:h + 1], scale=-1.0,
                                         accum_out=rs_s[:, h, w:w + 1])
                    nc.scalar.activation(p_s[:, h, n:n + 32], sm_n[:, h, :], ACT.Exp, bias=blk_o[:, h:h + 1], scale=-1.0,
                                         accum_out=rs_n[:, h, w:w + 1]).then_inc(sa_exp, 1)
                act.wait_ge(sa_t, 2 * w + 2)
                if w >= 1:
                    act.wait_ge(sa_pv, w)
                full = P * (n // P)
                if m == 0:
                    nc.scalar.activation(pt_s[0:64, 1, full:full + P], bk(3)[0:64, full:full + P], ACT.Copy)
                nc.scalar.activation(pt_s[:, 1, 0:full], bk(3)[:, 0:full], ACT.Copy).then_inc(sa_ph, 1)
                if values_by_act(w + 1, 0):
                    load_values(act, w + 1, 0)
                probs_b(2 * w)
                if values_by_act(w + 1, 1):
                    load_values(act, w + 1, 1)
                if values_by_act(w + 1, 2):
                    load_values(act, w + 1, 2)
                copy_b(2 * w)
                probs_b(2 * w + 1)
                act.wait_ge(sa_pv, w + 1)
                nc.scalar.activation(o_s[:, w, :], bk(4)[:, 0:P], ACT.Copy).then_inc(sa_o, 1)
                copy_b(2 * w + 1)
            act.wait_ge(rms_sq, 1)
            nc.scalar.activation(rms[:, 1, :], rms[:, 0, :], ACT.Sqrt).then_inc(rms_rt, 1)
            def high_of_wo(q):
                n, k = PIECES[q]
                act.wait_ge(w_in_slot[SLOT_OF[n]], slot_count(n))
                nc.scalar.activation(pair_of(n, slice(k, k + 2))[0], slot(SLOT_OF[n])[:, k:k + 2, :], ACT.Copy).then_inc(wo_high, 1)

            for q in range(4):
                high_of_wo(q)
            for f in range(KT_D):
                act.wait_ge(mt_mm, f + 1)
                nc.scalar.activation(ht[:, f, 0:SEQ], bk(4 + (f + 1) % 4), ACT.Copy, scale=1.0 if f < 4 else g8[:, 0:1])\
                    .then_inc(mt_a, 1)
            for q in range(4, 8):
                high_of_wo(q)
            act.wait_ge(sa_q, 1)
            nc.scalar.activation(ob_q, ob_q, ACT.Sqrt).then_inc(sa_r, 1)
            act.wait_ge(mt_mm, 8)
            for j in range(8):
                act.wait_ge(gb_mm, j + 1)
                which, kind, half = j // 4, (j // 2) % 2, j % 2
                g = gate if which == 0 else gate2
                rows = P if kind == 0 else NS
                nc.scalar.activation(g[0:rows, kind, CH * half:CH * half + CH], bk(j % 2)[0:rows, :], ACT.Copy)\
                    .then_inc(gb_a, 1)
            for t in range(TP + 1):
                act.wait_ge(n_var, t + 1)
                nc.scalar.activation(mv[:, 2:3], mv[:, 1:2], ACT.Sqrt).then_inc(n_rt, 1)
            high_of_ht(1, h2_mm, h2_d, h2_a, 24, 32, lambda f: bk(f))
            act.wait_ge(halo, 1)
            for k in range(2 * FT):
                f = k // 2 + FT * (k % 2)
                act.wait_ge(up_mm, k + 1)
                if k >= 2:
                    act.wait_ge(up_x, k - 1)
                    act.wait_ge(up_cv, k - 1)
                pair = up_bank(k)
                nc.scalar.activation(u_b[:, k % 2, 2:2 + NT].rearrange("p (h t) -> p h t", h=2), pair, ACT.Identity,
                                     bias=vec_t[:, 0, 48 + f:49 + f]).then_inc(up_u, 1)
                act.wait_ge(up_u, k + 1)
                if k >= 2:
                    if k % 2 == 0:
                        act.wait_ge(up_ge, k // 2)
                    else:
                        act.wait_ge(up_gt, k // 2)
                nc.scalar.activation(cv[:, k % 2, :], u_b[:, k % 2, 2:2 + NT], ACT.Identity,
                                     bias=vec_t[:, 2, 44 + f:45 + f], scale=vec_t[:, 2, f:f + 1]).then_inc(up_c0, 1)
                if k % 2 == 1:
                    act.wait_ge(up_cv, k)
                    if k >= 5:
                        act.wait_ge(up_gt, k // 2 - 1)
                    nc.scalar.activation(ga[:, (k // 2) % 2, :], cv[:, 0, :], ACT.Gelu).then_inc(up_ge, 1)
            for i in range(11):
                act.wait_ge(us_mm, i + 1)
                if i >= 2:
                    act.wait_ge(conv_st[i % 2], 32 * (i // 2))
                nc.scalar.activation(conv_out(i), bk(6 + i % 2)[0:18, :], ACT.Copy).then_inc(us_a, 1)
            def scale_norm(t):
                rows = P if t < TP else NS
                act.wait_ge(n2_fac, t + 1)
                x = x_sb[0:rows, t, :]
                nc.scalar.activation(x, x, ACT.Identity, bias=mv2[0:rows, t, 4:5], scale=mv2[0:rows, t, 3:4]).then_inc(n2_scaled, 1)

            for t in range(TP + 1):
                rows = P if t < TP else NS
                act.wait_ge(n2_var, t + 1)
                nc.scalar.activation(mv2[0:rows, t, 2:3], mv2[0:rows, t, 1:2], ACT.Sqrt).then_inc(n2_rt, 1)
                scale_norm(t)

        @block.vector
        def _(dve):
            steps = [0]

            def then(ins):
                steps[0] += 1
                ins.then_inc(dve_seq, 1)
                dve.wait_ge(dve_seq, steps[0])

            nc.vector.memset(bk(6), 0.0).then_inc(bank6_zero, 1)
            dve.wait_ge(act_setup, 1)
            then(nc.vector.tensor_scalar(c_e, c_e, 1.0, None, ALU.add))
            then(nc.vector.reciprocal(c_e, c_e))
            nc.vector.tensor_tensor(c_t[:, :, :], c_cols, c_e, ALU.mult).then_inc(c_cp, 1)
            dve.wait_ge(vecs_t, 1)
            nc.vector.tensor_copy(vec_t[:, 0, 0:93], bk(0)[:, 0:93])
            then(nc.vector.tensor_copy(vec_t[:, 1:3, 0:88], bk(0)[:, P:3 * P].rearrange("p (r d) -> p r d", r=2)[:, :, 0:88]))
            nc.vector.tensor_copy(bada[:, :], vec_t[:, 0, 0:48])
            then(nc.vector.tensor_scalar(g8[:, :], vec_t[:, 0, 92:93], 1.0 - LAM_INIT, None, ALU.mult))
            for at in (8, 32):
                then(nc.vector.tensor_scalar(bada[:, at:at + 8], bada[:, at:at + 8], 1.0, None, ALU.add))
            dve.wait_ge(early, 16 * 12)
            for i in range(2):
                nc.vector.tensor_tensor_reduce(out=lam4[:, 2 * i, :], in0=lam4[:, 2 * i, :], in1=lam4[:, 2 * i + 1, :],
                                               scale=1.0, scalar=0.0, op0=ALU.mult, op1=ALU.add,
                                               accum_out=lam_s[:, i:i + 1]).then_inc(lam_dot, 1)
            dve.wait_ge(lam_dot, 2)
            nc.vector.memset(lam_s[:, 7:8], 0.0).then_inc(vecs_c, 1)
            dve.wait_ge(act_setup, 2)
            then(nc.vector.tensor_tensor(lam_s[:, 4:5], lam_s[:, 3:4], lam_s[:, 2:3], ALU.subtract))
            then(nc.vector.tensor_scalar(lam_s[:, 5:6], lam_s[:, 4:5], -LAM_INIT, None, ALU.add))

            def ada_rows(ch):
                dve.wait_ge(ada_mm, ch + 1)
                if ch >= 2:
                    dve.wait_ge(ada_tt, ch - 1)
                nc.vector.tensor_copy(mod_s[:, ch % 2, :], bk(6)).then_inc(ada_ms, 1)

            def ada_sum(ch):
                dve.wait_ge(ada_tt, ch + 1)
                nc.vector.tensor_tensor(mod_t[:, 4 * ch:4 * ch + 4, :],
                                        bk(7)[:, 0:64].rearrange("p (c r) -> p c r", c=4)[:, :, 0:C],
                                        bada[:, 4 * ch:4 * ch + 4][:, :, None].to_broadcast([P, 4, C]), ALU.add)\
                    .then_inc(ada_ok, 1)

            def high_of_piece(q):
                n, k = PIECES[q]
                dve.wait_ge(w_in_slot[SLOT_OF[n]], slot_count(n))
                nc.vector.tensor_copy(pair_of(n, slice(k, k + 2))[0], slot(SLOT_OF[n])[:, k:k + 2, :]).then_inc(wl_high, 1)

            def modulate_sample(mm, done, shift, scale, bank):
                dve.wait_ge(mm, 1)
                src = bank.rearrange("p (f b s) -> p f b s", f=KT_D, b=DB)
                dst = ht[:, :, SEQ:NT].rearrange("p f (b s) -> p f b s", b=DB)
                col = lambda at: mod_t[:, at:at + 8, 1:C][:, :, :, None].to_broadcast([P, KT_D, DB, DS])
                then(nc.vector.tensor_tensor(dst, src, col(scale), ALU.mult))
                nc.vector.tensor_tensor(dst, dst, col(shift), ALU.add).then_inc(done, 1)

            def modulate(mm, done, shift, scale, bank, tiles=range(0, KT_D, 2)):
                for f in tiles:
                    dve.wait_ge(mm, f + 2)
                    nc.vector.tensor_scalar(ht[:, f, 0:SEQ], bank(f), mod_t[:, scale + f, 0:1],
                                            mod_t[:, shift + f, 0:1], ALU.mult, ALU.add).then_inc(done, 1)

            def rest_of_ht(phase, f):
                dve.wait_ge(ht_hi, ht_high_count(phase, f))
                at, cols = (slice(0, KT_D), slice(SEQ, NT)) if f is None else (f, slice(0, SEQ))
                nc.vector.tensor_tensor(ht_r[:, at, cols], ht[:, at, cols], ht_high_r[:, at, cols].bitcast(F32),
                                        ALU.subtract).then_inc(ht_rest, 1)

            def split_in(c, k):
                n = CHUNK_AT[("in", c)]
                if c == 0 and k % 2 == 0:
                    return
                if k == (c == 0):
                    dve.wait_ge(w_in_slot[SLOT_OF[n]], slot_count(n))
                if c:
                    dve.wait_ge(win_free, 8 * (c - 1) + k + 1)
                w = slot(SLOT_OF[n])[:, k, :]
                high, rest = pair_of(n, k)
                if k % 2 == 0:
                    nc.vector.tensor_copy(high, w).then_inc(win_high, 1)
                else:
                    then(nc.vector.tensor_copy(high, w))
                    nc.vector.tensor_tensor(rest, w, high.bitcast(F32), ALU.subtract).then_inc(win_dve, 1)

            for ch in range(3):
                ada_rows(ch)
                ada_sum(ch)
            dve.wait_ge(ada_ok, 3)
            modulate(xt_mm, xt_d, 0, 8, lambda f: bk(f % 4), (0, 2))
            ada_rows(3)
            ada_sum(3)
            dve.wait_ge(ada_ok, 4)
            modulate_sample(xt_mm, xt_d, 0, 8, bk(4))
            modulate(xt_mm, xt_d, 0, 8, lambda f: bk(f % 4), (4, 6))
            for k in range(4):
                split_in(0, k)
            for k in range(0, KT_D, 2):
                rest_of_ht(0, k)
                for kk in range(min(KT_D, 4 + k), min(KT_D, 6 + k)):
                    split_in(0, kk)
            rest_of_ht(0, None)

            jobs = [(n, "rope", n) for n in rope_units]
            jobs += [(n + 2.5, "t", n) for n in tr_units if not (units[n][0] in (0, 3) and units[n][1] < TP)]
            jobs += [(5 * c - 1.4, "split", c) for c in range(1, 6)]
            dve.wait_ge(rope_in, 16)
            for _, what, n in sorted(jobs):
                if what == "split":
                    for k in range(KT_D):
                        split_in(n, k)
                    continue
                s, t = units[n]
                rows = P if t < TP else NS
                if what == "rope":
                    r = rope_units.index(n)
                    dve.wait_ge(pj_mm, n + 1)
                    if r >= 2:
                        dve.wait_ge(rope_ok, r - 1)
                    src = bk(n % 4)[0:rows].rearrange("p (h d) -> p h d", h=MAPS)
                    w = 0 if s in (0, 3) else 1
                    tb = tmp_b[0:rows, r % 2, :].rearrange("p (h d) -> p h d", h=MAPS)
                    ta = tmp_a[0:rows, r % 2, :].rearrange("p (h d) -> p h d", h=MAPS)
                    tab = lambda x, k: rope[0:rows, t, w, x:x + k][:, None, :].to_broadcast([rows, MAPS, k])
                    nc.vector.tensor_tensor(ta, src, tab(0, 64), ALU.mult)
                    nc.vector.tensor_tensor(tb[:, :, 0:32], src[:, :, 32:64], tab(64, 32), ALU.mult)
                    nc.vector.tensor_tensor(tb[:, :, 32:64], src[:, :, 0:32], tab(96, 32), ALU.mult).then_inc(pj_d, 1)
                else:
                    k = tr_units.index(n)
                    dve.wait_ge(qk_t, k + 1)
                    src = bk(4 + k % 2).rearrange("p (f t) -> p f t", f=4)
                    if t < TP:
                        nc.vector.tensor_copy(kt[:, 4 * (s // 3):4 * (s // 3) + 4, P * t:P * t + P], src).then_inc(qk_d, 1)
                    else:
                        for i in range(4):
                            for g in range(4):
                                last = nc.vector.tensor_copy(
                                    qrep[32 * i:32 * i + 32, s // 3, g:16:4, :],
                                    bk(4 + k % 2)[32 * g:32 * g + 32, 0:4 * NS].rearrange("p (f t) -> p f t", f=4))
                        last.then_inc(qk_d, 1)

            def turn_keys(w, g, tiles=None):
                m, b = sa[w]
                G = NG[w] + g
                dve.wait_ge(kg_in[G % NK], k_count(m, w, g))
                if G >= NK:
                    dve.wait_ge(sa_g, G - NK + 1)
                for t in tiles or range(groups[m][g]):
                    last = nc.vector.transpose(ktg[:, G % NK, :, 32 * t:32 * t + 32],
                                               kraw[G % NK][:, t, :].rearrange("p (g d) -> p g d", d=32))
                if t == groups[m][g] - 1:
                    last.then_inc(kg_t, 1)

            dve.wait_ge(tables, 16 * 8)
            for s in range(NU + 3):
                if s < NU:
                    m, n, qb = pa[s]
                    w = P * (qb + 1)
                    dve.wait_ge(pa_s, s + 1)
                    if s >= 2:
                        dve.wait_ge(pa_exp, s - 1)
                    else:
                        dve.wait_ge(rope_ok, len(rope_units))
                    nc.vector.tensor_tensor_reduce(out=s_m[:, s % 2, 0:w], in0=bk(s % 2)[:, 0:w],
                                                   in1=maskt[:, m, SEQ - w:SEQ], scale=1.0, scalar=NEG, op0=ALU.add,
                                                   op1=ALU.min, accum_out=mn[:, s:s + 1]).then_inc(pa_min, 1)
                if 0 <= (x := s - 2) < NU:
                    w = P * (pa[x][2] + 1)
                    dve.wait_ge(pa_t, x + 1)
                    if x >= 2:
                        dve.wait_ge(pa_pv, x - 1)
                    nc.vector.tensor_copy(pt_b[:, x % 2, 0:w], bk(2 + x % 2)[:, 0:w]).then_inc(pa_pt, 1)
                if s % 4 == 0 and s >= 4:
                    ada_sum(4 + s // 4 - 1)
                if 0 <= (x := s - 3) < NU:
                    m, n, qb = pa[x]
                    if x == 0:
                        for st in range(4):
                            dve.wait_ge(stg[st], 16 * n_stored[st])
                    dve.wait_ge(pa_exp, x + 1)
                    then(nc.vector.reciprocal(rcp[:, x:x + 1], rs[:, x:x + 1]))
                    dve.wait_ge(pa_pv, x + 1)
                    nc.vector.tensor_scalar(mixv[:, qb, 64 * n:64 * n + 64], bk(4 + x % 2)[:, 64 * (n % 2):64 * (n % 2) + 64],
                                            rcp[:, x:x + 1], None, ALU.mult).then_inc(pa_o, 1)
                if s < NU and s % 4 == 3:
                    ada_rows(4 + s // 4)
                if 0 <= (i := s - (NU - 2)) < 4:
                    if i == 0:
                        dve.wait_ge(w_used, CHUNK_AT[("ada", 10)] + 1)
                    turn_keys(0, i // 2, (2 * (i % 2), 2 * (i % 2) + 1))

            def mask_b(y):
                w = P * (pb[y][2] + 1)
                dve.wait_ge(pb_s, y + 1)
                if y >= 2:
                    dve.wait_ge(pb_exp, y - 1)
                else:
                    dve.wait_ge(pa_exp, NU)
                nc.vector.tensor_tensor_reduce(out=s_m[:, y % 2, 0:w], in0=bk(5)[:, 0:w], in1=maskt[:, 1, SEQ - w:SEQ],
                                               scale=1.0, scalar=NEG, op0=ALU.add, op1=ALU.min,
                                               accum_out=mn[:, NU + y:NU + y + 1]).then_inc(pb_min, 1)

            def out_b(y):
                m, n, qb = pb[y]
                r = rcp[:, NU + y:NU + y + 1]
                dve.wait_ge(pb_exp, y + 1)
                then(nc.vector.reciprocal(r, rs[:, NU + y:NU + y + 1]))
                dve.wait_ge(pb_pv, y + 1)
                if n % 2 == 0:
                    nc.vector.tensor_scalar(o_1, bk(7)[:, 0:P], r, None, ALU.mult).then_inc(pb_o, 1)
                    dve.wait_ge(pb_o, y + 1)
                else:
                    then(nc.vector.tensor_scalar(r, r, lam_s[:, 5:6], None, ALU.mult))
                    mb = mixv[:, qb, WID + 64 * (n - 1):WID + 64 * (n + 1)]
                    nc.vector.scalar_tensor_tensor(out=mb, in0=bk(7)[:, 0:P], scalar=r, in1=o_1, op0=ALU.mult, op1=ALU.add)\
                        .then_inc(pb_o, 1)
                    dve.wait_ge(pb_o, y + 1)
                    at = 4 * qb + n // 2
                    then(nc.vector.tensor_tensor_reduce(out=sq_b, in0=mb, in1=mb, scale=1.0, scalar=0.0, op0=ALU.mult,
                                                        op1=ALU.add, accum_out=rms[:, 2, at:at + 1]))

            dve.wait_ge(w_used, CHUNK_AT[("ada", 11)] + 1)

            def turn_new(w):
                dve.wait_ge(new_in[w % 2], 32 * (w // 2 + 1))
                if w >= 2:
                    dve.wait_ge(sa_s, w - 1)
                nc.vector.transpose(ktn[0:32, w % 2, :, :], kn[0:32, w % 2, :].rearrange("p (g d) -> p g d", d=32))\
                    .then_inc(kn_t, 1)

            for g in range(2, len(groups[0])):
                turn_keys(0, g)
            dve.wait_ge(new_zero, 3)
            turn_new(0)
            for w, (m, b) in enumerate(sa):
                n = 32 * sum(groups[m])
                dve.wait_ge(sa_s, w + 1)
                if w >= 1:
                    dve.wait_ge(sa_exp, 2 * w)
                for h in range(2):
                    if m == 0:
                        then(nc.vector.tensor_tensor_reduce(out=sm_s[:, h, 0:n], in0=bk(h)[:, 0:n], in1=smask[:, 0:n],
                                                            scale=1.0, scalar=NEG, op0=ALU.add, op1=ALU.min,
                                                            accum_out=blk[:, h:h + 1]))
                    else:
                        then(nc.vector.tensor_reduce(blk[:, h:h + 1], bk(h)[:, 0:n], AX_X, ALU.min))
                here = smask[:, 320 + 32 * m:352 + 32 * m]
                then(nc.vector.tensor_tensor(sm_n, bk(4)[:, 384:448].rearrange("p (h n) -> p h n", h=2),
                                             here[:, None, :].to_broadcast([P, 2, 32]), ALU.add))
                then(nc.vector.tensor_reduce(blk[:, 2:4], sm_n, AX_X, ALU.min))
                then(nc.vector.tensor_tensor(blk[:, 0:2], blk[:, 0:2], blk[:, 2:4], ALU.min))
                then(nc.vector.transpose(blk_t, blk))
                then(nc.vector.tensor_reduce(small[:, 176:184], blk_t.rearrange("p (i q) -> p q i", i=4), AX_X, ALU.min))
                then(nc.vector.tensor_copy(blk_r.rearrange("p (i q) -> p i q", i=4),
                                           small[:, 176:184][:, None, :].to_broadcast([P, 4, DS])))
                nc.vector.transpose(blk_o, blk_r).then_inc(sa_min, 1)
                last_g = len(groups[sa[w + 1][0]]) if w + 1 < len(sa) else 0
                if last_g:
                    turn_keys(w + 1, 0)
                full = P * (n // P)
                dve.wait_ge(sa_t, 2 * w + 1)
                if w >= 1:
                    dve.wait_ge(sa_pv, w)
                if m == 0:
                    nc.vector.tensor_copy(pt_s[0:64, 0, full:full + P], bk(2)[0:64, full:full + P])
                nc.vector.tensor_copy(pt_s[:, 0, 0:full], bk(2)[:, 0:full]).then_inc(sa_pt, 1)
                dve.wait_ge(sa_t, 2 * w + 2)
                nc.vector.tensor_copy(ptn[0:32, :, :], bk(4)[0:32, P:3 * P].rearrange("p (h c) -> p h c", h=2)).then_inc(sa_pt, 1)
                if last_g:
                    turn_keys(w + 1, 1)
                if w:
                    out_b(2 * w - 1)
                mask_b(2 * w)
                if last_g:
                    turn_keys(w + 1, 2)
                if last_g == 4:
                    turn_keys(w + 1, 3)
                mask_b(2 * w + 1)
                if last_g:
                    turn_new(w + 1)
                out_b(2 * w)
            out_b(2 * len(sa) - 1)
            nc.vector.tensor_scalar(rms[:, 0, :], rms[:, 2, :], 1.0 / P, EPS, ALU.mult, ALU.add).then_inc(rms_sq, 1)
            dve.wait_ge(sa_l, 1)
            then(nc.vector.reciprocal(l_s, bk(0)[:, 0:16]))
            then(nc.vector.tensor_scalar(lam_s[:, 6:7], diff_c[:, 1:2], lam_s[:, 5:6], diff_c[:, 0:1], ALU.mult, ALU.add))
            l_b = l_s.rearrange("p (b m) -> p b m", m=2)
            then(nc.vector.tensor_scalar(l_b[:, :, 1], l_b[:, :, 1], lam_s[:, 6:7], None, ALU.mult))
            dve.wait_ge(sa_o, 16)
            then(nc.vector.tensor_tensor(o_s, o_s, l_s[:, :, None].to_broadcast([P, 16, P]), ALU.mult))
            o_a = o_s.rearrange("p (b m) d -> p b m d", m=2)[:, :, 0, :]
            nc.vector.tensor_tensor(o_a, o_a, colmask[:, None, :].to_broadcast([P, DB, P]), ALU.mult).then_inc(sa_n, 1)
            dve.wait_ge(rms_rt, 1)
            then(nc.vector.reciprocal(rms[:, 2, :], rms[:, 1, :]))
            for t in range(TP):
                mb = mixv[:, t, WID:D].rearrange("p (h d) -> p h d", h=4)
                last = nc.vector.tensor_tensor(mb, mb, rms[:, 2, 4 * t:4 * t + 4][:, :, None].to_broadcast([P, 4, P]), ALU.mult)
            last.then_inc(rms_ok, 1)
            dve.wait_ge(pb_pv, len(pb))
            for g, at in enumerate((16, 40)):
                last = nc.vector.tensor_copy(gexp[:, 8 * g:8 * g + 8], mod_t[:, at:at + 8, 1:C][:, :, :, None]
                                             .to_broadcast([P, 8, DB, DS]))
            last.then_inc(mt_d, 1)

            def split_mixed(f):
                dve.wait_ge(mt_a, f + 1)
                high = mt_high_r[:, f, 0:SEQ]
                then(nc.vector.tensor_copy(high, ht[:, f, 0:SEQ]))
                nc.vector.tensor_tensor(ht_r[:, f, 0:SEQ], ht[:, f, 0:SEQ], high.bitcast(F32), ALU.subtract).then_inc(mt_rest, 1)

            dve.wait_ge(sa_x, 1)
            tok = lambda f: ht[:, f:f + 4, SEQ:NT].rearrange("p j (b q) -> p j b q", b=DB)
            bjq = lambda ap: ap.rearrange("p (b j q) -> p j b q", b=DB, j=4)
            jbq = lambda ap: ap.rearrange("p (j b q) -> p j b q", b=DB, j=4)
            dve.wait_ge(sa_pv, len(sa))
            nc.vector.tensor_copy(tok(0), bjq(bk(1)[:, 0:256])).then_inc(sa_fin, 1)
            then(nc.vector.tensor_copy(jbq(ob_t), bjq(bk(2)[:, 0:256])))
            nc.vector.tensor_tensor(ob_q, ob_t, ob_t, ALU.mult).then_inc(sa_n, 1)
            for f in range(4):
                split_mixed(f)
            dve.wait_ge(sa_sq, 1)
            nc.vector.tensor_scalar(ob_q, bk(3)[:, 0:256], 1.0 / P, EPS, ALU.mult, ALU.add).then_inc(sa_q, 1)
            for f in range(4, KT_D):
                split_mixed(f)
            dve.wait_ge(sa_r, 1)
            then(nc.vector.reciprocal(ob_r, ob_q))
            then(nc.vector.tensor_tensor(ob_t, ob_t, ob_r, ALU.mult))
            nc.vector.tensor_scalar(tok(4), jbq(ob_t), g8[:, 0:1], None, ALU.mult).then_inc(sa_fin, 1)
            dve.wait_ge(sa_fin, 2)
            then(nc.vector.tensor_copy(mt_high_r[:, :, SEQ:NT], ht[:, :, SEQ:NT]))
            nc.vector.tensor_tensor(ht_r[:, :, SEQ:NT], ht[:, :, SEQ:NT], mt_high_r[:, :, SEQ:NT].bitcast(F32), ALU.subtract)\
                .then_inc(mt_hi, 1)

            def norm(t, rows, g_row, b_row, k):
                x = x_sb[0:rows, t, :]
                for h in range(2):
                    then(nc.vector.bn_stats(stat[0:rows, h, :], x[:, 512 * h:512 * h + 512]))
                then(nc.vector.bn_aggr(mv[0:rows, 0:2], stat[0:rows, :, :].rearrange("p h s -> p (h s)")))
                nc.vector.tensor_scalar(mv[0:rows, 1:2], mv[0:rows, 1:2], EPS, None, ALU.add).then_inc(n_var, 1)
                dve.wait_ge(n_rt, k + 1)
                then(nc.vector.reciprocal(mv[0:rows, 3:4], mv[0:rows, 2:3]))
                then(nc.vector.tensor_scalar(x, x, mv[0:rows, 0:1], mv[0:rows, 3:4], ALU.subtract, ALU.mult))
                then(nc.vector.tensor_tensor(x, x, g_row[0:rows], ALU.mult))
                return nc.vector.tensor_tensor(x, x, b_row[0:rows], ALU.add)

            dve.wait_ge(gb_a, 4)
            dve.wait_ge(gb_mm, 8)
            dve.wait_ge(ln_in, 32)
            dve.wait_ge(x_back, 32)
            for i, t in enumerate(WO_TILES):
                rows, kind = (P, 0) if t < TP else (NS, 1)
                for half in range(2):
                    j = 2 * i + half
                    dve.wait_ge(wo_mm, j + 1)
                    nc.vector.tensor_tensor(y_sb[0:rows, i % 2, 512 * half:512 * half + 512], bk(4 + j % 4)[0:rows],
                                            gate[0:rows, kind, 512 * half:512 * half + 512], ALU.mult).then_inc(wo_d, 1)
                    for q in st_after.get(j, []):
                        dve.wait_ge(st_mm, q + 1)
                        nc.vector.tensor_copy(st_t[:, 4 * q:4 * q + 4, :],
                                              bk(2 + q % 2)[:, 0:64].rearrange("p (f r) -> p f r", f=4)).then_inc(st_ok, 1)
                dve.wait_ge(wo_d, 2 * i + 2)
                x = x_sb[0:rows, t, :]
                then(nc.vector.scalar_tensor_tensor(out=x, in0=x, scalar=ALPHA, in1=y_sb[0:rows, i % 2, :],
                                                    op0=ALU.mult, op1=ALU.add))
                norm(t, rows, ln1[:, 0, :], ln1[:, 1, :], i).then_inc(x1_ok, 1)
                if i == 3:
                    modulate_sample(h2_mm, h2_d, 24, 32, bk(0))
            modulate(h2_mm, h2_d, 24, 32, lambda f: bk(f))
            for k in range(0, KT_D, 2):
                if k in (0, 4):
                    dve.wait_ge(up0_high, k // 2 + 1)
                    n, kk = PIECES[UP0[k // 2]]
                    high, rest = pair_of(n, slice(kk, kk + 2))
                    nc.vector.tensor_tensor(rest, slot(SLOT_OF[n])[:, kk:kk + 2, :], high.bitcast(F32), ALU.subtract)\
                        .then_inc(up0_dve, 1)
                rest_of_ht(1, k)
            rest_of_ht(1, None)

            def split_gated(z):
                f, b = z % FT, z % NG_BUF
                if z >= NG_BUF:
                    dve.wait_ge(g_used, z - NG_BUF + 1)
                then(nc.vector.tensor_copy(g_high_r[:, b, :], gt[:, f, :]))
                nc.vector.tensor_tensor(g_rest_r[b], gt[:, f, :], g_high_r[:, b, :].bitcast(F32), ALU.subtract)\
                    .then_inc(g_split, 1)

            for k in range(2 * FT):
                f = k // 2 + FT * (k % 2)
                tap = lambda j: vec_t[:, 1, 44 * j + f:44 * j + f + 1]
                c_p, c_sm = cv[:, k % 2, 0:SEQ], cv[:, k % 2, SEQ:NT].rearrange("p (b s) -> p b s", b=DB)
                high_of_piece(12 + k)
                if k == 2 * FT - 1:
                    dve.wait_ge(up_mm, 2 * FT)
                    split_gated(0)
                    split_gated(1)
                dve.wait_ge(up_c0, k + 1)
                then(nc.vector.scalar_tensor_tensor(out=c_p, in0=u_b[:, k % 2, 1:1 + SEQ], scalar=tap(1), in1=c_p,
                                                    op0=ALU.mult, op1=ALU.add))
                nc.vector.scalar_tensor_tensor(out=c_p, in0=u_b[:, k % 2, 0:SEQ], scalar=tap(0), in1=c_p,
                                               op0=ALU.mult, op1=ALU.add)
                dve.wait_ge(up_x, k + 1)
                then(nc.vector.scalar_tensor_tensor(out=c_sm, in0=ext[:, k % 2, :, 1:1 + DS], scalar=tap(1), in1=c_sm,
                                                    op0=ALU.mult, op1=ALU.add))
                nc.vector.scalar_tensor_tensor(out=c_sm, in0=ext[:, k % 2, :, 0:DS], scalar=tap(0), in1=c_sm,
                                               op0=ALU.mult, op1=ALU.add).then_inc(up_cv, 1)
                if k % 2 == 1:
                    dve.wait_ge(up_ge, k // 2 + 1)
                    dve.wait_ge(up_cv, k + 1)
                    nc.vector.tensor_tensor(gt[:, k // 2, :], ga[:, (k // 2) % 2, :], cv[:, 1, :], ALU.mult).then_inc(up_gt, 1)

            def add_half(half, t):
                rows, kind = (P, 0) if t < TP else (NS, 1)
                cols = slice(CH * half, CH * half + CH)
                j = (TP + 1) * half + t
                dve.wait_ge(dn_mm, j + 1)
                nc.vector.tensor_tensor(y3[0:rows], bk(j % 8)[0:rows], gate2[0:rows, kind, cols], ALU.mult).then_inc(dn_d, 1)
                dve.wait_ge(dn_d, j + 1)
                x = x_sb[0:rows, t, cols]
                then(nc.vector.tensor_tensor(x, x, y3[0:rows], ALU.add))
                then(nc.vector.bn_stats(stat2[0:rows, t, half, :], x))

            dve.wait_ge(up_gt, FT)
            for z in range(2, NG_BUF):
                split_gated(z)
            q = 12 + 2 * FT
            starts = [FT * half + 8 * kg for half in range(2) for kg in range(3)][1:]
            piece_at = {z: sum(n == CHUNK_AT[("down", 1 + i)] for n, k in PIECES) for i, z in enumerate(starts)}
            dve.wait_ge(ln2_in, 48)
            dve.wait_ge(gb_a, 8)
            dve.wait_ge(x1_back, 32)
            pre = []
            for t in range(TP + 1):
                pre += [(0, t), (1, t)]
            for z in range(NG_BUF, 2 * FT):
                split_gated(z)
                for _ in range(min(2, piece_at.get(z, 0))):
                    high_of_piece(q)
                    q += 1
                for _ in range(max(0, piece_at.get(z - 1, 0) - 2)):
                    high_of_piece(q)
                    q += 1
                if pre:
                    half, t = pre.pop(0)
                    rows, kind = (P, 0) if t < TP else (NS, 1)
                    cols = slice(CH * half, CH * half + CH)
                    then(nc.vector.tensor_tensor(y3[0:rows], gate2[0:rows, kind, cols], ln2[0:rows, 0, cols], ALU.mult))
                    x = x_sb[0:rows, t, cols]
                    then(nc.vector.scalar_tensor_tensor(out=x, in0=x, scalar=ALPHA, in1=y3[0:rows], op0=ALU.mult, op1=ALU.add))
                if z == FT + NG_BUF - 1:
                    add_half(0, 0)
                    add_half(0, 1)
                elif FT + NG_BUF <= z < FT + NG_BUF + TP - 1:
                    add_half(0, z - FT - NG_BUF + 2)
            def weight_norm(t):
                rows = P if t < TP else NS
                x = x_sb[0:rows, t, :]
                dve.wait_ge(n2_scaled, t + 1)
                nc.vector.tensor_tensor(x, x, ln2[0:rows, 1, :], ALU.mult).then_inc(n2_w, 1)

            for t in range(TP + 1):
                rows = P if t < TP else NS
                add_half(1, t)
                v = mv2[0:rows, t, :]
                then(nc.vector.bn_aggr(v[:, 0:2], stat2[0:rows, t].rearrange("p h s -> p (h s)")))
                nc.vector.tensor_scalar(v[:, 1:2], v[:, 1:2], EPS, None, ALU.add).then_inc(n2_var, 1)
                if 0 < t < TP:
                    weight_norm(t - 1)
                dve.wait_ge(n2_rt, t + 1)
                then(nc.vector.reciprocal(v[:, 3:4], v[:, 2:3]))
                nc.vector.scalar_tensor_tensor(out=v[:, 4:5], in0=v[:, 0:1], scalar=-1.0, in1=v[:, 3:4],
                                               op0=ALU.mult, op1=ALU.mult).then_inc(n2_fac, 1)
            weight_norm(TP - 1)
            weight_norm(TP)
            dve.wait_ge(n2_w, TP + 1)
            x = x_sb[0:NS, TP, :]
            nc.vector.tensor_tensor(x, x, ln2[0:NS, 2, :], ALU.add).then_inc(y_last, 1)

        @block.tensor
        def _(pe):
            def landed(n):
                pe.wait_ge(w_in_slot[SLOT_OF[n]], slot_count(n))

            pe.wait_ge(c_in, 16 * 3)
            for k in range(KT_D):
                last = nc.tensor.transpose(bk(1)[:, 16 * k:16 * k + C], c_r[:, P * k:P * k + P], ident[0:C, 0:C])
            last.then_inc(c_tr, 1)
            pe.wait_ge(early, 16 * 12)
            for r, k in enumerate((93, 88, 88)):
                last = nc.tensor.transpose(bk(0)[:, P * r:P * r + k], vec_r[0:k, r, :], ident[0:k, 0:k])
            last.then_inc(vecs_t, 1)

            def ada_rows(ch):
                n = CHUNK_AT[("ada", ch)]
                landed(n)
                if ch:
                    pe.wait_ge(ada_ms, ch)
                for k in range(KT_D):
                    j = k % 4
                    last = nc.tensor.matmul(bk(6)[32 * j:32 * j + C, :], c_t[:, k, :], slot(SLOT_OF[n])[:, k, :],
                                            start=(k < 4), stop=(k >= 4))
                last.then_inc(ada_mm, 1)

            def ada_sum(ch):
                pe.wait_ge(ada_mm, ch + 1)
                pe.wait_ge(ada_ms, ch + 1)
                pe.sem_inc(w_used, 1)
                if ch:
                    pe.wait_ge(ada_ok, ch)
                for c in range(4):
                    last = nc.tensor.matmul(bk(7)[:, 16 * c:16 * c + C], mod_s[:, ch % 2, P * c:P * c + P], sum9[:, :],
                                            start=True, stop=True)
                last.then_inc(ada_tt, 1)

            pe.wait_ge(bank6_zero, 1)
            pe.wait_ge(c_cp, 1)
            def turn_sample(mm, bank):
                for f in range(KT_D):
                    last = nc.tensor.transpose(bank[:, NS * f:NS * f + NS], x_sb[0:NS, TP, P * f:P * f + P], ident[0:NS, 0:NS])
                last.then_inc(mm, 1)

            def turn_tile(bank, t, f):
                return nc.tensor.transpose(bank[:, P * t:P * t + P], x_sb[:, t, P * f:P * f + P], ident[:, :])

            for ch in range(2):
                ada_rows(ch)
                ada_sum(ch)
            pe.wait_ge(x_in, 32)
            pe.wait_ge(vecs_c, 1)
            turn_sample(xt_mm, bk(4))
            for f in range(KT_D):
                if f == 4:
                    for ch in range(2, 4):
                        ada_rows(ch)
                        ada_sum(ch)
                if f >= 4:
                    if f % 2 == 0:
                        pe.wait_ge(xt_d, (f - 4) // 2 + 1)
                    else:
                        pe.wait_ge(xt_a, (f - 4) // 2 + 1)
                for t in range(TP):
                    last = turn_tile(bk(f % 4), t, f)
                last.then_inc(xt_mm, 1)
            pe.wait_ge(xt_d, 5)
            pe.wait_ge(xt_a, 4)

            def product(out, left, right, first, last):
                nc.tensor.matmul(out, left[0], right[0], start=first, stop=False)
                nc.tensor.matmul(out, left[0], right[1], start=False, stop=False)
                return nc.tensor.matmul(out, left[1], right[0], start=False, stop=last)

            for n in range(len(units) + 3):
                if n < len(units):
                    s, t = units[n]
                    ch = CHUNK_AT[("in", s)]
                    if n >= 4:
                        if n - 4 in rope_units:
                            pe.wait_ge(pj_d, d_units(n - 4))
                        else:
                            pe.wait_ge(pj_a, a_units(n - 4))
                    rows = P if t < TP else NS
                    for k in range(KT_D):
                        if t == 0:
                            if k % 2 == 0:
                                pe.wait_ge(win_pool, 4 * s + k // 2 + 1)
                            else:
                                pe.wait_ge(win_dve, 4 * s + k // 2 + 1)
                        if n == 0 and k % 2 == 0:
                            pe.wait_ge(ht_rest, k // 2 + 1)
                        elif n == 0:
                            pe.wait_ge(ht_rest_p, k // 2 + 1)
                        if n == TP:
                            pe.wait_ge(ht_rest, 5)
                        cols = slice(P * t, P * t + rows)
                        last = product(bk(n % 4)[0:rows, :], (ht_high_r[:, k, cols], ht_r[:, k, cols]),
                                       pair_of(ch, k), k == 0, k == KT_D - 1)
                        if t == TP and k < KT_D - 1:
                            last.then_inc(win_free, 1)
                    last.then_inc(pj_mm, 1)
                    if t == TP:
                        pe.wait_ge(pj_mm, n + 1)
                        pe.sem_inc(win_free, 1)
                        pe.sem_inc(w_used, 1)
                if (n - 2) in tr_units:
                    s, t = units[n - 2]
                    k = tr_units.index(n - 2)
                    r = rope_units.index(n - 2)
                    pe.wait_ge(rope_ok, r + 1)
                    if k >= 2:
                        s2, t2 = units[tr_units[k - 2]]
                        by_act = [x for x in tr_units[:k - 1] if units[x][0] in (0, 3) and units[x][1] < TP]
                        if s2 in (0, 3) and t2 < TP:
                            pe.wait_ge(qk_a, len(by_act))
                        else:
                            pe.wait_ge(qk_d, k - 1 - len(by_act))
                    rows = P if t < TP else NS
                    for f in range(4):
                        last = nc.tensor.transpose(bk(4 + k % 2)[:, rows * f:rows * f + rows],
                                                   stage[0:rows, r % 4, P * f:P * f + P], ident[0:rows, 0:rows])
                    last.then_inc(qk_t, 1)

            pe.wait_ge(qk_a, 2 * TP)
            pe.wait_ge(qk_d, len(tr_units) - 2 * TP)
            pe.wait_ge(pj_a, len(v_units))
            pe.wait_ge(pj_d, len(rope_units))

            def prompt_scores(u, bank):
                m, n, qb = pa[u]
                return nc.tensor.matmul(bank[:, 0:P * (qb + 1)], qtp[:, 8 * m + n, P * qb:P * qb + P],
                                        kt[:, 4 * m + n // 2, 0:P * (qb + 1)], start=True, stop=True)

            def prompt_turn(u, bank):
                for kb in range(pa[u][2] + 1):
                    last = nc.tensor.transpose(bank[:, P * kb:P * kb + P], p_b[:, u % 2, P * kb:P * kb + P], ident[:, :])
                return last

            def prompt_weigh(u, bank):
                m, n, qb = pa[u]
                for kb in range(qb + 1):
                    last = nc.tensor.matmul(bank[:, 0:P], pt_b[:, u % 2, P * kb:P * kb + P],
                                            vp[:, kb, m, P * (n // 2):P * (n // 2) + P], start=(kb == 0), stop=(kb == qb))
                return last

            for s in range(NU + 3):
                if s < NU:
                    if s >= 2:
                        pe.wait_ge(pa_min, s - 1)
                    prompt_scores(s, bk(s % 2)).then_inc(pa_s, 1)
                if 0 <= (x := s - 2) < NU:
                    pe.wait_ge(pa_exp, x + 1)
                    if x >= 2:
                        pe.wait_ge(pa_pt, x - 1)
                    prompt_turn(x, bk(2 + x % 2)).then_inc(pa_t, 1)
                if s % 4 == 0 and s >= 4:
                    ada_sum(4 + s // 4 - 1)
                if 0 <= (x := s - 3) < NU:
                    pe.wait_ge(pa_pt, x + 1)
                    if x >= 2:
                        pe.wait_ge(pa_o, x - 1)
                    prompt_weigh(x, bk(4 + x % 2)).then_inc(pa_pv, 1)
                if s < NU and s % 4 == 3:
                    ada_rows(4 + s // 4)

            def scores_b(y):
                pe.wait_ge(pb_min, y)
                prompt_scores(NU + y, bk(5)).then_inc(pb_s, 1)

            def turn_b(y):
                pe.wait_ge(pb_exp, y + 1)
                if y:
                    pe.wait_ge(pb_pt, y)
                prompt_turn(NU + y, bk(6)).then_inc(pb_t, 1)

            def weigh_b(y):
                pe.wait_ge(pb_pt, y + 1)
                if y:
                    pe.wait_ge(pb_o, y)
                prompt_weigh(NU + y, bk(7)).then_inc(pb_pv, 1)

            pe.wait_ge(pa_min, NU)
            pe.wait_ge(pa_pt, NU)
            pe.wait_ge(pa_o, NU)
            pe.wait_ge(ada_ok, 12)

            def score(w, h, bank, keys, at, nk):
                for d in range(2):
                    for nn in range(4):
                        g = 2 * (4 * h + nn) + d
                        last = nc.tensor.matmul(bank[32 * nn:32 * nn + 32, at:at + nk],
                                                qbd[:, w % 2, g].rearrange("p i q -> p (i q)"), keys[:, g, 0:nk],
                                                start=(d == 0), stop=(d == 1), skip_group_check=True)
                return last

            def score_group(w, g):
                m, b = sa[w]
                G = NG[w] + g
                if g == 0:
                    pe.wait_ge(q_bd, w + 1)
                    if w >= 1:
                        pe.wait_ge(sa_min, w)
                        pe.wait_ge(sa_exp, 2 * w)
                pe.wait_ge(kg_t, G + 1)
                score(w, 0, bk(0), ktg[:, G % NK], P * g, 32 * groups[m][g])
                score(w, 1, bk(1), ktg[:, G % NK], P * g, 32 * groups[m][g]).then_inc(sa_g, 1)

            def score_new(w):
                pe.wait_ge(kn_t, w + 1)
                if w:
                    pe.wait_ge(sa_o, w)
                score(w, 0, bk(4), ktn[:, w % 2], 384, 32)
                score(w, 1, bk(4), ktn[:, w % 2], 416, 32).then_inc(sa_s, 1)

            def weigh_group(w, g):
                m, b = sa[w]
                G = NG[w] + g
                pe.wait_ge(vg_in[G % NV], v_count(m, w, g))
                k = 32 * groups[m][g]
                for i in range(4):
                    for j in range(4):
                        at = P * g + 32 * i + 16 * (j % 2)
                        last = nc.tensor.matmul(bk(4)[32 * j:32 * j + 16, 0:P], pt_s[0:k, j // 2, at:at + 16],
                                                vg[G % NV][0:k, i, P * j:P * j + P], start=(g == 0 and i == 0),
                                                stop=False, skip_group_check=True)
                last.then_inc(sa_vg, 1)

            for g in range(len(groups[0])):
                score_group(0, g)
            score_new(0)
            for w, (m, b) in enumerate(sa):
                n = 32 * sum(groups[m])
                if w:
                    weigh_b(2 * w - 1)
                scores_b(2 * w)
                for h in range(2):
                    pe.wait_ge(sa_exp, 2 * w + h + 1)
                    if w >= 1:
                        pe.wait_ge(sa_pt, 2 * w)
                        pe.wait_ge(sa_ph, w)
                    for u in range((n + P - 1) // P):
                        k = min(P, n - P * u)
                        nc.tensor.transpose(bk(2 + h)[0:k, P * u:P * u + P], p_s[:, h, P * u:P * u + k], perm[:, :])
                    nc.tensor.transpose(bk(4)[0:32, P + P * h:2 * P + P * h], p_s[:, h, n:n + 32], perm[:, :]).then_inc(sa_t, 1)
                nxt = groups[sa[w + 1][0]] if w + 1 < len(sa) else []
                for g in range(4):
                    if g < len(nxt):
                        score_group(w + 1, g)
                    if g == 0:
                        pe.wait_ge(sa_pt, 2 * w + 2)
                        pe.wait_ge(sa_ph, w + 1)
                    if g < len(groups[m]):
                        weigh_group(w, g)
                    if g == 2:
                        turn_b(2 * w)
                        scores_b(2 * w + 1)
                pe.wait_ge(new_in[w % 2], 32 * (w // 2 + 1))
                for j in range(4):
                    at = 16 * (j % 2)
                    last = nc.tensor.matmul(bk(4)[32 * j:32 * j + 16, 0:P], ptn[0:DS, j // 2, at:at + 16],
                                            vn[0:DS, w % 2, P * j:P * j + P], start=False, stop=True, skip_group_check=True)
                last.then_inc(sa_pv, 1)
                weigh_b(2 * w)
                if nxt:
                    score_new(w + 1)
                turn_b(2 * w + 1)
            weigh_b(2 * len(sa) - 1)
            pe.wait_ge(sa_exp, 32)
            for h in range(2):
                nc.tensor.matmul(bk(0)[:, 0:16], sums[:, h, :], rs_s[:, h, :], start=(h == 0), stop=False)
                last = nc.tensor.matmul(bk(0)[:, 0:16], sums[:, h, :], rs_n[:, h, :], start=False, stop=(h == 1))
            last.then_inc(sa_l, 1)

            def turn_mixed(f):
                if f >= 4:
                    pe.wait_ge(mt_a, f - 3)
                for t in range(TP):
                    last = nc.tensor.transpose(bk(4 + (f + 1) % 4)[:, P * t:P * t + P], mixv[:, t, P * f:P * f + P], ident[:, :])
                last.then_inc(mt_mm, 1)

            pe.wait_ge(sa_o, len(sa))
            pe.wait_ge(sa_pt, 2 * len(sa))
            pe.wait_ge(pb_pt, len(pb))
            pe.wait_ge(pb_o, len(pb))
            for f in range(4):
                turn_mixed(f)
            pe.wait_ge(sa_n, 1)
            pe.wait_ge(sa_ph, len(sa))
            for w, (m, b) in enumerate(sa):
                last = nc.tensor.matmul(bk(1 + m)[:, 32 * b:32 * b + 32], o_s[:, w, :], pick[:, :], start=True, stop=True)
            last.then_inc(sa_x, 1)
            pe.wait_ge(rms_ok, 1)
            for f in range(4, KT_D):
                turn_mixed(f)
            pe.wait_ge(sa_n, 2)
            nc.tensor.matmul(bk(3)[:, 0:256], ones[:, :], ob_q, start=True, stop=True).then_inc(sa_sq, 1)

            def spread_gates():
                pe.wait_ge(mt_d, 1)
                pe.wait_ge(sa_fin, 1)
                for j in range(8):
                    which, kind, half = j // 4, (j // 2) % 2, j % 2
                    rows = P if kind == 0 else NS
                    if j >= 2:
                        pe.wait_ge(gb_a, j - 1)
                    for c in range(4):
                        f = 4 * half + c
                        col = mod_t[:, (16, 40)[which] + f, 0:1].to_broadcast([P, P]) if kind == 0 else \
                            gexp[:, 8 * which + f].rearrange("p b s -> p (b s)")
                        last = nc.tensor.matmul(bk(j % 2)[0:rows, P * c:P * c + P], col, ident[:, :], start=True, stop=True)
                    last.then_inc(gb_mm, 1)

            pe.wait_ge(mt_a, KT_D)
            for j in range(2 * (TP + 1)):
                i, half = divmod(j, 2)
                t = WO_TILES[i]
                rows = P if t < TP else NS
                n = CHUNK_AT[("o", half)]
                if j >= 4:
                    pe.wait_ge(wo_d, j - 3)
                for k in range(KT_D):
                    if i == 0 and k % 2 == 0:
                        pe.wait_ge(wl_rest, 4 * half + k // 2 + 1)
                    if j == 0:
                        pe.wait_ge(mt_rest, k + 1)
                    if t == TP:
                        pe.wait_ge(mt_hi, 1)
                    cols = slice(P * t, P * t + rows)
                    last = product(bk(4 + j % 4)[0:rows, :], (mt_high_r[:, k, cols], ht_r[:, k, cols]),
                                   pair_of(n, k), k == 0, k == KT_D - 1)
                last.then_inc(wo_mm, 1)
                if j == 2 * TP:
                    pe.wait_ge(wo_mm, j + 1)
                    pe.sem_inc(w_used, 1)
                if j == 0:
                    spread_gates()
                for q in st_after.get(j, []):
                    if q == 0:
                        pe.wait_ge(st_in, 16)
                        pe.wait_ge(sa_fin, 2)
                    if q >= 2:
                        pe.wait_ge(st_ok, q - 1)
                    for c in range(4):
                        last = nc.tensor.transpose(bk(2 + q % 2)[:, 16 * c:16 * c + 16],
                                                   st_r[:, 512 * q + P * c:512 * q + P * c + P], ident[0:16, 0:16])
                    last.then_inc(st_mm, 1)
                if j == 7:
                    pe.wait_ge(x1_ok, 3)
                    pe.wait_ge(gb_a, 8)
                    turn_sample(h2_mm, bk(0))
            pe.wait_ge(wo_mm, 2 * TP + 2)
            pe.sem_inc(w_used, 1)
            pe.wait_ge(wo_d, 2 * TP + 2)
            pe.wait_ge(st_ok, 11)
            pe.wait_ge(x1_ok, TP)
            for f in range(KT_D):
                if f == 0:
                    pe.wait_ge(h2_d, 1)
                for t in range(TP - 1):
                    turn_tile(bk(f), t, f)
            pe.wait_ge(x1_ok, TP + 1)
            for f in range(KT_D):
                turn_tile(bk(f), TP - 1, f).then_inc(h2_mm, 1)
            pe.wait_ge(h2_d, 5)
            pe.wait_ge(h2_a, 4)
            for h in range(2):
                cols = slice(HALF_NT * h, HALF_NT * h + HALF_NT)
                if h == 1:
                    pe.wait_ge(ht_rest, 10)
                for kk in range(KT_D):
                    if h == 0:
                        if kk % 4 == 0:
                            pe.wait_ge(up0_dve, kk // 4 + 1)
                        elif kk % 4 == 2:
                            pe.wait_ge(up0_pool, kk // 4 + 1)
                        if kk % 2:
                            pe.wait_ge(ht_rest_p, 4 + kk // 2 + 1)
                        else:
                            pe.wait_ge(ht_rest, 5 + kk // 2 + 1)
                    last = product(up_bank(0)[:, h, :], pair_of(CHUNK_AT[("up", 0)], kk, slice(0, P)),
                                   (ht_high_r[:, kk, cols], ht_r[:, kk, cols]), kk == 0, kk == KT_D - 1)
            last.then_inc(up_mm, 1)
            for k in range(1, 2 * FT):
                f, g = divmod(k, 2)
                n = CHUNK_AT[("up", f // 2)]
                if k >= 3:
                    pe.wait_ge(up_u, k - 2)
                at = 256 * g + P * (f % 2)
                for kk in range(KT_D):
                    if k % 4 == 0 and kk % 2 == 0:
                        pe.wait_ge(wl_rest, piece_count(8 + k + kk // 2))
                    for h in range(2):
                        cols = slice(HALF_NT * h, HALF_NT * h + HALF_NT)
                        last = product(up_bank(k)[:, h, :], pair_of(n, kk, slice(at, at + P)),
                                       (ht_high_r[:, kk, cols], ht_r[:, kk, cols]), kk == 0, kk == KT_D - 1)
                last.then_inc(up_mm, 1)
                if k % 4 == 3:
                    pe.wait_ge(up_mm, k + 1)
                    pe.sem_inc(w_used, 1)
            def last_rows(i):
                if i >= 2:
                    pe.wait_ge(us_a, i - 1)
                for c in range(4):
                    last = nc.tensor.transpose(bk(6 + i % 2)[0:18, P * c:P * c + P], u_last[:, 4 * i + c, :], ident[:, :])
                last.then_inc(us_mm, 1)

            pe.wait_ge(up_u, 2 * FT)
            pe.wait_ge(up_x, 2 * FT - 2)
            for half in range(2):
                steps = [(f, t) for f in range(16) for t in range(TP + 1)]
                if half == 0:
                    steps += [(f, t) for f in range(16, FT) for t in range(TP + 1)]
                else:
                    steps += [(f, t) for t in range(TP + 1) for f in range(16, FT)]
                for f, t in steps:
                    n = CHUNK_AT[("down", 3 * half + f // 8)]
                    z, j = FT * half + f, (TP + 1) * half + t
                    if t == 0:
                        if half == 0 and f == 10:
                            pe.wait_ge(up_x, 2 * FT)
                        if half == 0 and f % 2 == 0:
                            last_rows(f // 2)
                        if half == 1 and f == 0:
                            pe.wait_ge(us_a, 11)
                        pe.wait_ge(g_split, z + 1)
                        pe.wait_ge(wl_rest, piece_count(first_piece(n) + (f % 8) // 2))
                    if f == 0 and j >= 8:
                        pe.wait_ge(dn_d, j - 7)
                    rows = P if t < TP else NS
                    cols = slice(P * t, P * t + rows)
                    last = product(bk(j % 8)[0:rows, :], (g_high_r[:, z % NG_BUF, cols], g_rest_r[z % NG_BUF][:, cols]),
                                   pair_of(n, f % 8), f == 0, f == FT - 1)
                    if f == FT - 1:
                        last.then_inc(dn_mm, 1)
                    elif t == TP:
                        last.then_inc(g_used, 1)
                if half == 0:
                    pe.wait_ge(dn_mm, TP + 1)
                    pe.sem_inc(g_used, 1)


def constants():
    import numpy as np

    f32 = np.float32
    c = {"ident": np.eye(P, dtype=f32), "ones": np.ones((P, P), f32)}
    half = 32
    inv = (f32(1.0) / (f32(10000.0) ** (np.arange(half, dtype=f32) / f32(half)))).astype(f32)
    pos = np.zeros((TP + 1, P), f32)
    pos[:TP] = np.arange(SEQ).reshape(TP, P)
    pos[TP, :NS] = PAST + np.arange(NS) % DS
    ang = (pos[:, :, None] * inv).astype(f32)
    cos, sin = np.cos(ang), np.sin(ang)
    k_tab = np.concatenate([cos, cos, -sin, sin], -1)
    c["rope"] = np.stack([k_tab * f32(-0.125), k_tab], 2).transpose(1, 0, 2, 3).astype(f32).copy()

    def penalty(dist):
        n = sum(((dist >= 0) & (dist <= w) & (dist % d == 0)).astype(int) for w, d in ((128, 1), (512, 4), (2048, 16)))
        return np.where(n > 0, -np.log(np.maximum(n, 1)), BIG).astype(f32)

    dist = np.arange(P)[:, None] + (SEQ - P) - np.arange(SEQ)[None, :]
    c["maskt"] = np.stack([penalty(dist), np.where(dist >= 0, 0, BIG).astype(f32)], 1)
    i = (np.arange(P) // 8) % 4
    q = np.arange(P) % 8
    m = np.arange(32)
    cols = [16 * (32 * i[:, None] + m) + t for t in range(8)] + [16 * (96 + m[None, :]) + 8 + 4 * x + i[:, None] for x in range(2)]
    sm = np.concatenate([penalty(PAST + q[:, None] - k) for k in cols], 1)
    here = (i[:, None] == 0) & (m[None, :] < DS) & (m[None, :] <= q[:, None])
    c["smask"] = np.concatenate([sm, np.where(here, penalty(q[:, None] - m[None, :]), f32(BIG)),
                                 np.where(here, f32(0), f32(BIG))], 1).astype(f32)
    sums = np.zeros((2, P, P), f32)
    for h in range(2):
        for r in range(P):
            for out in range(P):
                j, n2 = out // 32, min((out % 32) // 8, 1)
                sums[h, r, out] = 4 * h + r // 32 == 2 * j + n2 and r % 8 == out % 8
    c["sums"] = sums.transpose(1, 0, 2).copy()
    r = np.arange(P)
    c["pick"] = ((r[:, None] // 32 == np.arange(32)[None, :] // 8) & (r[:, None] % 8 == np.arange(32)[None, :] % 8)
                 & (r[:, None] % 32 < 16)).astype(f32)
    c["colmask"] = ((np.arange(P)[None, :] // 64) == ((r[:, None] % 32) // 8)).astype(f32)
    c["sum9"] = (r[:, None] % 32 == np.arange(C)[None, :]).astype(f32)
    c["diff_c"] = np.stack([(r % 32 // 8 != 1), (r % 32 // 8 == 1)], 1).astype(f32)
    perm = np.zeros((P, P), f32)
    for n in range(4):
        for i_ in range(4):
            for q_ in range(8):
                perm[32 * n + 8 * i_ + q_, 32 * i_ + 8 * n + q_] = 1
    c["perm"] = perm
    return c


_OUTS = [("yp", (1, SEQ, D)), ("ys", (DB, DS, D)),
         ("wkp", (1, 1, SEQ, 8, 64)), ("wvp", (1, 1, SEQ, 8, 64)),
         ("wks", (1, DB, PAST, 8, 64)), ("wvs", (1, DB, PAST, 8, 64)),
         ("kkp", (1, 1, SEQ, 4, 128)), ("kvp", (1, 1, SEQ, 4, 128)),
         ("kks", (1, DB, DS, 4, 128)), ("kvs", (1, DB, DS, 4, 128)),
         ("cp", (1, 1, 2, 2 * DFF)), ("cs", (1, DB, 2, 2 * DFF))]


def kernel(**inputs):
    import numpy as _np
    import concourse.bacc as _bacc
    from concourse.bass_utils import run_bass_kernel_spmd as _run

    nc = _bacc.Bacc("TRN2", target_bir_lowering=False, num_devices=1, dynamic_dma_scratch_size=1024)
    arrays, ins, outs = {}, {}, {}
    for name, value in {**inputs, **constants()}.items():
        value = _np.ascontiguousarray(value)
        arrays[f"in_{name}"] = value
        ins[name] = nc.dram_tensor(f"in_{name}", value.shape, mybir.dt.from_np(value.dtype), kind="ExternalInput").ap()
    for name, shape in _OUTS:
        outs[name] = nc.dram_tensor(f"out_{name}", shape, F32, kind="ExternalOutput").ap()
    spill = nc.dram_tensor("x1_spill", (NT, D), F32).ap()
    build(nc, ins, outs, spill)
    r = _run(nc, [arrays], core_ids=[0])
    return tuple(r.results[0][f"out_{name}"] for name, _ in _OUTS)
```
